# Optimizing a Trainium2 kernel written in Bass

```python
import math
import jax, jax.numpy as jnp
from jax import lax
import numpy as np

D_MODEL = 1024
BATCH = 1
SEQ = 128
DEPTH = 1
DEC_BATCH = 1
DEC_SEQ = 512
PAST_LEN = 256

GRID_W = 64
N_HEADS = 8
HEAD_DIM = 64
V_HEAD_DIM = 2 * HEAD_DIM
Q_WIDTH = N_HEADS * 2 * HEAD_DIM
ATTN_WIDTH = N_HEADS * V_HEAD_DIM
ROPE_AXIS_DIM = HEAD_DIM // 2
ROPE_BASE = 10000.0
Q_BLOCK = 128
CHUNK = 128
GMLP_WIDTH = D_MODEL
N_GMLP_GROUPS = 8
GMLP_GROUP_DIM = GMLP_WIDTH // N_GMLP_GROUPS
N_EXPERTS = 16
EC_CAPACITY_FACTOR = 2
D_EXPERT = 2048
IN_WIDTH = 2 * Q_WIDTH + ATTN_WIDTH + 2 * GMLP_WIDTH + 2 * D_MODEL
EPS = 1e-6

kernel_name = "hybrid_diffattn_gmlp_ecmoe_prefix_step"

def rms_norm(x, g):
    xf = x.astype(jnp.float32)
    y = xf * lax.rsqrt(jnp.mean(xf * xf, axis=-1, keepdims=True) + EPS)
    return (y * g.astype(jnp.float32)).astype(x.dtype)

def layer_norm(x, g, b):
    xf = x.astype(jnp.float32)
    mu = jnp.mean(xf, axis=-1, keepdims=True)
    var = jnp.mean(jnp.square(xf - mu), axis=-1, keepdims=True)
    y = (xf - mu) * lax.rsqrt(var + EPS)
    return (y * g.astype(jnp.float32) + b.astype(jnp.float32)).astype(x.dtype)

def lambda_init_for(layer):
    return 0.8 - 0.6 * math.exp(-0.3 * layer)

def rope_2d(n_tokens, dtype):
    rows = n_tokens // GRID_W
    row = jnp.broadcast_to(jnp.arange(rows, dtype=jnp.float32)[:, None], (rows, GRID_W)).reshape(-1)
    col = jnp.broadcast_to(jnp.arange(GRID_W, dtype=jnp.float32)[None, :], (rows, GRID_W)).reshape(-1)
    half = ROPE_AXIS_DIM // 2
    inv_freq = ROPE_BASE ** (-jnp.arange(half, dtype=jnp.float32) / half)
    ar = row[:, None] * inv_freq
    ac = col[:, None] * inv_freq
    ang = jnp.concatenate([ar, ar, ac, ac], axis=-1)
    cos = jnp.cos(ang)[:, None, None, :].astype(dtype)
    sin = jnp.sin(ang)[:, None, None, :].astype(dtype)
    return cos, sin

def apply_rope(x, cos, sin):
    x1, x2, x3, x4 = jnp.split(x, 4, axis=-1)
    rot = jnp.concatenate([-x2, x1, -x4, x3], axis=-1)
    return x * cos + rot * sin

def diff_attention(q, k, v, lam):
    B, N = q.shape[0], q.shape[1]
    nb = N // Q_BLOCK
    scale = HEAD_DIM ** -0.5
    kf = k.astype(jnp.float32)
    vf = v.astype(jnp.float32)
    qb = q.reshape(B, nb, Q_BLOCK, N_HEADS, 2, HEAD_DIM).transpose(1, 0, 2, 3, 4, 5)

    def block(qblk):
        s = jnp.einsum('bqhsd,bkhsd->bshqk', qblk.astype(jnp.float32), kf) * scale
        p = jax.nn.softmax(s, axis=-1)
        a = p[:, 0] - lam * p[:, 1]
        return jnp.einsum('bhqk,bkhv->bqhv', a, vf)

    o = lax.map(block, qb)
    return o.transpose(1, 0, 2, 3, 4).reshape(B, N, N_HEADS, V_HEAD_DIM).astype(v.dtype)

def spatial_gating(zu, zv, ln_g, ln_b, w_sp, b_sp):
    B, N, _ = zu.shape
    zu = jax.nn.gelu(zu)
    zv = layer_norm(jax.nn.gelu(zv), ln_g, ln_b)
    zc = zv.reshape(B, N // CHUNK, CHUNK, N_GMLP_GROUPS, GMLP_GROUP_DIM)
    sp = jnp.einsum('gpq,bnqgc->bnpgc', w_sp, zc) + b_sp.T[:, :, None]
    return zu * sp.reshape(B, N, GMLP_WIDTH)

def token_mixer(h, lp, lambda_init, rope, ctx_kv):
    B, N, _ = h.shape
    proj = h @ lp['w_in']
    offs = np.cumsum([Q_WIDTH, Q_WIDTH, ATTN_WIDTH, GMLP_WIDTH, GMLP_WIDTH, D_MODEL]).tolist()
    q, k, v, zu, zv, g_a, g_b = jnp.split(proj, offs, axis=-1)
    q = rms_norm(q.reshape(B, N, N_HEADS, 2, HEAD_DIM), lp['q_norm_g'])
    k = rms_norm(k.reshape(B, N, N_HEADS, 2, HEAD_DIM), lp['k_norm_g'])
    v = v.reshape(B, N, N_HEADS, V_HEAD_DIM)
    if rope is not None:
        cos, sin = rope
        q = apply_rope(q, cos, sin)
        k = apply_rope(k, cos, sin)
    if ctx_kv is not None:
        k_all = jnp.concatenate([ctx_kv[0].astype(k.dtype), k], axis=1)
        v_all = jnp.concatenate([ctx_kv[1].astype(v.dtype), v], axis=1)
    else:
        k_all, v_all = k, v
    f32 = jnp.float32
    lam = (jnp.exp(jnp.sum(lp['lambda_q1'].astype(f32) * lp['lambda_k1'].astype(f32)))
           - jnp.exp(jnp.sum(lp['lambda_q2'].astype(f32) * lp['lambda_k2'].astype(f32)))
           + lambda_init)
    o_a = diff_attention(q, k_all, v_all, lam)
    o_a = (rms_norm(o_a, lp['subln_g']) * (1.0 - lambda_init)).reshape(B, N, ATTN_WIDTH)
    o_b = spatial_gating(zu, zv, lp['gmlp_ln_g'], lp['gmlp_ln_b'], lp['w_spatial'], lp['b_spatial'])
    merged = jax.nn.sigmoid(g_a) * o_a + jax.nn.sigmoid(g_b) * o_b
    return merged @ lp['w_out'], k, v

def expert_choice_moe(h, w_router, w_gate, w_up, w_down):
    B, N, D = h.shape
    cap = max(1, EC_CAPACITY_FACTOR * N // N_EXPERTS)
    aff = jax.nn.softmax((h @ w_router).astype(jnp.float32), axis=-1)
    gates, idx = lax.top_k(aff.transpose(0, 2, 1), cap)

    def one(hb, gb, ib):
        xe = hb[ib]
        hid = jax.nn.silu(jnp.einsum('ecd,edf->ecf', xe, w_gate)) * jnp.einsum('ecd,edf->ecf', xe, w_up)
        ye = jnp.einsum('ecf,efd->ecd', hid, w_down) * gb[..., None].astype(hb.dtype)
        return jnp.zeros_like(hb).at[ib.reshape(-1)].add(ye.reshape(-1, D))

    return jax.vmap(one)(h, gates, idx)

def trunk_layer(x, cond, lp, lambda_init, rope, ctx_kv):
    m = jax.nn.silu(cond) @ lp['w_ada'] + lp['b_ada']
    shift1, scale1, gate1, shift2, scale2, gate2 = jnp.split(m[:, None, :], 6, axis=-1)
    h = rms_norm(x, lp['norm1_g']) * (1.0 + scale1) + shift1
    mix, k, v = token_mixer(h, lp, lambda_init, rope, ctx_kv)
    x = x + gate1 * mix
    h2 = rms_norm(x, lp['norm2_g']) * (1.0 + scale2) + shift2
    x = x + gate2 * expert_choice_moe(h2, lp['w_router'], lp['w_gate_e'], lp['w_up_e'], lp['w_down_e'])
    return x, k, v

def setup_inputs(seed: int = 0) -> dict:
    key = jax.random.key(seed)
    ks = jax.random.split(key, 32)
    f32 = jnp.float32
    nrm = lambda k, shape, s: jax.random.normal(k, shape, f32) * s
    D = D_MODEL
    return {
        'x_prompt': nrm(ks[0], (BATCH, SEQ, D), 1.0),
        'x_sample': nrm(ks[1], (DEC_BATCH, DEC_SEQ, D), 1.0),
        'cache_k': nrm(ks[2], (DEC_BATCH, DEPTH, PAST_LEN, N_HEADS, 2, HEAD_DIM), 1.0),
        'cache_v': nrm(ks[3], (DEC_BATCH, DEPTH, PAST_LEN, N_HEADS, V_HEAD_DIM), 1.0),
        'c': nrm(ks[4], (DEC_BATCH, D), 1.0),
        'c_ctx': nrm(ks[5], (D,), 1.0),
        'w_ada': nrm(ks[6], (DEPTH, D, 6 * D), D ** -0.5),
        'b_ada': nrm(ks[7], (DEPTH, 6 * D), 0.02),
        'norm1_g': 1.0 + nrm(ks[8], (DEPTH, D), 0.02),
        'norm2_g': 1.0 + nrm(ks[9], (DEPTH, D), 0.02),
        'w_in': nrm(ks[10], (DEPTH, D, IN_WIDTH), D ** -0.5),
        'q_norm_g': 1.0 + nrm(ks[11], (DEPTH, HEAD_DIM), 0.02),
        'k_norm_g': 1.0 + nrm(ks[12], (DEPTH, HEAD_DIM), 0.02),
        'lambda_q1': nrm(ks[13], (DEPTH, HEAD_DIM), 0.1),
        'lambda_k1': nrm(ks[14], (DEPTH, HEAD_DIM), 0.1),
        'lambda_q2': nrm(ks[15], (DEPTH, HEAD_DIM), 0.1),
        'lambda_k2': nrm(ks[16], (DEPTH, HEAD_DIM), 0.1),
        'subln_g': 1.0 + nrm(ks[17], (DEPTH, V_HEAD_DIM), 0.02),
        'gmlp_ln_g': 1.0 + nrm(ks[18], (DEPTH, GMLP_WIDTH), 0.02),
        'gmlp_ln_b': nrm(ks[19], (DEPTH, GMLP_WIDTH), 0.02),
        'w_spatial': nrm(ks[20], (DEPTH, N_GMLP_GROUPS, CHUNK, CHUNK), CHUNK ** -0.5),
        'b_spatial': 1.0 + nrm(ks[21], (DEPTH, N_GMLP_GROUPS, CHUNK), 0.02),
        'w_out': nrm(ks[22], (DEPTH, D, D), D ** -0.5),
        'w_router': nrm(ks[23], (DEPTH, D, N_EXPERTS), D ** -0.5),
        'w_gate_e': nrm(ks[24], (DEPTH, N_EXPERTS, D, D_EXPERT), D ** -0.5),
        'w_up_e': nrm(ks[25], (DEPTH, N_EXPERTS, D, D_EXPERT), D ** -0.5),
        'w_down_e': nrm(ks[26], (DEPTH, N_EXPERTS, D_EXPERT, D), D_EXPERT ** -0.5),
    }

def reference(x_prompt, x_sample, cache_k, cache_v, c, c_ctx, w_ada, b_ada, norm1_g, norm2_g, w_in,
              q_norm_g, k_norm_g, lambda_q1, lambda_k1, lambda_q2, lambda_k2, subln_g, gmlp_ln_g,
              gmlp_ln_b, w_spatial, b_spatial, w_out, w_router, w_gate_e, w_up_e, w_down_e):
    rope_lat = rope_2d(x_sample.shape[1], x_sample.dtype)
    cond_ctx = c_ctx[None, :]
    xp, xs = x_prompt, x_sample
    new_k, new_v = [], []
    for l in range(DEPTH):
        lp = {
            'w_ada': w_ada[l], 'b_ada': b_ada[l], 'norm1_g': norm1_g[l], 'norm2_g': norm2_g[l],
            'w_in': w_in[l], 'q_norm_g': q_norm_g[l], 'k_norm_g': k_norm_g[l],
            'lambda_q1': lambda_q1[l], 'lambda_k1': lambda_k1[l],
            'lambda_q2': lambda_q2[l], 'lambda_k2': lambda_k2[l], 'subln_g': subln_g[l],
            'gmlp_ln_g': gmlp_ln_g[l], 'gmlp_ln_b': gmlp_ln_b[l],
            'w_spatial': w_spatial[l], 'b_spatial': b_spatial[l], 'w_out': w_out[l],
            'w_router': w_router[l], 'w_gate_e': w_gate_e[l], 'w_up_e': w_up_e[l], 'w_down_e': w_down_e[l],
        }
        lam_init = lambda_init_for(l)
        xp, kp, vp = trunk_layer(xp, cond_ctx, lp, lam_init, None, None)
        new_k.append(kp)
        new_v.append(vp)
        xs, _, _ = trunk_layer(xs, c, lp, lam_init, rope_lat, (cache_k[:, l], cache_v[:, l]))
    new_cache_k = jnp.stack(new_k, axis=1)
    new_cache_v = jnp.stack(new_v, axis=1)
    return (xp, xs, new_cache_k, new_cache_v)


_drawn_inputs = setup_inputs


def setup_inputs(seed=0):
    import zlib

    import numpy as np

    out = dict(_drawn_inputs(seed))
    spreads = {}
    factors = {'norm1_g': 3.367,
     'norm2_g': 2.952,
     'q_norm_g': 8.0,
     'k_norm_g': 3.112,
     'lambda_q1': 4.781,
     'lambda_k1': 5.044,
     'lambda_q2': 4.768,
     'lambda_k2': 4.994,
     'subln_g': 3.882,
     'gmlp_ln_g': 5.567,
     'gmlp_ln_b': 5.296,
     'b_spatial': 4.607}
    for name, (base, spread) in spreads.items():
        noise = np.random.default_rng([zlib.crc32(name.encode()), seed]).standard_normal(out[name].shape)
        drawn = base * np.exp(spread * noise) if base else spread * noise
        out[name] = __import__('jax').numpy.asarray(drawn.astype(out[name].dtype))
    for name, factor in factors.items():
        out[name] = (out[name] * factor).astype(out[name].dtype)
    return out
```

```python
from contextlib import ExitStack

import numpy as np
import concourse.bass as bass
from concourse import mybir

F32 = mybir.dt.float32
F32R = mybir.dt.float32r
U32 = mybir.dt.uint32
ALU = mybir.AluOpType
ACT = mybir.ActivationFunctionType
AX = mybir.AxisListType

P = 128
D = 1024
KT = D // P
LAT = 512
CTX = 128
NL = LAT // P
NT = NL + CTX // P
TOK = LAT + CTX
PAST = 256
NPAST = PAST // P
H = 8
HD = 64
VD = 128
G = 8
E = 16
FE = 2048
CAP_L = 2 * LAT // E
CAP_C = 2 * CTX // E
CAP = CAP_L + CAP_C
GRID_W = 64
EPS = 1e-6
LAMBDA_INIT = 0.8 - 0.6
CW = 512
CK = 4
NRAW = 3
NSPLIT = 4

BLOCKS = ([("ada", a) for a in range(4)]
          + [("k", 0), ("k", 1), ("q", 0), ("q", 1), ("v", 0), ("ada", 4), ("v", 1), ("ada", 5),
             ("zv", 0), ("ada", 6), ("zv", 1), ("ada", 7), ("ga", 0), ("ada", 8), ("ga", 1), ("ada", 9),
             ("zu", 0), ("ada", 10), ("zu", 1), ("ada", 11), ("gb", 0), ("gb", 1), ("wo", 0), ("wo", 1)])
COLUMN = {"q": 0, "k": 2, "v": 4, "zu": 6, "zv": 8, "ga": 10, "gb": 12}
NB = len(BLOCKS)
FIRST_WO = NB - 2
PRE = 2 * NB
EC = 24
GATES = [4, 5, 10, 11]
VEC = {0: 0, 1: 0, 2: 1, 3: 1, 6: 2, 7: 2, 8: 3, 9: 3}
SPATIAL_AFTER = BLOCKS.index(("ada", 8))


def is_in(kind):
    return kind in COLUMN


def piece_plan():
    plan = [("xt", i, "dve") for i in range(2 * NT)]
    for b, (kind, j) in enumerate(BLOCKS[:FIRST_WO]):
        if is_in(kind):
            plan += [(b, t, "act") for t in range(NT)]
        if b == SPATIAL_AFTER:
            plan += [("sp", i, "dve") for i in range(2 * NT)]
    return plan


PIECES = piece_plan()
PIECE_AT = {(a, i): n for n, (a, i, _) in enumerate(PIECES)}
RING = 6


def emptied_before(n, who):
    return sum(1 for p in PIECES[:n] if p[2] == who)


STAGED = [(b, t) for b, (kind, _) in enumerate(BLOCKS) if kind in ("v", "ga", "zu", "gb") for t in range(NT)]
STAGE_AT = {s: n for n, s in enumerate(STAGED)}
NSTAGE = 3


def stores_of(n):
    b, t = STAGED[n]
    kind = BLOCKS[b][0]
    return (2 if kind == "v" and t == NL else 1) if kind in ("v", "ga") else 0


def stage_stored(n):
    return 16 * sum(stores_of(m) for m in range(n % NSTAGE, n + 1, NSTAGE))


def multiplied(n):
    return sum(1 for m in range(n + 1) if stores_of(m) == 0)


NU = H * NT


def unit_keys(u):
    return (0, NPAST + NL) if u % NT < NL else (NPAST + NL, 1)


def transposed_plan():
    def of_head(h):
        return [("qk", h, i, 4) for i in range(0, 12, 4)]

    def of_unit(u):
        n = unit_keys(u)[1]
        return [("a", u, i, min(4, n - i)) for i in range(0, n, 4)]

    plan = of_head(0)
    for u in range(NU):
        if u >= 1:
            plan += of_unit(u - 1)
        if u % NT == 2 and u // NT + 1 < H:
            plan += of_head(u // NT + 1)
    return plan + of_unit(NU - 1)


TRANSPOSED = transposed_plan()


def transposed_upto(what, which):
    return max(n for n, p in enumerate(TRANSPOSED) if p[:2] == (what, which)) + 1


HT_STEP = {5: 0, 9: 1, 13: 2, 17: 3}
N_P2 = 2 * NT + 2 * NT + 3 * NT + NT + 2 + 3 * KT


def constants():
    half = HD // 4
    inv = np.float32(10000.0) ** (-np.arange(half, dtype=np.float32) / np.float32(half))
    row = np.repeat(np.arange(LAT // GRID_W, dtype=np.float32), GRID_W)[:, None] * inv
    col = np.tile(np.arange(GRID_W, dtype=np.float32), LAT // GRID_W)[:, None] * inv
    ang = np.concatenate([row, row, col, col], axis=-1).astype(np.float32)
    sign = np.repeat(np.array([-1, 1, -1, 1], np.float32), half)
    cos = np.ones((TOK, HD), np.float32)
    sin = np.zeros((TOK, HD), np.float32)
    cos[:LAT] = np.cos(ang)
    sin[:LAT] = np.sin(ang) * sign
    rope = np.stack([a.reshape(NT, P, HD).transpose(1, 0, 2) for a in (cos, sin)], axis=1)
    ident = np.eye(P, dtype=np.float32)
    token = (np.arange(P)[:, None] + P * np.arange(NT)[None]).astype(np.float32)
    tokens = np.tile(np.arange(TOK, dtype=np.float32)[None], (P, 1))
    hilo = np.zeros((P, 2), np.float32)
    hilo[:4] = np.tile(np.eye(2, dtype=np.float32), (2, 1))
    pick = np.zeros((P, 12, 2), np.float32)
    for a in range(12):
        pick[a, a] = 1.0
    return {"rope": rope.reshape(P, -1), "ident": ident, "token": token, "tokens": tokens,
            "hilo": hilo, "pick": pick.reshape(P, -1)}


def trunk_program(nc, A, O_y, O_ys, O_k, O_v):
    def scratch(name, shape):
        return nc.dram_tensor(name, shape, F32, kind="Internal").ap()

    q_d, k_d, v_d = (scratch(n, [TOK, D]) for n in ("q_scr", "k_scr", "v_scr"))
    sa_d, ob_d, x2_d = (scratch(n, [TOK, D]) for n in ("sa_scr", "ob_scr", "x2_scr"))
    gate_d = scratch("gate_scr", [2, 2, D])
    idx_d = scratch("idx_scr", [E, CAP])
    w_ada = A["w_ada"].rearrange("z k n -> (z k) n")
    w_in = A["w_in"].rearrange("z k n -> (z k) n")
    w_out = A["w_out"].rearrange("z k n -> (z k) n")
    w_gate = A["w_gate_e"].rearrange("z e (k p) n -> (z e) p k n", p=P)
    w_up = A["w_up_e"].rearrange("z e (k p) n -> (z e) p k n", p=P)
    w_down = A["w_down_e"].rearrange("z e (k p) n -> (z e) p k n", p=P)
    x_l = A["x_sample"].rearrange("b (t p) d -> p (b t) d", p=P)
    x_c = A["x_prompt"].rearrange("b p d -> p b d")
    ck = A["cache_k"].rearrange("b z (t p) h s d -> p (b z t) h (s d)", p=P)
    cv = A["cache_v"].rearrange("b z (t p) h d -> p (b z t) h d", p=P)
    out_k = O_k.rearrange("b z p h s d -> p (b z h s d)")
    out_v = O_v.rearrange("b z p h d -> p (b z h d)")
    y_l = O_ys.rearrange("b (t p) d -> p (b t) d", p=P)
    y_c = O_y.rearrange("b p d -> p b d")

    def tiles(d):
        return d.rearrange("(t p) n -> p t n", p=P)

    def chunk_source(n):
        kind, j = BLOCKS[n // 2]
        w = {"ada": w_ada, "wo": w_out}.get(kind, w_in)
        c = (COLUMN.get(kind, 0) + j) * CW
        r = (n % 2) * CK * P
        return w[r:r + CK * P, c:c + CW].rearrange("(k p) n -> p k n", p=P)

    def expert_source(e, i):
        if i < 16:
            w, fb, half = (w_gate, w_up)[i // 2 % 2], i // 4, i % 2
            return w[e, :, half * CK:half * CK + CK, fb * CW:fb * CW + CW] if isinstance(e, int) else \
                w[bass.ds(e, 1), :, half * CK:half * CK + CK, fb * CW:fb * CW + CW].rearrange("e p k n -> p (e k) n")
        half, q = (i - 16) // 4, (i - 16) % 4
        return w_down[e, :, q * CK:q * CK + CK, half * CW:half * CW + CW] if isinstance(e, int) else \
            w_down[bass.ds(e, 1), :, q * CK:q * CK + CK, half * CW:half * CW + CW].rearrange("e p k n -> p (e k) n")

    base = (nc.sbuf_base + 31) // 32 * 32
    end = nc.sbuf_usable_end // 32 * 32
    at = [base]

    def place(name, shape, dt=F32, offset=None):
        size = 4 * int(np.prod(shape[1:]))
        o = at[0] if offset is None else offset
        assert o + size <= end, (name, o + size - end)
        if offset is None:
            at[0] += (size + 31) // 32 * 32
        return nc.alloc_sbuf_tensor_at(name, list(shape), dt, offset=o)

    raw = place("raw", [P, NRAW, CK, CW])
    w_hi = place("w_hi", [P, NSPLIT, CK, CW], F32R)
    w_lo = place("w_lo", [P, NSPLIT, CK, CW], F32R)
    MID = at[0]
    h_hi = place("h_hi", [P, KT, TOK], F32R)
    h_lo = place("h_lo", [P, KT, TOK], F32R)
    LOW = at[0]
    ident = place("ident_sb", [P, P])
    token = place("token_sb", [P, NT])
    cols = place("cols", [P, 40])
    mcol = place("mcol", [P, 4, KT, 2])
    amp1 = place("amp1", [P, KT, 2])
    amp2 = place("amp2", [P, KT, 2])
    var = place("var", [P, 40])
    root = place("root", [P, 40])
    rstd = place("rstd", [P, 40])
    newton = place("newton", [P, 40])
    lam = place("lam", [P, 8])
    w_r = place("w_r", [P, KT, E])
    g_sub = place("g_sub", [P, VD])
    gate_v = place("gate_v", [E, CAP])
    idx_u = place("idx_u", [E, CAP], U32)
    idx_f = place("idx_f", [E, CAP])
    rst5 = place("rst5", [P, NT])
    KEEP = at[0]
    tab = place("tab", [P, 2, 2, NT, HD])
    gain = place("gain", [P, 2, HD])
    hilo = place("hilo_sb", [P, 2])
    pick = place("pick_sb", [P, 12, 2])
    b12 = place("b12", [12, CW])
    m4 = place("m4", [4, 2, CW])
    grow = place("grow", [2, 2, CW])
    silu_c = place("silu_c", [P, 2, KT])
    cond = place("cond", [P, KT, 4], F32R)
    bstat = place("bstat", [P, NT, 2, 6])
    mv = place("mv", [P, NT, 2])
    wspT = place("wspT", [P, G, P])
    stage = place("stage", [P, NSTAGE, CW])
    WORK = at[0]
    qk_raw = [place(f"qk_raw{i}", [P, NT, CW]) for i in range(2)]
    qk_swp = [place(f"qk_swp{i}", [P, NT, CW]) for i in range(2)]
    qk_sq = place("qk_sq", [P, NT, CW])
    lamv = place("lamv", [P, 4, HD], offset=WORK + 4 * 4 * NT * CW)
    x_in = place("x_in", [P, NT, D], offset=WORK)
    x_junk = place("x_junk", [P, D], offset=WORK + 4 * NT * D)
    rows40 = place("rows40", [40, P], offset=WORK + 4 * NT * D + 4096)
    w_sp = place("w_sp", [P, G, P], offset=WORK + 4 * NT * D + 8192)
    ob = place("ob", [P, NT, D], offset=WORK)
    ln_g = place("ln_g", [P, D], offset=WORK + 4 * NT * D)
    ln_b = place("ln_b", [P, D], offset=WORK + 4 * NT * D + 4096)
    at[0] = MID
    q_h = place("q_h", [P, 2, NT, P])
    k_h = place("k_h", [P, 2, NPAST + NT, P])
    v_h = place("v_h", [P, 2, NPAST + NT, P])
    qT = place("qT", [P, 2, TOK])
    kT = place("kT", [P, 2, PAST + TOK])
    assert at[0] <= LOW
    NK = PAST + LAT
    at[0] = WORK
    o_t = place("o_t", [P, NT, D])
    p_0 = place("p_0", [P, 2, NK])
    p_1 = place("p_1", [P, 2, NK])
    aT = place("aT", [P, 2, NK])
    nbias = place("nbias", [P, 2, 2])
    rsum = place("rsum", [P, 2, 2])
    rinv = place("rinv", [P, 2])
    m_hi = place("m_hi", [P, KT, TOK], F32R, offset=MID)
    m_lo = place("m_lo", [P, KT, TOK], F32R, offset=MID + 4 * KT * TOK)
    at[0] = WORK + 4 * NT * D
    x2 = place("x2", [P, NT, D])
    gate1 = place("gate1", [P, 2, D])
    at[0] = KEEP
    sa_t = place("sa_t", [P, D])
    ob_t = place("ob_t", [P, D])
    p_sq = place("p_sq", [P, D])
    xw = place("xw", [P, 2 * CW])
    affT = place("affT", [E, TOK])
    affW = place("affW", [E, TOK])
    assert at[0] <= WORK
    xn_hi = place("xn_hi", [P, NT, D], F32R, offset=MID)
    xn_lo = place("xn_lo", [P, NT, D], F32R, offset=MID + 4 * NT * D)
    xn = [place(f"xn{i}", [P, D], offset=WORK + 4096 * i) for i in range(2)]
    h2T = [place(f"h2T{i}", [P, KT, P], offset=WORK + 8192 + 4096 * i) for i in range(2)]
    lg = place("lg", [P, NT, E], offset=WORK + 16384)
    rst = place("rst", [P, NT, 4], offset=WORK + 16384 + 4 * NT * E)
    at[0] = KEEP
    idx_c = place("idx_c", [CAP, E])
    gate_c = place("gate_c", [CAP, E])
    tokens = place("tokens_sb", [P, TOK])
    selT = place("selT", [CAP, TOK], F32R)
    XE = at[0]
    sel_l = place("sel_l", [P, NL, E, CAP_L], F32R, offset=end - 4 * (NL * E * CAP_L + E * CAP_C) - 32)
    sel_c = place("sel_c", [P, E, CAP_C], F32R, offset=end - 4 * E * CAP_C - 32)
    idx_b = place("idx_b", [P, E, CAP], offset=XE)
    xeT = place("xeT", [P, E, KT * CAP], offset=XE + 4 * E * CAP)
    assert XE + 4 * E * CAP + 4 * E * KT * CAP <= end - 4 * (NL * E * CAP_L + E * CAP_C) - 32
    at[0] = XE + 4 * E * CAP + 4 * E * KT * CAP
    yacc = place("yacc", [P, NT, D])
    ye_hi = place("ye_hi", [CAP, D], F32R, offset=XE)
    at[0] = MID
    hT_hi = place("hT_hi", [P, FE // P, CAP], F32R)
    hT_lo = place("hT_lo", [P, FE // P, CAP], F32R)
    xe_hi = place("xe_hi", [P, KT * CAP], F32R)
    xe_lo = place("xe_lo", [P, KT * CAP], F32R)
    sg = place("sg", [CAP, 2, CW])
    hid = place("hid", [CAP, 2, CW])
    ye_lo = place("ye_lo", [CAP, D], F32R)
    assert at[0] <= LOW
    x2_end = place("x2_end", [P, NT, D], offset=MID)
    gate2 = place("gate2", [P, 2, D], offset=MID + 4 * NT * D)

    ctx = ExitStack()
    bank_all = nc.alloc_psum_tensor("banks", [P, 8, CW], F32)

    def bank(i):
        return bank_all[:, i, :]

    with ctx:
        def sem(name):
            return ctx.enter_context(nc.semaphore(name))

        raw_in = [sem(f"raw_in{i}") for i in range(NRAW)]
        hi_done, lo_done, used = sem("hi_done"), sem("lo_done"), sem("used")
        rows_in, const_in, x_load, lam_in = sem("rows_in"), sem("const_in"), sem("x_load"), sem("lam_in")
        wsp_in, ln_in = sem("wsp_in"), sem("ln_in")
        rowsT_done, cols_ready, silu_ready, cond_ready = (sem(n) for n in ("rowsT_done", "cols_ready", "silu_ready", "cond_ready"))
        var_ready, root_done = sem("var_ready"), sem("root_done")
        ssum_ready, xn_ready = sem("ssum_ready"), sem("xn_ready")
        ada_done, m4_ready, conv_done, conv_ev = (sem(n) for n in ("ada_done", "m4_ready", "conv_done", "conv_ev"))
        grow_out = [sem(f"grow_out{i}") for i in range(2)]
        piece_done, ev_act, ev_dve = sem("piece_done"), sem("ev_act"), sem("ev_dve")
        hf_ready, h_hi_ready, h_ready = sem("hf_ready"), sem("h_hi_ready"), sem("h_ready")
        tab_ready, wspT_done, wspT_ready = sem("tab_ready"), sem("wspT_done"), sem("wspT_ready")
        sq_free, rstd_ready, swp_ready, qk_ready = (sem(n) for n in ("sq_free", "rstd_ready", "swp_ready", "qk_ready"))
        qk_out = [sem(f"qk_out{i}") for i in range(2)]
        stage_out = [sem(f"stage_out{i}") for i in range(NSTAGE)]
        stage_full, stage_mul = sem("stage_full"), sem("stage_mul")
        zn_pre, zn_ready, ob_out = sem("zn_pre"), sem("zn_ready"), sem("ob_out")
        dv, po = sem("dv"), sem("po")
        lam_e, lam_x = sem("lam_e"), sem("lam_x")
        qkv_in = [sem(f"qkv_in{i}") for i in range(2)]
        tr_done, tr_ev = sem("tr_done"), sem("tr_ev")
        sc_done = [sem(f"sc_done{i}") for i in range(2)]
        nb_done, exp_done = [sem(f"nb_done{i}") for i in range(2)], [sem(f"exp_done{i}") for i in range(2)]
        a_done, pv_done, o_ev = sem("a_done"), sem("pv_done"), sem("o_ev")
        osq_ready, merged, sa_in, sa_used = (sem(n) for n in ("osq_ready", "merged", "sa_in", "sa_used"))
        p2_done, p2_ev, mhi_ready = sem("p2_done"), sem("p2_ev"), sem("mhi_ready")
        x2_in, x2_ready, x2_sq, xn2_ready, xnhi_ready, x2_out = (sem(n) for n in ("x2_in", "x2_ready", "x2_sq", "xn2_ready", "xnhi_ready", "x2_out"))
        wr_in, lgb_ready, lge_ready, aff_ready = (sem(n) for n in ("wr_in", "lgb_ready", "lge_ready", "aff_ready"))
        idx_ready, idx_out, idxb_in, tok_in, sel_ready = (sem(n) for n in ("idx_ready", "idx_out", "idxb_in", "tok_in", "sel_ready"))
        xeh_done, xe_ready, gu_done, sg_ready, hid_ready = (sem(n) for n in ("xeh_done", "xe_ready", "gu_done", "sg_ready", "hid_ready"))
        ht_done, hth_ready, ht_ready, dn_done, yeh_ready, ye_ready = (sem(n) for n in ("ht_done", "hth_ready", "ht_ready", "dn_done", "yeh_ready", "ye_ready"))
        sc2_done, sc2_ev, end_in, y_ready, y_out, warm = (sem(n) for n in ("sc2_done", "sc2_ev", "end_in", "y_ready", "y_out", "warm"))

        block = ctx.enter_context(nc.Block())

        def raw_count(n):
            return 16 * (n // NRAW + 1)

        def wait_read(eng, n):
            b = n // 2
            kind, j = BLOCKS[b]
            if kind == "ada":
                eng.wait_ge(ada_done, j + 1)
            elif kind == "wo":
                eng.wait_ge(p2_done, 2 * NT + NT * (j + 1))
            else:
                eng.wait_ge(piece_done, PIECE_AT[b, NT - 1] + 1)

        @block.sync
        def _(sp):
            def load(n):
                if n >= NRAW:
                    sp.wait_ge(lo_done, n - NRAW + 1)
                src = chunk_source(n) if n < PRE else expert_source(0, n - PRE)
                sp.dma_start(raw[:, n % NRAW], src).then_inc(raw_in[n % NRAW], 16)

            for i, name in enumerate(["c", "c_ctx", "norm1_g", "norm2_g"]):
                v = A[name]
                flat = v.rearrange("(k p) -> k p", p=P) if len(v.shape) == 1 else v.rearrange("z (k p) -> (z k) p", p=P)
                sp.dma_start(rows40[8 * i:8 * i + 8, :], flat).then_inc(rows_in, 16)
            sp.dma_start(rows40[32:40, :], A["b_spatial"].rearrange("z g p -> (z g) p")).then_inc(rows_in, 16)
            sp.dma_start(ident[:, :], A["ident"]).then_inc(rows_in, 16)
            load(0)
            load(1)
            sp.dma_start(x_in[:, 0:NL, :], x_l).then_inc(x_load, 16)
            sp.dma_start(x_in[:, NL:NT, :], x_c).then_inc(x_load, 16)
            sp.dma_start(hilo[:, :], A["hilo"]).then_inc(const_in, 16)
            sp.dma_start(pick[:, :, :].rearrange("p a b -> p (a b)"), A["pick"]).then_inc(const_in, 16)
            sp.dma_start(b12[:, :], A["b_ada"].rearrange("z (a n) -> (z a) n", n=CW)).then_inc(const_in, 16)
            load(2)
            for i, name in enumerate(["q_norm_g", "k_norm_g"]):
                sp.dma_start(tab[:, i, :, :, :].rearrange("p a t d -> p (a t d)"), A["rope"]).then_inc(lam_in, 16)
                sp.dma_start(gain[:, i, :], A[name].broadcast_to([P, HD])).then_inc(lam_in, 16)
            for i, name in enumerate(["lambda_q1", "lambda_k1", "lambda_q2", "lambda_k2"]):
                sp.dma_start(lamv[:, i, :], A[name].broadcast_to([P, HD])).then_inc(lam_in, 16)
            sp.dma_start(g_sub[:, :], A["subln_g"].broadcast_to([P, VD])).then_inc(lam_in, 16)
            sp.dma_start(w_sp[:, :, :], A["w_spatial"].rearrange("z g p q -> p (z g) q")).then_inc(wsp_in, 16)
            sp.dma_start(w_r[:, :, :], A["w_router"].rearrange("z (k p) e -> p (z k) e", p=P)).then_inc(wr_in, 16)
            sp.dma_start(token[:, :], A["token"]).then_inc(wr_in, 16)

            def gate_store(g):
                a = GATES[g]
                sp.wait_ge(conv_ev, a + 1)
                sp.dma_start(gate_d[:, g // 2, (g % 2) * CW:(g % 2 + 1) * CW], grow[:, g % 2, :]).then_inc(grow_out[g % 2], 16)

            def stores(b):
                kind, j = BLOCKS[b]
                c = j * CW
                if b > 4 and BLOCKS[b - 1][0] in ("k", "q"):
                    qk_store(BLOCKS[b - 1])
                if b > 4 and BLOCKS[b - 1][0] == "ada" and BLOCKS[b - 1][1] in GATES:
                    gate_store(GATES.index(BLOCKS[b - 1][1]))
                if kind in ("v", "ga"):
                    for t in range(NT):
                        n = STAGE_AT[b, t]
                        sp.wait_ge(ev_act, emptied_before(PIECE_AT[b, t] + 1, "act"))
                        out = (v_d if kind == "v" else sa_d)[t * P:(t + 1) * P, c:c + CW]
                        sp.dma_start(out, stage[:, n % NSTAGE, :]).then_inc(stage_out[n % NSTAGE], 16)
                        if stores_of(n) == 2:
                            sp.dma_start(out_v[:, c:c + CW], stage[:, n % NSTAGE, :]).then_inc(stage_out[n % NSTAGE], 16)
                if kind == "gb":
                    sp.wait_ge(stage_mul, multiplied(STAGE_AT[b, NT - 1]))
                    sp.dma_start(tiles(ob_d)[:, :, c:c + CW], ob[:, :, c:c + CW]).then_inc(ob_out, 16)

            def qk_store(which):
                kind, j = which
                i = {"k": 0, "q": 2}[kind] + j
                sp.wait_ge(qk_ready, i + 1)
                c = j * CW
                src = qk_raw[i % 2]
                sp.dma_start(tiles(k_d if kind == "k" else q_d)[:, :, c:c + CW], src[:, :, :]).then_inc(qk_out[i % 2], 16)
                if kind == "k":
                    sp.dma_start(out_k[:, c:c + CW], src[:, NL, :]).then_inc(qk_out[i % 2], 16)
                if (kind, j) == ("q", 1):
                    sp.wait_ge(sq_free, 4)
                    sp.wait_ge(qk_out[0], 48)
                    sp.wait_ge(qk_out[1], 48)
                    sp.dma_start(ln_g[:, :], A["gmlp_ln_g"].broadcast_to([P, D])).then_inc(ln_in, 16)
                    sp.dma_start(ln_b[:, :], A["gmlp_ln_b"].broadcast_to([P, D])).then_inc(ln_in, 16)

            for b in range(FIRST_WO):
                load(2 * b + 3)
                load(2 * b + 4)
                stores(b)
            for n in range(2 * FIRST_WO + 3, PRE + NRAW):
                load(n)

            sp.wait_ge(qk_out[0], 48)
            sp.wait_ge(qk_out[1], 48)
            for s in range(NSTAGE):
                last = max(n for n in range(len(STAGED)) if n % NSTAGE == s and stores_of(n))
                sp.wait_ge(stage_out[s], stage_stored(last))
            sp.wait_ge(ob_out, 32)
            sp.wait_ge(grow_out[0], 32)
            sp.wait_ge(grow_out[1], 32)

            def load_head(h):
                p = h % 2
                if h == 0:
                    sp.wait_ge(piece_done, len(PIECES))
                if h >= 2:
                    sp.wait_ge(pv_done, NT * (h - 1))
                c = slice(h * P, h * P + P)
                sp.dma_start(q_h[:, p], tiles(q_d)[:, :, c]).then_inc(qkv_in[p], 16)
                sp.dma_start(k_h[:, p, 0:NPAST], ck[:, :, h, :]).then_inc(qkv_in[p], 16)
                sp.dma_start(k_h[:, p, NPAST:], tiles(k_d)[:, :, c]).then_inc(qkv_in[p], 16)
                sp.dma_start(v_h[:, p, 0:NPAST], cv[:, :, h, :]).then_inc(qkv_in[p], 16)
                sp.dma_start(v_h[:, p, NPAST:], tiles(v_d)[:, :, c]).then_inc(qkv_in[p], 16)

            for h in range(H):
                load_head(h)
            sp.wait_ge(o_ev, NU)
            sp.dma_start(x2[:, 0:NL, :], x_l).then_inc(x2_in, 16)
            sp.dma_start(x2[:, NL:NT, :], x_c).then_inc(x2_in, 16)
            for i in range(2):
                sp.dma_start(gate1[:, i, :], gate_d[i, 0:1, :].broadcast_to([P, D])).then_inc(x2_in, 16)
            for t in range(NT):
                if t >= 1:
                    sp.wait_ge(sa_used, t)
                sp.dma_start(sa_t[:, :], sa_d[t * P:(t + 1) * P, :]).then_inc(sa_in, 16)
                sp.dma_start(ob_t[:, :], ob_d[t * P:(t + 1) * P, :]).then_inc(sa_in, 16)
            for t in range(NT):
                sp.wait_ge(x2_ready, t + 1)
                sp.dma_start(x2_d[t * P:(t + 1) * P, :], x2[:, t, :]).then_inc(x2_out, 16)
            sp.wait_ge(idx_ready, 1)
            sp.dma_start(idx_d, idx_f[:, :]).then_inc(idx_out, 16)
            sp.wait_ge(idx_out, 16)
            sp.dma_start(idx_b[:, :, :].rearrange("p e c -> p (e c)"),
                         idx_d.rearrange("e c -> (e c)").unsqueeze(0).broadcast_to([P, E * CAP])).then_inc(idxb_in, 16)
            sp.dma_start(tokens[:, :], A["tokens"]).then_inc(tok_in, 16)

            def expert_loads(e, last):
                for i in range(EC):
                    j = i + NRAW
                    if j >= EC and last:
                        continue
                    slot = (PRE + j) % NRAW
                    src = expert_source(e, j) if j < EC else expert_source(e + 1, j - EC)
                    if not last:
                        sp.lower_val(src.offset * 4)
                    sp.wait_ge(lo_done, e * EC + (PRE + i + 1))
                    sp.dma_start(raw[:, slot], src).then_inc(raw_in[slot], 16)

            with sp.Fori(0, E - 1) as e:
                expert_loads(e, False)
            expert_loads(E - 1, True)

            sp.wait_ge(sc2_done, 2 * NT * E)
            sp.wait_ge(x2_out, 16 * NT)
            sp.dma_start(x2_end[:, :, :], tiles(x2_d)).then_inc(end_in, 16)
            for i in range(2):
                sp.dma_start(gate2[:, i, :], gate_d[i, 1:2, :].broadcast_to([P, D])).then_inc(end_in, 16)
            for t in range(NT):
                sp.wait_ge(y_ready, t + 1)
                out = y_l[:, t, :] if t < NL else y_c[:, 0, :]
                sp.dma_start(out, x2_end[:, t, :]).then_inc(y_out, 16)
            sp.wait_ge(y_out, 16 * NT)

        @block.scalar
        def _(act):
            def hi(n):
                act.wait_ge(raw_in[n % NRAW], raw_count(n))
                if n >= NSPLIT:
                    wait_read(act, n - NSPLIT)
                nc.scalar.activation(w_hi[:, n % NSPLIT], raw[:, n % NRAW], ACT.Copy).then_inc(hi_done, 1)

            def ahead(b):
                hi(2 * b + 2)
                hi(2 * b + 3)

            def take_root(n, width):
                act.wait_ge(var_ready, n + 1)
                nc.scalar.activation(root[:, 0:width], var[:, 0:width], ACT.Sqrt).then_inc(root_done, 1)

            act.wait_ge(cols_ready, 1)
            nc.scalar.activation(silu_c[:, :, :].rearrange("p a k -> p (a k)"), cols[:, 0:16], ACT.Silu).then_inc(silu_ready, 1)
            hi(0)
            hi(1)
            act.wait_ge(x_load, 32)
            for t in range(NT):
                if t >= 1:
                    act.wait_ge(ssum_ready, t)
                nc.scalar.activation(x_junk[:, :], x_in[:, t, :], ACT.Square, accum_out=newton[:, t:t + 1]).then_inc(ssum_ready, 1)
            take_root(0, NT)
            act.wait_ge(lam_e, 1)
            nc.scalar.activation(lam[:, 2:4], lam[:, 0:2], ACT.Exp).then_inc(lam_x, 1)

            roots = [1]
            qk_pending = []
            for b in range(FIRST_WO):
                kind, j = BLOCKS[b]
                ahead(b)
                if qk_pending:
                    take_root(roots[0], 8 * NT)
                    roots[0] += 1
                    qk_pending.clear()
                if kind == "ga" and j == 0:
                    take_root(roots[0], NT)
                    roots[0] += 1
                if kind == "ada":
                    act.wait_ge(ada_done, j + 1)
                    if j >= 2:
                        act.wait_ge(conv_done, j - 1)
                    nc.scalar.activation(m4[:, j % 2, :], bank(6)[0:4, :], ACT.Copy).then_inc(m4_ready, 1)
                    if j == 3:
                        for p in range(2 * NT):
                            act.wait_ge(ev_dve, p + 1)
                            src = stage[:, p % NSTAGE, :]
                            if p < KT:
                                out = h_hi[:, p, 0:LAT]
                            else:
                                k0 = 4 * (p - KT)
                                out = h_hi[:, k0:k0 + 4, LAT:TOK]
                                src = src.rearrange("p (k t) -> p k t", k=4)
                            nc.scalar.activation(out, src, ACT.Copy).then_inc(h_hi_ready, 1)
                    continue
                for t in range(NT):
                    n = PIECE_AT[b, t]
                    act.wait_ge(piece_done, n + 1)
                    ps = bank(n % RING)
                    if kind in ("q", "k"):
                        i = {"k": 0, "q": 2}[kind] + j
                        if t == 0 and i >= 2:
                            act.wait_ge(qk_out[i % 2], 32)
                        if t == 0 and i >= 1:
                            act.wait_ge(sq_free, i)
                        swapped = qk_swp[i % 2][:, t, :].rearrange("p (a s c) -> p a s c", s=2, c=HD // 4)[:, :, ::-1, :]
                        nc.scalar.activation(qk_raw[i % 2][:, t, :], ps, ACT.Copy)
                        nc.scalar.activation(swapped, ps.rearrange("p (a s c) -> p a s c", s=2, c=HD // 4), ACT.Copy)
                        nc.scalar.activation(qk_sq[:, t, :], ps, ACT.Square).then_inc(ev_act, 1)
                        qk_pending.append(1)
                    elif kind == "zv":
                        if t == 0 and j == 0:
                            act.wait_ge(qk_out[0], 48)
                            act.wait_ge(qk_out[1], 48)
                        nc.scalar.activation(ob[:, t, j * CW:(j + 1) * CW], ps, ACT.Gelu_apprx_tanh).then_inc(ev_act, 1)
                    else:
                        s = STAGE_AT[b, t]
                        if s >= NSTAGE:
                            m = s - NSTAGE
                            if stores_of(m):
                                act.wait_ge(stage_out[m % NSTAGE], stage_stored(m))
                            else:
                                act.wait_ge(stage_mul, multiplied(m))
                        func = {"v": ACT.Copy, "ga": ACT.Sigmoid, "gb": ACT.Sigmoid, "zu": ACT.Gelu_apprx_tanh}[kind]
                        nc.scalar.activation(stage[:, s % NSTAGE, :], ps, func).then_inc(ev_act, 1)
            ahead(FIRST_WO)

            seen = [0]

            def copy_out(want):
                while seen[0] < want:
                    n = seen[0]
                    what, which, first, k = TRANSPOSED[n]
                    act.wait_ge(tr_done, n + 1)
                    ps = bank(4 + n % 2)
                    if what == "a":
                        if which >= 2 and first == 0:
                            act.wait_ge(pv_done, which - 1)
                        out = aT[:, which % 2, first * P:(first + k) * P]
                        nc.scalar.activation(out, ps[:, 0:k * P], ACT.Copy).then_inc(tr_ev, 1)
                    elif first < 4:
                        nc.scalar.activation(qT[:, which % 2, 0:4 * P], ps[:, 0:4 * P], ACT.Copy).then_inc(tr_ev, 1)
                    elif first < 8:
                        nc.scalar.activation(qT[:, which % 2, 4 * P:5 * P], ps[:, 0:P], ACT.Copy)
                        nc.scalar.activation(kT[:, which % 2, 0:3 * P], ps[:, P:4 * P], ACT.Copy).then_inc(tr_ev, 1)
                    else:
                        nc.scalar.activation(kT[:, which % 2, 3 * P:7 * P], ps[:, 0:4 * P], ACT.Copy).then_inc(tr_ev, 1)
                    seen[0] += 1

            copy_out(transposed_upto("qk", 0))
            for u in range(NU):
                nk = unit_keys(u)[1] * P
                for s in range(2):
                    act.wait_ge(nb_done[s], u + 1)
                    if u >= 2 and s == 0:
                        act.wait_ge(tr_done, transposed_upto("a", u - 2))
                    if u == 0 and s == 0:
                        act.wait_ge(ob_out, 32)
                    out = (p_0, p_1)[s][:, u % 2, 0:nk]
                    nc.scalar.activation(out, bank_all[:, 2 * s:2 * s + 2, :].rearrange("p a n -> p (a n)")[:, 0:nk], ACT.Exp,
                                         bias=nbias[:, u % 2, s:s + 1], scale=HD ** -0.5,
                                         accum_out=rsum[:, u % 2, s:s + 1]).then_inc(exp_done[s], 1)
                if u >= 1:
                    copy_out(transposed_upto("a", u - 1))
                if u % NT == 2 and u // NT + 1 < H:
                    copy_out(transposed_upto("qk", u // NT + 1))
            copy_out(len(TRANSPOSED))

            for t in range(NT):
                act.wait_ge(o_ev, NU)
                if t >= 1:
                    act.wait_ge(merged, t)
                nc.scalar.activation(p_sq[:, :], o_t[:, t, :], ACT.Square).then_inc(osq_ready, 1)
            take_root(roots[0], 8 * NT)
            roots[0] += 1
            for p in range(2 * NT):
                t, half = p // 2, p % 2
                act.wait_ge(p2_done, p + 1)
                nc.scalar.activation(m_hi[:, 4 * half:4 * half + 4, t * P:(t + 1) * P],
                                     bank(p % RING).rearrange("p (k t) -> p k t", k=4), ACT.Copy).then_inc(mhi_ready, 1)
            hi(2 * FIRST_WO + 4)
            hi(2 * FIRST_WO + 5)
            for t in range(NT):
                act.wait_ge(x2_ready, t + 1)
                nc.scalar.activation(p_sq[:, :], x2[:, t, :], ACT.Square, accum_out=newton[:, 8 + t:9 + t]).then_inc(x2_sq, 1)
                take_root(roots[0], 1)
                roots[0] += 1
            hi(2 * FIRST_WO + 6)
            for t in range(NT):
                act.wait_ge(xn2_ready, t + 1)
                nc.scalar.activation(xn_hi[:, t, :], xn[t % 2][:, :], ACT.Copy).then_inc(xnhi_ready, 1)
            for t in range(NT):
                act.wait_ge(lgb_ready, t + 1)
                nc.scalar.activation(lg[:, t, :], lg[:, t, :], ACT.Exp, bias=rst[:, t, 0:1], scale=1.0,
                                     accum_out=rst[:, t, 1:2]).then_inc(lge_ready, 1)

            act.wait_ge(p2_ev, N_P2)

            def expert(e, first, last):
                for i in range(EC):
                    j = i + NRAW
                    if not (last and j >= EC):
                        act.wait_ge(raw_in[(PRE + j) % NRAW], e * (16 * EC // NRAW) + 16 * ((PRE + j) // NRAW + 1))
                        if first and j < NSPLIT:
                            wait_read(act, PRE + j - NSPLIT)
                        else:
                            act.wait_ge(used, e * EC + (j - NSPLIT + 1))
                        nc.scalar.activation(w_hi[:, j % NSPLIT], raw[:, (PRE + j) % NRAW], ACT.Copy).then_inc(hi_done, 1)
                    if i < 16 and i % 4 == 2:
                        fb = i // 4
                        act.wait_ge(used, e * EC + (i))
                        if not first or fb >= 2:
                            act.wait_ge(hid_ready, e * 4 + (fb - 1))
                        nc.scalar.activation(sg[:, fb % 2, :], bank(fb % 2 * 2)[0:CAP, :], ACT.Silu).then_inc(sg_ready, 1)
                    fb = HT_STEP.get(i)
                    if fb is not None:
                        act.wait_ge(ht_done, e * 4 + (fb + 1))
                        nc.scalar.activation(hT_hi[:, 4 * fb:4 * fb + 4, :], bank(6)[:, 0:4 * CAP].rearrange("p (k c) -> p k c", k=4),
                                             ACT.Copy).then_inc(hth_ready, 1)
                    if i in (20, 23):
                        half = int(i == 23)
                        act.wait_ge(used, e * EC + (20 + 4 * half))
                        nc.scalar.activation(ye_hi[:, half * CW:(half + 1) * CW], bank(4 + half)[0:CAP, :],
                                             ACT.Copy).then_inc(yeh_ready, 1)

            expert(0, True, False)
            with act.Fori(1, E - 1) as e:
                expert(e, False, False)
            expert(E - 1, False, True)

        @block.vector
        def _(dve):
            chain = [0]

            def link(ins):
                chain[0] += 1
                ins.then_inc(dv, 1)
                dve.wait_ge(dv, chain[0])

            def lo(n):
                dve.wait_ge(hi_done, n + 1)
                nc.vector.tensor_tensor(w_lo[:, n % NSPLIT], raw[:, n % NRAW], w_hi[:, n % NSPLIT], ALU.subtract).then_inc(lo_done, 1)

            def ahead(b):
                lo(2 * b + 2)
                lo(2 * b + 3)

            rooted = [0]

            def ask_root(ins):
                ins.then_inc(var_ready, 1)

            def finish_root(width, signal=None):
                rooted[0] += 1
                dve.wait_ge(root_done, rooted[0])
                r, t, v = rstd[:, 0:width], newton[:, 0:width], var[:, 0:width]
                link(nc.vector.reciprocal(r, root[:, 0:width]))
                link(nc.vector.tensor_tensor(t, r, r, ALU.mult))
                link(nc.vector.tensor_tensor(t, t, v, ALU.mult))
                link(nc.vector.tensor_scalar(t, t, -0.5, 1.5, ALU.mult, ALU.add))
                last = nc.vector.tensor_tensor(r, r, t, ALU.mult)
                if signal is None:
                    link(last)
                else:
                    last.then_inc(signal[0], 1)
                    dve.wait_ge(*signal)

            dve.wait_ge(rowsT_done, 1)
            nc.vector.tensor_copy(cols[:, :], bank(7)[:, 0:40]).then_inc(cols_ready, 1)
            dve.wait_ge(silu_ready, 1)
            sc = silu_c[:, :, :].rearrange("p a k -> p k a")
            link(nc.vector.tensor_copy(cond[:, :, 0:2], sc))
            nc.vector.tensor_tensor(cond[:, :, 2:4], sc, cond[:, :, 0:2], ALU.subtract).then_inc(cond_ready, 1)
            lo(0)
            lo(1)
            dve.wait_ge(ssum_ready, NT)
            ask_root(nc.vector.tensor_scalar(var[:, 0:NT], newton[:, 0:NT], 1.0 / D, EPS, ALU.mult, ALU.add))
            dve.wait_ge(var_ready, 1)
            finish_root(NT)
            for t in range(NT):
                nc.vector.tensor_scalar(x_in[:, t, :], x_in[:, t, :], rstd[:, t:t + 1], None, ALU.mult).then_inc(xn_ready, 1)
            dve.wait_ge(lam_in, 16 * 9)
            for i in range(2):
                link(nc.vector.tensor_tensor(lamv[:, 2 * i, :], lamv[:, 2 * i, :], lamv[:, 2 * i + 1, :], ALU.mult))
            nc.vector.tensor_reduce(lam[:, 0:2], lamv[:, :, :].rearrange("p (a b) d -> p a b d", b=2)[:, :, 0, :], axis=AX.X,
                                    op=ALU.add).then_inc(lam_e, 1)
            dve.wait_ge(lam_x, 1)
            link(nc.vector.tensor_tensor(lam[:, 4:5], lam[:, 2:3], lam[:, 3:4], ALU.subtract))
            link(nc.vector.tensor_scalar(lam[:, 5:6], lam[:, 4:5], LAMBDA_INIT, None, ALU.add))
            for i in range(2):
                for c in range(2):
                    g = gain[:, i, :].rearrange("p (a s c) -> p a s c", s=2, c=HD // 4)
                    g = g[:, :, ::-1, :] if c else g
                    for t in range(NT):
                        v = tab[:, i, c, t, :].rearrange("p (a s c) -> p a s c", s=2, c=HD // 4)
                        nc.vector.tensor_tensor(v, v, g, ALU.mult)
            nc.vector.tensor_scalar(g_sub[:, :], g_sub[:, :], 1.0 - LAMBDA_INIT, None, ALU.mult).then_inc(tab_ready, 1)
            dve.wait_ge(tab_ready, 1)
            for i in range(2):
                dve.wait_ge(wspT_done, i + 1)
                nc.vector.tensor_copy(wspT[:, 4 * i:4 * i + 4, :].rearrange("p g q -> p (g q)"), bank(5)[:, :]).then_inc(wspT_ready, 1)

            def conv(a):
                dve.wait_ge(conv_done, a + 1)
                if a in GATES:
                    g = GATES.index(a)
                    if g >= 2:
                        dve.wait_ge(grow_out[g % 2], 16)
                    nc.vector.tensor_copy(grow[:, g % 2, :], bank(7)[0:2, :]).then_inc(conv_ev, 1)
                else:
                    nc.vector.tensor_copy(mcol[:, VEC[a], 4 * (a % 2):4 * (a % 2) + 4, :].rearrange("p k c -> p (k c)"),
                                          bank(7)[:, 0:8]).then_inc(conv_ev, 1)
                dve.wait_ge(conv_ev, a + 1)

            def amplitude(out, vec, first):
                g = cols[:, first:first + KT].unsqueeze(2).broadcast_to([P, KT, 2])
                link(nc.vector.scalar_tensor_tensor(out=out[:, :, :], in0=mcol[:, vec, :, :], scalar=1.0, in1=g,
                                                    op0=ALU.add, op1=ALU.mult))

            def modulated(out, ps, k, n, amp, shift):
                v = ps.rearrange("p (k t) -> p k t", k=n)
                o = out.rearrange("p (k t) -> p k t", k=n)
                link(nc.vector.tensor_tensor(o, v, amp.unsqueeze(2).broadcast_to([P, n, P]), ALU.mult))
                return nc.vector.tensor_tensor(o, o, shift.unsqueeze(2).broadcast_to([P, n, P]), ALU.add)

            pending = []
            i_qk = [0]

            def qk_first():
                n = pending[0]
                dve.wait_ge(ev_act, emptied_before(PIECE_AT[n, NT - 1] + 1, "act"))
                nc.vector.tensor_reduce(var[:, 0:8 * NT], qk_sq[:, :, :].rearrange("p t (s d) -> p (t s) d", d=HD), axis=AX.X,
                                        op=ALU.add).then_inc(sq_free, 1)
                dve.wait_ge(sq_free, i_qk[0] + 1)
                nc.vector.tensor_scalar(var[:, 0:8 * NT], var[:, 0:8 * NT], 1.0 / HD, EPS, ALU.mult, ALU.add).then_inc(var_ready, 1)

            def qk_rest():
                i = i_qk[0]
                dve.wait_ge(var_ready, rooted[0] + 1)
                finish_root(8 * NT, (rstd_ready, i + 1))
                v = qk_raw[i % 2][:, :, :].rearrange("p t (s d) -> p (t s) d", d=HD)
                link(nc.vector.tensor_tensor(v, v, rstd[:, 0:8 * NT].unsqueeze(2).broadcast_to([P, 8 * NT, HD]), ALU.mult))
                c = tab[:, 1 if i < 2 else 0, 0]
                for t in range(NT):
                    w = qk_raw[i % 2][:, t, :].rearrange("p (s d) -> p s d", d=HD)
                    last = nc.vector.tensor_tensor(w, w, c[:, t, :].unsqueeze(1).broadcast_to([P, 8, HD]), ALU.mult)
                link(last)
                dve.wait_ge(swp_ready, i + 1)
                nc.vector.tensor_tensor(qk_raw[i % 2][:, :, :], qk_raw[i % 2][:, :, :], qk_swp[i % 2][:, :, :], ALU.add).then_inc(qk_ready, 1)
                i_qk[0] += 1
                pending.clear()

            converted = [0]
            for b in range(FIRST_WO):
                kind, j = BLOCKS[b]
                if pending:
                    qk_first()
                ahead(b)
                if pending:
                    qk_rest()
                if kind == "ada" and b < 4:
                    if j >= 1:
                        conv(j - 1)
                    if j == 3:
                        conv(3)
                        amplitude(amp1, 1, 16)
                        for p in range(2 * NT):
                            dve.wait_ge(piece_done, p + 1)
                            if p >= NSTAGE:
                                dve.wait_ge(h_ready, p - NSTAGE + 1)
                            if p < KT:
                                last = nc.vector.tensor_scalar(stage[:, p % NSTAGE, :], bank(p % RING), amp1[:, p, 0:1], mcol[:, 0, p, 0:1],
                                                               ALU.mult, ALU.add)
                            else:
                                k0 = 4 * (p - KT)
                                last = modulated(stage[:, p % NSTAGE, :], bank(p % RING), k0, 4, amp1[:, k0:k0 + 4, 1], mcol[:, 0, k0:k0 + 4, 1])
                            last.then_inc(ev_dve, 1)
                    continue
                if kind in ("q", "k"):
                    pending.append(b)
                if kind == "ga" and j == 0:
                    for t in range(NT):
                        last = nc.vector.bn_aggr(mv[:, t, :], bstat[:, t, :, :].rearrange("p a s -> p (a s)"))
                    link(last)
                    nc.vector.tensor_scalar(var[:, 0:NT], mv[:, :, 1], EPS, None, ALU.add).then_inc(var_ready, 1)
                    dve.wait_ge(var_ready, rooted[0] + 1)
                    finish_root(NT)
                    dve.wait_ge(ln_in, 32)
                    for t in range(NT):
                        link(nc.vector.tensor_scalar(ob[:, t, :], ob[:, t, :], mv[:, t, 0:1], rstd[:, t:t + 1], ALU.subtract, ALU.mult))
                        nc.vector.tensor_tensor(ob[:, t, :], ob[:, t, :], ln_g[:, :], ALU.mult).then_inc(zn_pre, 1)
                for t in range(NT):
                    if kind == "zv":
                        n = PIECE_AT[b, t]
                        dve.wait_ge(ev_act, emptied_before(n + 1, "act"))
                        last = nc.vector.bn_stats(bstat[:, t, j, :], ob[:, t, j * CW:(j + 1) * CW])
                        if t == NT - 1:
                            link(last)
                    if kind in ("zu", "gb"):
                        s = STAGE_AT[b, t]
                        dve.wait_ge(ev_act, emptied_before(PIECE_AT[b, t] + 1, "act"))
                        if kind == "gb":
                            dve.wait_ge(stage_mul, multiplied(STAGE_AT[BLOCKS.index(("zu", j)), t]))
                        w = ob[:, t, j * CW:(j + 1) * CW]
                        nc.vector.tensor_tensor(w, w, stage[:, s % NSTAGE, :], ALU.mult).then_inc(stage_mul, 1)
                    if t == 0 and b > 4 and BLOCKS[b - 1][0] == "ada":
                        conv(BLOCKS[b - 1][1])
                if b == SPATIAL_AFTER:
                    for i in range(2 * NT):
                        t, half = i // 2, i % 2
                        n = PIECE_AT["sp", i]
                        dve.wait_ge(piece_done, n + 1)
                        w = ob[:, t, half * CW:(half + 1) * CW].rearrange("p (g c) -> p g c", c=P)
                        bias = cols[:, 32 + 4 * half:36 + 4 * half].unsqueeze(2).broadcast_to([P, 4, P])
                        nc.vector.tensor_tensor(w, bank(n % RING).rearrange("p (g c) -> p g c", c=P), bias, ALU.add).then_inc(ev_dve, 1)
                    dve.wait_ge(ev_dve, emptied_before(PIECE_AT["sp", 2 * NT - 1] + 1, "dve"))
            ahead(FIRST_WO)
            amplitude(amp2, 3, 24)

            def combine(u):
                p, nk = u % 2, unit_keys(u)[1] * P
                dve.wait_ge(exp_done[0], u + 1)
                dve.wait_ge(exp_done[1], u + 1)
                link(nc.vector.reciprocal(rinv[:, :], rsum[:, p, :]))
                link(nc.vector.tensor_tensor(rinv[:, 1:2], rinv[:, 1:2], lam[:, 5:6], ALU.mult))
                link(nc.vector.tensor_scalar(p_1[:, p, 0:nk], p_1[:, p, 0:nk], rinv[:, 1:2], None, ALU.mult))
                nc.vector.scalar_tensor_tensor(out=p_0[:, p, 0:nk], in0=p_0[:, p, 0:nk], scalar=rinv[:, 0:1], in1=p_1[:, p, 0:nk],
                                               op0=ALU.mult, op1=ALU.subtract).then_inc(a_done, 1)

            def o_out(u):
                h, t = u // NT, u % NT
                dve.wait_ge(pv_done, u + 1)
                if u == 0:
                    dve.wait_ge(ob_out, 32)
                nc.vector.tensor_copy(o_t[:, t, h * P:(h + 1) * P], bank(6 + u % 2)[:, 0:P]).then_inc(o_ev, 1)

            for u in range(NU):
                nk = unit_keys(u)[1] * P
                for s in range(2):
                    dve.wait_ge(sc_done[s], u + 1)
                    if u == 0 and s == 0:
                        dve.wait_ge(ob_out, 32)
                    nb = nbias[:, u % 2, s:s + 1]
                    src = bank_all[:, 2 * s:2 * s + 2, :].rearrange("p a n -> p (a n)")[:, 0:nk]
                    link(nc.vector.tensor_reduce(nb, src, axis=AX.X, op=ALU.max))
                    nc.vector.tensor_scalar(nb, nb, -HD ** -0.5, None, ALU.mult).then_inc(nb_done[s], 1)
                if u >= 1:
                    combine(u - 1)
                if u >= 2:
                    o_out(u - 2)
            combine(NU - 1)
            o_out(NU - 2)
            o_out(NU - 1)
            dve.wait_ge(o_ev, NU)

            for t in range(NT):
                dve.wait_ge(osq_ready, t + 1)
                nc.vector.tensor_reduce(var[:, 8 * t:8 * t + 8], p_sq[:, :].rearrange("p (h d) -> p h d", d=VD), axis=AX.X, op=ALU.add).then_inc(merged, 1)
            dve.wait_ge(merged, NT)
            nc.vector.tensor_scalar(var[:, 0:8 * NT], var[:, 0:8 * NT], 1.0 / VD, EPS, ALU.mult, ALU.add).then_inc(var_ready, 1)
            dve.wait_ge(var_ready, rooted[0] + 1)
            finish_root(8 * NT)
            for t in range(NT):
                o3 = o_t[:, t, :].rearrange("p (h d) -> p h d", d=VD)
                link(nc.vector.tensor_tensor(o3, o3, rstd[:, 8 * t:8 * t + 8].unsqueeze(2).broadcast_to([P, H, VD]), ALU.mult))
                link(nc.vector.tensor_tensor(o3, o3, g_sub[:, :].unsqueeze(1).broadcast_to([P, H, VD]), ALU.mult))
                dve.wait_ge(sa_in, 32 * (t + 1))
                link(nc.vector.tensor_tensor(o_t[:, t, :], o_t[:, t, :], sa_t[:, :], ALU.mult))
                nc.vector.tensor_tensor(o_t[:, t, :], o_t[:, t, :], ob_t[:, :], ALU.add).then_inc(sa_used, 1)
            n2 = [0]
            for p in range(2 * NT):
                t, half = p // 2, p % 2
                dve.wait_ge(mhi_ready, p + 1)
                mh = m_hi[:, 4 * half:4 * half + 4, t * P:(t + 1) * P]
                ml = m_lo[:, 4 * half:4 * half + 4, t * P:(t + 1) * P]
                nc.vector.tensor_tensor(ml, bank(p % RING).rearrange("p (k t) -> p k t", k=4), mh, ALU.subtract).then_inc(p2_ev, 1)
                n2[0] += 1
            dve.wait_ge(x2_in, 64)
            for half in range(2):
                if half == 1:
                    lo(2 * FIRST_WO + 4)
                    lo(2 * FIRST_WO + 5)
                for t in range(NT):
                    n = n2[0]
                    dve.wait_ge(p2_done, n + 1)
                    c = slice(half * CW, (half + 1) * CW)
                    tmp = xw[:, (n % 2) * CW:(n % 2 + 1) * CW]
                    nc.vector.tensor_tensor(tmp, bank(n % RING), gate1[:, int(t == NL), c], ALU.mult).then_inc(p2_ev, 1)
                    n2[0] += 1
                    dve.wait_ge(p2_ev, n2[0])
                    last = nc.vector.tensor_tensor(x2[:, t, c], x2[:, t, c], tmp, ALU.add)
                    if half == 1:
                        last.then_inc(x2_ready, 1)
            for t in range(NT):
                dve.wait_ge(x2_sq, t + 1)
                nc.vector.tensor_scalar(var[:, 0:1], newton[:, 8 + t:9 + t], 1.0 / D, EPS, ALU.mult, ALU.add).then_inc(var_ready, 1)
                dve.wait_ge(var_ready, rooted[0] + 1)
                finish_root(1)
                link(nc.vector.tensor_copy(rst5[:, t:t + 1], rstd[:, 0:1]))
            lo(2 * FIRST_WO + 6)
            dve.wait_ge(wr_in, 32)
            for t in range(NT):
                if t >= 2:
                    dve.wait_ge(p2_done, n2[0])
                nc.vector.tensor_scalar(xn[t % 2][:, :], x2[:, t, :], rst5[:, t:t + 1], None, ALU.mult).then_inc(xn2_ready, 1)
                dve.wait_ge(xnhi_ready, t + 1)
                link(nc.vector.tensor_tensor(xn_lo[:, t, :], xn[t % 2][:, :], xn_hi[:, t, :], ALU.subtract))
                cd = int(t == NL)
                for half in range(2):
                    n = n2[0]
                    dve.wait_ge(p2_done, n + 1)
                    k = 4 * half
                    last = modulated(h2T[t % 2][:, k:k + 4, :].rearrange("p k t -> p (k t)"), bank(n % RING), k, 4,
                                     amp2[:, k:k + 4, cd], mcol[:, 2, k:k + 4, cd])
                    last.then_inc(p2_ev, 1)
                    n2[0] += 1
                    dve.wait_ge(p2_ev, n2[0])
                n = n2[0]
                dve.wait_ge(p2_done, n + 1)
                nc.vector.tensor_copy(lg[:, t, :], bank(n % RING)[:, 0:E]).then_inc(p2_ev, 1)
                n2[0] += 1
                dve.wait_ge(p2_ev, n2[0])
                link(nc.vector.tensor_reduce(rst[:, t, 2:3], lg[:, t, :], axis=AX.X, op=ALU.max))
                nc.vector.tensor_scalar(rst[:, t, 0:1], rst[:, t, 2:3], -1.0, None, ALU.mult).then_inc(lgb_ready, 1)
            for t in range(NT):
                dve.wait_ge(lge_ready, t + 1)
                link(nc.vector.reciprocal(rst[:, t, 3:4], rst[:, t, 1:2]))
                nc.vector.tensor_scalar(lg[:, t, :], lg[:, t, :], rst[:, t, 3:4], None, ALU.mult).then_inc(aff_ready, 1)
            for t in range(NT):
                n = n2[0]
                dve.wait_ge(p2_done, n + 1)
                nc.vector.tensor_copy(affT[:, t * P:(t + 1) * P], bank(n % RING)[0:E, 0:P]).then_inc(p2_ev, 1)
                n2[0] += 1
            dve.wait_ge(p2_ev, n2[0])
            for start, width, cap, off in ((0, LAT, CAP_L, 0), (LAT, CTX, CAP_C, CAP_L)):
                bufs = [affT, affW]
                for r in range(cap // 8):
                    v = gate_v[:, off + 8 * r:off + 8 * r + 8]
                    src, dst = bufs[r % 2][:, start:start + width], bufs[(r + 1) % 2][:, start:start + width]
                    link(nc.vector.max(v, src))
                    link(nc.vector.max_index(idx_u[:, off + 8 * r:off + 8 * r + 8], v, src))
                    if r < cap // 8 - 1:
                        link(nc.vector.match_replace(dst, v, src, -1.0))
            link(nc.vector.tensor_copy(idx_f[:, :], idx_u[:, :]))
            nc.vector.tensor_scalar(idx_f[:, CAP_L:CAP], idx_f[:, CAP_L:CAP], float(LAT), None, ALU.add).then_inc(idx_ready, 1)
            for dst in (idx_c, gate_c):
                n = n2[0]
                dve.wait_ge(p2_done, n + 1)
                nc.vector.tensor_copy(dst[:, :], bank(n % RING)[0:CAP, 0:E]).then_inc(p2_ev, 1)
                n2[0] += 1
            dve.wait_ge(p2_ev, n2[0])
            dve.wait_ge(idxb_in, 16)
            dve.wait_ge(x2_out, 16 * NT)
            for t in range(NL):
                nc.vector.tensor_scalar(sel_l[:, t, :, :], idx_b[:, :, 0:CAP_L], token[:, t:t + 1], None, ALU.is_equal)
            nc.vector.tensor_scalar(sel_c[:, :, :], idx_b[:, :, CAP_L:CAP], token[:, NL:NT], None, ALU.is_equal).then_inc(sel_ready, 1)
            xe4 = xeT[:, :, :].rearrange("p e (k c) -> p e k c", k=KT)
            for k in range(KT):
                for part in range(3):
                    n = n2[0]
                    dve.wait_ge(p2_done, n + 1)
                    if part < 2:
                        out, src, cd = xe4[:, 8 * part:8 * part + 8, k, 0:CAP_L], bank(n % RING).rearrange("p (e c) -> p e c", c=CAP_L), 0
                    else:
                        out, src, cd = xe4[:, :, k, CAP_L:CAP], bank(n % RING)[:, 0:E * CAP_C].rearrange("p (e c) -> p e c", c=CAP_C), 1
                    nc.vector.tensor_scalar(out, src, amp2[:, k, cd:cd + 1], mcol[:, 2, k, cd:cd + 1], ALU.mult, ALU.add).then_inc(p2_ev, 1)
                    n2[0] += 1
            assert n2[0] == N_P2, n2[0]
            dve.wait_ge(p2_ev, N_P2)
            dve.wait_ge(tok_in, 16)

            nc.vector.memset(yacc[:, :, :], 0.0).then_inc(sc2_ev, 1)
            dve.wait_ge(sc2_ev, 1)
            link(nc.vector.tensor_scalar(xe_hi[:, :], xeT[:, 0, :], 1.0, None, ALU.mult))
            nc.vector.tensor_tensor(xe_lo[:, :], xeT[:, 0, :], xe_hi[:, :], ALU.subtract).then_inc(xe_ready, 1)

            def expert(e, first, last):
                def col(a, x):
                    return a[:, x:x + 1] if isinstance(x, int) else a[:, bass.ds(x, 1)]

                for i in range(EC):
                    j = i + NRAW
                    if not (last and j >= EC):
                        dve.wait_ge(hi_done, e * EC + (PRE + j + 1))
                        nc.vector.tensor_tensor(w_lo[:, j % NSPLIT], raw[:, (PRE + j) % NRAW], w_hi[:, j % NSPLIT],
                                                ALU.subtract).then_inc(lo_done, 1)
                    if i < 16 and i % 4 == 3:
                        fb = i // 4
                        dve.wait_ge(sg_ready, e * 4 + (fb + 1))
                        dve.wait_ge(used, e * EC + (i + 1))
                        if not first or fb >= 2:
                            dve.wait_ge(ht_done, e * 4 + (fb - 1))
                        nc.vector.scalar_tensor_tensor(out=hid[:, fb % 2, :], in0=bank(fb % 2 * 2 + 1)[0:CAP, :], scalar=col(gate_c, e),
                                                       in1=sg[:, fb % 2, :], op0=ALU.mult, op1=ALU.mult).then_inc(hid_ready, 1)
                    fb = HT_STEP.get(i)
                    if fb is not None:
                        dve.wait_ge(hth_ready, e * 4 + (fb + 1))
                        nc.vector.tensor_tensor(hT_lo[:, 4 * fb:4 * fb + 4, :], bank(6)[:, 0:4 * CAP].rearrange("p (k c) -> p k c", k=4),
                                                hT_hi[:, 4 * fb:4 * fb + 4, :], ALU.subtract).then_inc(ht_ready, 1)
                    if i == 16 and not last:
                        src = xeT[:, e + 1, :] if isinstance(e, int) else xeT[:, bass.ds(e + 1, 1), :].rearrange("p e n -> p (e n)")
                        dve.wait_ge(used, e * EC + 16)
                        nc.vector.tensor_scalar(xe_hi[:, :], src, 1.0, None, ALU.mult).then_inc(xeh_done, 1)
                        dve.wait_ge(xeh_done, e + 1)
                        nc.vector.tensor_tensor(xe_lo[:, :], src, xe_hi[:, :], ALU.subtract).then_inc(xe_ready, 1)
                    if i in (20, 23):
                        half = int(i == 23)
                        c = slice(half * CW, (half + 1) * CW)
                        dve.wait_ge(yeh_ready, e * 2 + (half + 1))
                        if half == 0:
                            nc.vector.tensor_scalar(selT[:, :], tokens[0:CAP, :], col(idx_c, e), None, ALU.is_equal)
                        nc.vector.tensor_tensor(ye_lo[:, c], bank(4 + half)[0:CAP, :], ye_hi[:, c], ALU.subtract).then_inc(ye_ready, 1)
                    if 2 <= i < 12 and not first:
                        added(e - 1, i - 2)

            def added(e, s):
                dve.wait_ge(sc2_done, e * (2 * NT) + (s + 1))
                w = yacc[:, s // 2, (s % 2) * CW:(s % 2 + 1) * CW]
                nc.vector.tensor_tensor(w, w, bank(7)[:, :], ALU.add).then_inc(sc2_ev, 1)

            expert(0, True, False)
            with dve.Fori(1, E - 1) as e:
                expert(e, False, False)
            expert(E - 1, False, True)
            for s in range(2 * NT):
                added(E - 1, s)
            dve.wait_ge(sc2_ev, 2 * NT * E + 1)
            dve.wait_ge(end_in, 48)
            for t in range(NT):
                link(nc.vector.tensor_tensor(yacc[:, t, :], yacc[:, t, :], gate2[:, int(t == NL), :], ALU.mult))
                nc.vector.tensor_tensor(x2_end[:, t, :], x2_end[:, t, :], yacc[:, t, :], ALU.add).then_inc(y_ready, 1)

        @block.gpsimd
        def _(pool):
            for p in range(2 * NT):
                pool.wait_ge(h_hi_ready, p + 1)
                src = stage[:, p % NSTAGE, :]
                if p < KT:
                    h, l = h_hi[:, p, 0:LAT], h_lo[:, p, 0:LAT]
                else:
                    k0 = 4 * (p - KT)
                    h, l = h_hi[:, k0:k0 + 4, LAT:TOK], h_lo[:, k0:k0 + 4, LAT:TOK]
                    src = src.rearrange("p (k t) -> p k t", k=4)
                nc.gpsimd.tensor_tensor(l, src, h, ALU.subtract).then_inc(h_ready, 1)
            pool.wait_ge(tab_ready, 1)
            for i in range(4):
                pool.wait_ge(rstd_ready, i + 1)
                w = qk_swp[i % 2]
                v = w[:, :, :].rearrange("p t (s d) -> p (t s) d", d=HD)
                nc.gpsimd.tensor_tensor(v, v, rstd[:, 0:8 * NT].unsqueeze(2).broadcast_to([P, 8 * NT, HD]), ALU.mult).then_inc(po, 1)
                pool.wait_ge(po, i + 1)
                s = tab[:, 1 if i < 2 else 0, 1]
                for t in range(NT):
                    x = w[:, t, :].rearrange("p (s d) -> p s d", d=HD)
                    last = nc.gpsimd.tensor_tensor(x, x, s[:, t, :].unsqueeze(1).broadcast_to([P, 8, HD]), ALU.mult)
                last.then_inc(swp_ready, 1)
            for t in range(NT):
                pool.wait_ge(zn_pre, t + 1)
                nc.gpsimd.tensor_tensor(ob[:, t, :], ob[:, t, :], ln_b[:, :], ALU.add).then_inc(zn_ready, 1)

        @block.tensor
        def _(pe):
            def split3(ps, hi, lo, wh, wl, first, last):
                nc.tensor.matmul(ps, hi, wh, start=first, stop=False)
                nc.tensor.matmul(ps, lo, wh, start=False, stop=False)
                return nc.tensor.matmul(ps, hi, wl, start=False, stop=last)

            def piece(n):
                if n >= RING:
                    who = PIECES[n - RING][2]
                    pe.wait_ge(ev_act if who == "act" else ev_dve, emptied_before(n - RING + 1, who))
                return bank(n % RING)

            def ada(a, b):
                pe.wait_ge(lo_done, 2 * b + 2)
                if a >= 1:
                    pe.wait_ge(m4_ready, a)
                ps = bank(6)[0:4, :]
                for n in (2 * b, 2 * b + 1):
                    for k in range(CK):
                        kk = (n % 2) * CK + k
                        nc.tensor.matmul(ps, cond[:, kk, :], w_hi[:, n % NSPLIT, k, :], start=(kk == 0), stop=False)
                        last = nc.tensor.matmul(ps, cond[:, kk, :], w_lo[:, n % NSPLIT, k, :], start=False, stop=(kk == KT - 1))
                last.then_inc(ada_done, 1)

            def conv(a):
                pe.wait_ge(m4_ready, a + 1)
                if a >= 1:
                    pe.wait_ge(conv_ev, a)
                if a in GATES:
                    nc.tensor.matmul(bank(7)[0:2, :], hilo[0:4, :], m4[:, a % 2, :], start=True, stop=False)
                    last = nc.tensor.matmul(bank(7)[0:2, :], pick[0:12, a, :], b12[:, :], start=False, stop=True)
                else:
                    for k in range(4):
                        out = bank(7)[:, 2 * k:2 * k + 2]
                        nc.tensor.matmul(out, m4[:, a % 2, k * P:(k + 1) * P], hilo[0:4, :], start=True, stop=False)
                        last = nc.tensor.matmul(out, b12[:, k * P:(k + 1) * P], pick[0:12, a, :], start=False, stop=True)
                last.then_inc(conv_done, 1)

            def token_pieces(lo_, hi_):
                for p in range(lo_, hi_):
                    ps = piece(p)
                    for i in range(4):
                        t, k = (i, p) if p < KT else (NL, 4 * (p - KT) + i)
                        last = nc.tensor.transpose(ps[:, i * P:(i + 1) * P], x_in[:, t, k * P:(k + 1) * P], ident[:, :])
                    last.then_inc(piece_done, 1)

            pe.wait_ge(rows_in, 96)
            nc.tensor.transpose(bank(7)[:, 0:40], rows40[:, :], ident[0:40, 0:40]).then_inc(rowsT_done, 1)
            pe.wait_ge(const_in, 48)
            pe.wait_ge(cond_ready, 1)
            ada(0, 0)
            pe.wait_ge(xn_ready, NT)
            pe.wait_ge(wsp_in, 16)
            for i in range(2):
                if i == 1:
                    pe.wait_ge(wspT_ready, 1)
                for g in range(4):
                    last = nc.tensor.transpose(bank(5)[:, g * P:(g + 1) * P], w_sp[:, 4 * i + g, :], ident[:, :])
                last.then_inc(wspT_done, 1)
            token_pieces(0, 3)
            ada(1, 1)
            conv(0)
            pe.wait_ge(wspT_ready, 2)
            token_pieces(3, 6)
            ada(2, 2)
            conv(1)
            ada(3, 3)
            conv(2)
            conv(3)
            token_pieces(6, 2 * NT)
            pe.wait_ge(h_ready, 2 * NT)
            for b in range(4, FIRST_WO):
                kind, j = BLOCKS[b]
                if kind == "ada":
                    ada(j, b)
                else:
                    pe.wait_ge(lo_done, 2 * b + 2)
                    for t in range(NT):
                        ps = piece(PIECE_AT[b, t])
                        for n in (2 * b, 2 * b + 1):
                            for k in range(CK):
                                kk = (n % 2) * CK + k
                                last = split3(ps, h_hi[:, kk, t * P:(t + 1) * P], h_lo[:, kk, t * P:(t + 1) * P],
                                              w_hi[:, n % NSPLIT, k, :], w_lo[:, n % NSPLIT, k, :], kk == 0, kk == KT - 1)
                        last.then_inc(piece_done, 1)
                        if t == 0 and BLOCKS[b - 1][0] == "ada" and b > 4:
                            conv(BLOCKS[b - 1][1])
                if b == SPATIAL_AFTER:
                    for i in range(2 * NT):
                        t, half = i // 2, i % 2
                        pe.wait_ge(zn_ready, t + 1)
                        ps = piece(PIECE_AT["sp", i])
                        for g in range(4):
                            gg = 4 * half + g
                            last = nc.tensor.matmul(ps[:, g * P:(g + 1) * P], wspT[:, gg, :], ob[:, t, gg * P:(gg + 1) * P], start=True, stop=True)
                        last.then_inc(piece_done, 1)

            pe.wait_ge(ev_act, emptied_before(len(PIECES), "act"))
            pe.wait_ge(ev_dve, emptied_before(len(PIECES), "dve"))
            pe.wait_ge(conv_ev, 12)
            done = [0]

            def transposes(want):
                while done[0] < want:
                    n = done[0]
                    what, which, first, k = TRANSPOSED[n]
                    if n >= 2:
                        pe.wait_ge(tr_ev, n - 1)
                    if what == "a":
                        pe.wait_ge(a_done, which + 1)
                    elif first == 0:
                        pe.wait_ge(qkv_in[which % 2], 80 * (which // 2 + 1))
                    for i in range(k):
                        m = first + i
                        if what == "a":
                            src = p_0[:, which % 2, m * P:(m + 1) * P]
                        else:
                            src = q_h[:, which % 2, m, :] if m < NT else k_h[:, which % 2, m - NT, :]
                        last = nc.tensor.transpose(bank(4 + n % 2)[:, i * P:(i + 1) * P], src, ident[:, :])
                    last.then_inc(tr_done, 1)
                    done[0] += 1

            def scores(u):
                h, t = u // NT, u % NT
                k0, nk = unit_keys(u)
                if t == 0:
                    pe.wait_ge(tr_ev, transposed_upto("qk", h))
                for s in range(2):
                    if u >= 1:
                        pe.wait_ge(exp_done[s], u)
                    q = qT[HD * s:HD * s + HD, h % 2, t * P:(t + 1) * P]
                    for b, w in ((0, min(nk, 4) * P), (1, (nk - 4) * P)):
                        if w > 0:
                            c = k0 * P + b * CW
                            last = nc.tensor.matmul(bank(2 * s + b)[:, 0:w], q, kT[HD * s:HD * s + HD, h % 2, c:c + w], start=True, stop=True)
                    last.then_inc(sc_done[s], 1)

            def weigh(u):
                h = u // NT
                k0, nk = unit_keys(u)
                pe.wait_ge(tr_ev, transposed_upto("a", u))
                if u >= 2:
                    pe.wait_ge(o_ev, u - 1)
                for k in range(nk):
                    last = nc.tensor.matmul(bank(6 + u % 2)[:, 0:P], aT[:, u % 2, k * P:(k + 1) * P], v_h[:, h % 2, k0 + k, :],
                                            start=(k == 0), stop=(k == nk - 1))
                last.then_inc(pv_done, 1)

            transposes(transposed_upto("qk", 0))
            for u in range(NU):
                scores(u)
                if u >= 1:
                    transposes(transposed_upto("a", u - 1))
                if u >= 2:
                    weigh(u - 2)
                if u % NT == 2 and u // NT + 1 < H:
                    transposes(transposed_upto("qk", u // NT + 1))
            transposes(len(TRANSPOSED))
            weigh(NU - 2)
            weigh(NU - 1)

            n2 = [0]

            def piece2():
                n = n2[0]
                if n >= RING:
                    pe.wait_ge(p2_ev, n - RING + 1)
                n2[0] += 1
                return bank(n % RING)

            pe.wait_ge(o_ev, NU)
            pe.wait_ge(tr_ev, len(TRANSPOSED))
            for p in range(2 * NT):
                t, half = p // 2, p % 2
                pe.wait_ge(sa_used, t + 1)
                ps = piece2()
                for i in range(4):
                    k = 4 * half + i
                    last = nc.tensor.transpose(ps[:, i * P:(i + 1) * P], o_t[:, t, k * P:(k + 1) * P], ident[:, :])
                last.then_inc(p2_done, 1)
            for half in range(2):
                b = FIRST_WO + half
                pe.wait_ge(lo_done, 2 * b + 2)
                for t in range(NT):
                    pe.wait_ge(p2_ev, 2 * t + 2)
                    ps = piece2()
                    for n in (2 * b, 2 * b + 1):
                        for k in range(CK):
                            kk = (n % 2) * CK + k
                            last = split3(ps, m_hi[:, kk, t * P:(t + 1) * P], m_lo[:, kk, t * P:(t + 1) * P],
                                          w_hi[:, n % NSPLIT, k, :], w_lo[:, n % NSPLIT, k, :], kk == 0, kk == KT - 1)
                    last.then_inc(p2_done, 1)
            for t in range(NT):
                pe.wait_ge(xn2_ready, t + 1)
                for half in range(2):
                    ps = piece2()
                    for i in range(4):
                        k = 4 * half + i
                        last = nc.tensor.transpose(ps[:, i * P:(i + 1) * P], xn[t % 2][:, k * P:(k + 1) * P], ident[:, :])
                    last.then_inc(p2_done, 1)
                pe.wait_ge(p2_ev, n2[0])
                ps = piece2()
                for k in range(KT):
                    last = nc.tensor.matmul(ps[:, 0:E], h2T[t % 2][:, k, :], w_r[:, k, :], start=(k == 0), stop=(k == KT - 1))
                last.then_inc(p2_done, 1)
            for t in range(NT):
                pe.wait_ge(aff_ready, t + 1)
                nc.tensor.transpose(piece2()[0:E, 0:P], lg[:, t, :], ident[:, :]).then_inc(p2_done, 1)
            pe.wait_ge(idx_ready, 1)
            for src in (idx_f, gate_v):
                nc.tensor.transpose(piece2()[0:CAP, 0:E], src[:, :], ident[0:E, 0:E]).then_inc(p2_done, 1)
            pe.wait_ge(sel_ready, 1)
            for k in range(KT):
                c = slice(k * P, (k + 1) * P)
                for part in range(3):
                    ps = piece2()
                    if part < 2:
                        for t in range(NL):
                            r = sel_l[:, t, 8 * part:8 * part + 8, :].rearrange("p e c -> p (e c)")
                            nc.tensor.matmul(ps, xn_hi[:, t, c], r, start=(t == 0), stop=False)
                            last = nc.tensor.matmul(ps, xn_lo[:, t, c], r, start=False, stop=(t == NL - 1))
                    else:
                        r = sel_c[:, :, :].rearrange("p e c -> p (e c)")
                        nc.tensor.matmul(ps[:, 0:E * CAP_C], xn_hi[:, NL, c], r, start=True, stop=False)
                        last = nc.tensor.matmul(ps[:, 0:E * CAP_C], xn_lo[:, NL, c], r, start=False, stop=True)
                    last.then_inc(p2_done, 1)
            pe.wait_ge(p2_ev, N_P2)

            def hid_transposes(e, fb):
                pe.wait_ge(hid_ready, e * 4 + (fb + 1))
                if not (isinstance(e, int) and e == 0 and fb == 0):
                    pe.wait_ge(ht_ready, e * 4 + fb)
                for k in range(4):
                    last = nc.tensor.transpose(bank(6)[:, k * CAP:(k + 1) * CAP], hid[:, fb % 2, k * P:(k + 1) * P], ident[0:CAP, 0:CAP])
                last.then_inc(ht_done, 1)

            def scatter(e, s):
                t, half = s // 2, s % 2
                pe.wait_ge(sc2_ev, e * (2 * NT) + (s + 1))
                if s == 0:
                    pe.wait_ge(ye_ready, e * 2 + 2)
                c = slice(half * CW, (half + 1) * CW)
                nc.tensor.matmul(bank(7), selT[:, t * P:(t + 1) * P], ye_hi[:, c], start=True, stop=False)
                nc.tensor.matmul(bank(7), selT[:, t * P:(t + 1) * P], ye_lo[:, c], start=False, stop=True).then_inc(sc2_done, 1)

            def expert(e, first, last_e):
                pe.wait_ge(xe_ready, e + 1)
                for i in range(EC):
                    s = i % NSPLIT
                    pe.wait_ge(lo_done, e * EC + (PRE + i + 1))
                    if i < 16:
                        fb, which, half = i // 4, i // 2 % 2, i % 2
                        ps = bank(fb % 2 * 2 + which)[0:CAP, :]
                        if half == 0 and (not first or fb >= 2):
                            pe.wait_ge(hid_ready, e * 4 + (fb - 1))
                        for k in range(CK):
                            kk = half * CK + k
                            c = slice(kk * CAP, (kk + 1) * CAP)
                            last = split3(ps, xe_hi[:, c], xe_lo[:, c], w_hi[:, s, k, :], w_lo[:, s, k, :], kk == 0, kk == KT - 1)
                    else:
                        half, q = (i - 16) // 4, (i - 16) % 4
                        ps = bank(4 + half)[0:CAP, :]
                        if q == 0 and not first:
                            pe.wait_ge(ye_ready, e * 2 + (half - 1))
                        pe.wait_ge(ht_ready, e * 4 + (q + 1))
                        for k in range(CK):
                            f = q * CK + k
                            last = split3(ps, hT_hi[:, f, :], hT_lo[:, f, :], w_hi[:, s, k, :], w_lo[:, s, k, :], f == 0, f == FE // P - 1)
                    last.then_inc(used, 1)
                    if HT_STEP.get(i) is not None:
                        hid_transposes(e, HT_STEP[i])
                    if 2 <= i < 12 and not first:
                        scatter(e - 1, i - 2)

            expert(0, True, False)
            with pe.Fori(1, E - 1) as e:
                expert(e, False, False)
            expert(E - 1, False, True)
            for s in range(2 * NT):
                scatter(E - 1, s)


_INS = ["x_prompt", "x_sample", "cache_k", "cache_v", "c", "c_ctx", "w_ada", "b_ada", "norm1_g", "norm2_g", "w_in",
        "q_norm_g", "k_norm_g", "lambda_q1", "lambda_k1", "lambda_q2", "lambda_k2", "subln_g", "gmlp_ln_g",
        "gmlp_ln_b", "w_spatial", "b_spatial", "w_out", "w_router", "w_gate_e", "w_up_e", "w_down_e"]
_OUTS = [(1, CTX, D), (1, LAT, D), (1, 1, CTX, H, 2, HD), (1, 1, CTX, H, VD)]


def kernel(**inputs):
    import numpy as _np
    import concourse.bacc as _bacc
    from concourse import mybir as _mybir
    from concourse.bass_utils import run_bass_kernel_spmd as _run

    nc = _bacc.Bacc("TRN2", target_bir_lowering=False, num_devices=1)
    arrays = {f"in_{name}": _np.ascontiguousarray(inputs[name]) for name in _INS}
    arrays.update({f"in_{name}": _np.ascontiguousarray(a) for name, a in constants().items()})
    aps = {name[3:]: nc.dram_tensor(name, a.shape, _mybir.dt.from_np(a.dtype), kind="ExternalInput").ap()
           for name, a in arrays.items()}
    outs = [nc.dram_tensor(f"out_{i}", shape, F32, kind="ExternalOutput").ap() for i, shape in enumerate(_OUTS)]
    trunk_program(nc, aps, *outs)
    r = _run(nc, [arrays], core_ids=[0])
    return tuple(r.results[0][f"out_{i}"] for i in range(len(_OUTS)))
```

```python
from contextlib import ExitStack

import numpy as np
import concourse.bass as bass
from concourse import mybir

F32 = mybir.dt.float32
F32R = mybir.dt.float32r
U32 = mybir.dt.uint32
ALU = mybir.AluOpType
ACT = mybir.ActivationFunctionType
AX = mybir.AxisListType

P = 128
D = 1024
KT = D // P
LAT = 512
CTX = 128
NL = LAT // P
NT = NL + CTX // P
TOK = LAT + CTX
PAST = 256
NPAST = PAST // P
H = 8
HD = 64
VD = 128
G = 8
E = 16
FE = 2048
CAP_L = 2 * LAT // E
CAP_C = 2 * CTX // E
CAP = CAP_L + CAP_C
GRID_W = 64
EPS = 1e-6
LAMBDA_INIT = 0.8 - 0.6
CW = 512
CK = 4
NRAW = 3
NRAWE = NRAW + 1
NP = 3
NSPLIT = 4

BLOCKS = ([("ada", a) for a in range(4)]
          + [("k", 0), ("k", 1), ("q", 0), ("q", 1), ("v", 0), ("ada", 4), ("v", 1), ("ada", 5),
             ("zv", 0), ("ada", 6), ("zv", 1), ("ada", 7), ("ga", 0), ("ada", 8), ("ga", 1), ("ada", 9),
             ("zu", 0), ("ada", 10), ("zu", 1), ("ada", 11), ("gb", 0), ("gb", 1), ("wo", 0), ("wo", 1)])
COLUMN = {"q": 0, "k": 2, "v": 4, "zu": 6, "zv": 8, "ga": 10, "gb": 12}
NB = len(BLOCKS)
FIRST_WO = NB - 2
PRE = 2 * NB
EC = 24
GATES = [4, 5, 10, 11]
VEC = {0: 0, 1: 0, 2: 1, 3: 1, 6: 2, 7: 2, 8: 3, 9: 3}
EXPERT_SLOT = [(PRE + j) % NRAW for j in range(NRAW)] + [NRAW]
RAW_BEFORE = [len(range(s, PRE, NRAW)) for s in range(NRAW)] + [0]
SPATIAL_AFTER = BLOCKS.index(("ada", 8))


def is_in(kind):
    return kind in COLUMN


def amid(b):
    return b > 4 and b < NB and BLOCKS[b][0] == "ada"


def split_pairs():
    pair = []
    for b in range(NB):
        pair.append(0 if b == 0 else pair[-1] if amid(b - 1) else 1 - pair[-1])
    return pair


PAIR = split_pairs()
assert PAIR[-1] == 1
AMID_TILE = 2


def split_slot(n):
    return 2 * PAIR[n // 2] + n % 2


def split_before(n):
    before = [m for m in range(n) if split_slot(m) == split_slot(n)]
    return before[-1] if before else None


def piece_plan():
    plan = [("xt", i, "dve") for i in range(2 * NT)]
    for b, (kind, j) in enumerate(BLOCKS[:FIRST_WO]):
        if is_in(kind):
            plan += [(b, t, "act") for t in range(NT)]
        if b == SPATIAL_AFTER:
            plan += [("sp", i, "dve") for i in range(2 * NT)]
    return plan


PIECES = piece_plan()
PIECE_AT = {(a, i): n for n, (a, i, _) in enumerate(PIECES)}
RING = 6


def emptied_before(n, who):
    return sum(1 for p in PIECES[:n] if p[2] == who)


STAGED = [(b, t) for b, (kind, _) in enumerate(BLOCKS) if kind in ("v", "ga", "zu", "gb") for t in range(NT)]
STAGE_AT = {s: n for n, s in enumerate(STAGED)}
NSTAGE = 3


def stores_of(n):
    b, t = STAGED[n]
    kind = BLOCKS[b][0]
    return (2 if kind == "v" and t == NL else 1) if kind in ("v", "ga") else 0


def stage_stored(n):
    return 16 * sum(stores_of(m) for m in range(n % NSTAGE, n + 1, NSTAGE))


def multiplied(n):
    return sum(1 for m in range(n + 1) if stores_of(m) == 0)


NU = H * NT


def unit_keys(u):
    return (0, NPAST + NL) if u % NT < NL else (NPAST + NL, 1)


def transposed_plan():
    def of_head(h):
        return [("qk", h, i, 4) for i in range(0, 12, 4)]

    def of_unit(u):
        n = unit_keys(u)[1]
        return [("a", u, i, min(4, n - i)) for i in range(0, n, 4)]

    plan = of_head(0)
    for u in range(NU):
        if u >= 2:
            plan += of_unit(u - 2)
        if u % NT == 3 and u // NT + 1 < H:
            plan += of_head(u // NT + 1)
    return plan + of_unit(NU - 2) + of_unit(NU - 1)


TRANSPOSED = transposed_plan()


def transposed_upto(what, which):
    return max(n for n, p in enumerate(TRANSPOSED) if p[:2] == (what, which)) + 1


SG_STEP = {4 * fb + 2: fb for fb in range(4)}
HID_STEP = {4 * fb + 4: fb for fb in range(4)}
HTO_STEP = {4 * fb + 5: fb for fb in range(4)}
YE_STEP = 20
XE_STEP = 21
SEL_STEP = 23
SC_STEPS = [0, 3, 5, 6, 9, 10, 13, 14, 17, 18]
AHEAD = NSPLIT - 1
END_BANKS = [7, 0, 1, 2, 3, 6]
STEPS = [("M", 0), ("M", 1), ("T", 0), ("T", 1), ("M", 2), ("M", 3), ("W", 0), ("T", 2), ("M", 4), ("W", 1), ("T", 3),
         ("X", 0), ("W", 2), ("L", 0), ("T", 4), ("X", 1), ("W", 3), ("L", 1), ("X", 2), ("W", 4), ("L", 2), ("X", 3),
         ("L", 3), ("X", 4), ("L", 4)]
P2 = [(what, t, i) for what, t in STEPS for i in range({"M": 0, "L": 1}.get(what, 2))]
N_P2 = len(P2) + NT + 2 + 3 * KT


def constants():
    half = HD // 4
    inv = np.float32(10000.0) ** (-np.arange(half, dtype=np.float32) / np.float32(half))
    row = np.repeat(np.arange(LAT // GRID_W, dtype=np.float32), GRID_W)[:, None] * inv
    col = np.tile(np.arange(GRID_W, dtype=np.float32), LAT // GRID_W)[:, None] * inv
    ang = np.concatenate([row, row, col, col], axis=-1).astype(np.float32)
    sign = np.repeat(np.array([-1, 1, -1, 1], np.float32), half)
    cos = np.ones((TOK, HD), np.float32)
    sin = np.zeros((TOK, HD), np.float32)
    cos[:LAT] = np.cos(ang)
    sin[:LAT] = np.sin(ang) * sign
    rope = np.stack([a.reshape(NT, P, HD).transpose(1, 0, 2) for a in (cos, sin)], axis=1)
    ident = np.eye(P, dtype=np.float32)
    token = (np.arange(P)[:, None] + P * np.arange(NT)[None]).astype(np.float32)
    tokens = np.tile(np.arange(TOK, dtype=np.float32)[None], (P, 1))
    hilo = np.zeros((P, 2), np.float32)
    hilo[:4] = np.tile(np.eye(2, dtype=np.float32), (2, 1))
    pick = np.zeros((P, 12, 2), np.float32)
    for a in range(12):
        pick[a, a] = 1.0
    return {"rope": rope.reshape(P, -1), "ident": ident, "token": token, "tokens": tokens,
            "hilo": hilo, "pick": pick.reshape(P, -1)}


def trunk_program(nc, A, O_y, O_ys, O_k, O_v):
    def scratch(name, shape):
        return nc.dram_tensor(name, shape, F32, kind="Internal").ap()

    q_d, k_d, v_d = (scratch(n, [TOK, D]) for n in ("q_scr", "k_scr", "v_scr"))
    sa_d, x2_d = (scratch(n, [TOK, D]) for n in ("sa_scr", "x2_scr"))
    gate_d = scratch("gate_scr", [2, 2, D])
    idx_d = scratch("idx_scr", [E, CAP])
    w_ada = A["w_ada"].rearrange("z k n -> (z k) n")
    w_in = A["w_in"].rearrange("z k n -> (z k) n")
    w_out = A["w_out"].rearrange("z k n -> (z k) n")
    w_gate = A["w_gate_e"].rearrange("z e (k p) n -> (z e) p k n", p=P)
    w_up = A["w_up_e"].rearrange("z e (k p) n -> (z e) p k n", p=P)
    w_down = A["w_down_e"].rearrange("z e (k p) n -> (z e) p k n", p=P)
    x_l = A["x_sample"].rearrange("b (t p) d -> p (b t) d", p=P)
    x_c = A["x_prompt"].rearrange("b p d -> p b d")
    ck = A["cache_k"].rearrange("b z (t p) h s d -> p (b z t) h (s d)", p=P)
    cv = A["cache_v"].rearrange("b z (t p) h d -> p (b z t) h d", p=P)
    out_k = O_k.rearrange("b z p h s d -> p (b z h s d)")
    out_v = O_v.rearrange("b z p h d -> p (b z h d)")
    y_l = O_ys.rearrange("b (t p) d -> p (b t) d", p=P)
    y_c = O_y.rearrange("b p d -> p b d")

    def tiles(d):
        return d.rearrange("(t p) n -> p t n", p=P)

    def chunk_source(n):
        kind, j = BLOCKS[n // 2]
        w = {"ada": w_ada, "wo": w_out}.get(kind, w_in)
        c = (COLUMN.get(kind, 0) + j) * CW
        r = (n % 2) * CK * P
        return w[r:r + CK * P, c:c + CW].rearrange("(k p) n -> p k n", p=P)

    def expert_source(e, i):
        if i < 16:
            w, fb, half = (w_gate, w_up)[i // 2 % 2], i // 4, i % 2
            return w[e, :, half * CK:half * CK + CK, fb * CW:fb * CW + CW] if isinstance(e, int) else \
                w[bass.ds(e, 1), :, half * CK:half * CK + CK, fb * CW:fb * CW + CW].rearrange("e p k n -> p (e k) n")
        half, q = (i - 16) // 4, (i - 16) % 4
        return w_down[e, :, q * CK:q * CK + CK, half * CW:half * CW + CW] if isinstance(e, int) else \
            w_down[bass.ds(e, 1), :, q * CK:q * CK + CK, half * CW:half * CW + CW].rearrange("e p k n -> p (e k) n")

    base = (nc.sbuf_base + 31) // 32 * 32
    end = nc.sbuf_usable_end // 32 * 32
    at = [base]

    def place(name, shape, dt=F32, offset=None):
        size = 4 * int(np.prod(shape[1:]))
        o = at[0] if offset is None else offset
        assert o + size <= end, (name, o + size - end)
        if offset is None:
            at[0] += (size + 31) // 32 * 32
        return nc.alloc_sbuf_tensor_at(name, list(shape), dt, offset=o)

    raw = place("raw", [P, NRAW, CK, CW])
    w_hi = place("w_hi", [P, NSPLIT, CK, CW], F32R)
    w_lo = place("w_lo", [P, NSPLIT, CK, CW], F32R)
    MID = at[0]
    h_hi = place("h_hi", [P, KT, TOK], F32R)
    h_lo = place("h_lo", [P, KT, TOK], F32R)
    LOW = at[0]
    ident = place("ident_sb", [P, P])
    token = place("token_sb", [P, NT])
    cols = place("cols", [P, 40])
    mcol = place("mcol", [P, 4, KT, 2])
    amp1 = place("amp1", [P, KT, 2])
    amp2 = place("amp2", [P, KT, 2])
    var = place("var", [P, 40])
    root = place("root", [P, 40])
    rstd = place("rstd", [P, 40])
    newton = place("newton", [P, 40])
    lam = place("lam", [P, 8])
    w_r = place("w_r", [P, KT, E])
    g_sub = place("g_sub", [P, VD])
    gate_v = place("gate_v", [E, CAP])
    idx_u = place("idx_u", [E, CAP], U32)
    idx_f = place("idx_f", [E, CAP])
    KEEP = at[0]
    tab = place("tab", [P, 2, 2, NT, HD])
    gain = place("gain", [P, 2, HD])
    hilo = place("hilo_sb", [P, 2])
    pick = place("pick_sb", [P, 12, 2])
    b12 = place("b12", [12, CW])
    m4 = place("m4", [4, 2, CW])
    grow = place("grow", [2, 2, CW])
    silu_c = place("silu_c", [P, 2, KT])
    cond = place("cond", [P, KT, 4], F32R)
    bstat = place("bstat", [P, NT, 2, 6])
    mv = place("mv", [P, NT, 2])
    wspT = place("wspT", [P, G, P])
    stage = place("stage", [P, NSTAGE, CW])
    WORK = at[0]
    qk_raw = [place(f"qk_raw{i}", [P, NT, CW]) for i in range(2)]
    qk_swp = [place(f"qk_swp{i}", [P, NT, CW]) for i in range(2)]
    qk_sq = place("qk_sq", [P, NT, CW])
    lamv = place("lamv", [P, 4, HD], offset=WORK + 4 * 4 * NT * CW)
    x_in = place("x_in", [P, NT, D], offset=WORK)
    x_junk = place("x_junk", [P, D], offset=WORK + 4 * NT * D)
    rows40 = place("rows40", [40, P], offset=WORK + 4 * NT * D + 4096)
    w_sp = place("w_sp", [P, G, P], offset=WORK + 4 * NT * D + 8192)
    ob = place("ob", [P, NT, D], offset=WORK)
    ln_g = place("ln_g", [P, D], offset=WORK + 4 * NT * D)
    ln_b = place("ln_b", [P, D], offset=WORK + 4 * NT * D + 4096)
    p_0 = place("p_0", [P, NP, PAST + LAT], offset=MID)
    at[0] = MID + 4 * NP * (PAST + LAT)
    p_1 = place("p_1", [P, NP, PAST + LAT])
    aT = place("aT", [P, 2, PAST + LAT])
    qT = place("qT", [P, 2, TOK])
    kT = place("kT", [P, 2, PAST + TOK])
    assert at[0] <= LOW

    def head_slot(i):
        return [place(f"{n}{i}", [P, w, P]) for n, w in (("q_h", NT), ("k_h", NPAST + NT), ("v_h", NPAST + NT))]

    at[0] = KEEP
    slot1 = head_slot(1)
    sa_h = place("sa_h", [P, 2, NT, P])
    gate1 = place("gate1", [P, 2, D])
    nbias = place("nbias", [P, 2, 2])
    rsum = place("rsum", [P, NP, 2])
    rinv = place("rinv", [P, 2, 2])
    sq_junk = place("sq_junk", [P, 2, P])
    lg = place("lg", [P, NT, E])
    rst = place("rst", [P, NT, 4])
    assert at[0] <= WORK
    at[0] = WORK + 4 * NT * D
    o_t = place("o_t", [P, NT, D])
    q_h, k_h, v_h = zip(head_slot(0), slot1)
    m_hi = place("m_hi", [P, NT, KT, P], F32R, offset=MID)
    m_lo = place("m_lo", [P, NT, KT, P], F32R, offset=MID + 4 * KT * TOK)
    x2 = place("x2", [P, NT, D], offset=WORK)
    xw = place("xw", [P, 2 * CW], offset=WORK + 4 * NT * D)
    p_sq = place("p_sq", [P, D], offset=WORK + 4 * NT * D + 4 * D)
    xn = [place(f"xn{i}", [P, D], offset=WORK + 8 * NT * D + 4 * D * i) for i in range(2)]
    h2T = [place(f"h2T{i}", [P, KT, P], offset=KEEP + 4 * D * i) for i in range(2)]
    affT = place("affT", [E, TOK], offset=KEEP + 4 * (3 * NT + 2 * NPAST) * P)
    affW = place("affW", [E, TOK], offset=KEEP + 4 * (4 * NT + 2 * NPAST) * P)
    xn_hi = place("xn_hi", [P, NT, D], F32R, offset=MID)
    xn_lo = place("xn_lo", [P, NT, D], F32R, offset=MID + 4 * NT * D)
    at[0] = KEEP
    idx_c = place("idx_c", [CAP, E])
    gate_c = place("gate_c", [CAP, E])
    tokens = place("tokens_sb", [P, TOK])
    selT = place("selT", [CAP, TOK], F32R)
    XE = at[0]
    sel_l = place("sel_l", [P, NL, E, CAP_L], F32R, offset=end - 4 * (NL * E * CAP_L + E * CAP_C) - 32)
    sel_c = place("sel_c", [P, E, CAP_C], F32R, offset=end - 4 * E * CAP_C - 32)
    idx_b = place("idx_b", [P, E, CAP], offset=XE)
    xeT = place("xeT", [P, E, KT * CAP], offset=XE + 4 * E * CAP)
    assert XE + 4 * E * CAP + 4 * E * KT * CAP <= end - 4 * (NL * E * CAP_L + E * CAP_C) - 32
    at[0] = XE + 4 * E * CAP + 4 * E * KT * CAP
    yacc = place("yacc", [P, NT, D])
    yeg = place("yeg", [CAP, D])
    ye_hi = place("ye_hi", [CAP, D], F32R, offset=XE)
    at[0] = MID
    hT_hi = place("hT_hi", [P, FE // P, CAP], F32R)
    hT_lo = place("hT_lo", [P, FE // P, CAP], F32R)
    xe_hi = place("xe_hi", [P, KT * CAP], F32R)
    xe_lo = place("xe_lo", [P, KT * CAP], F32R)
    sg = place("sg", [CAP, 2, CW])
    hid = place("hid", [CAP, 2, CW])
    ye_lo = place("ye_lo", [CAP, D], F32R)
    at[0] = (at[0] + 31) // 32 * 32
    raw_x = place("raw_x", [P, CK, CW])
    gate2 = place("gate2", [CAP, D])
    assert at[0] <= LOW

    def raw_slot(i):
        return raw[:, i] if i < NRAW else raw_x[:, :, :]

    ctx = ExitStack()
    bank_all = nc.alloc_psum_tensor("banks", [P, 8, CW], F32)

    def bank(i):
        return bank_all[:, i, :]

    with ctx:
        def sem(name):
            return ctx.enter_context(nc.semaphore(name))

        raw_in = [sem(f"raw_in{i}") for i in range(NRAWE)]
        hi_done, lo_done, used = sem("hi_done"), sem("lo_done"), sem("used")
        rows_in, const_in, x_load, lam_in = sem("rows_in"), sem("const_in"), sem("x_load"), sem("lam_in")
        wsp_in, ln_in = sem("wsp_in"), sem("ln_in")
        rowsT_done, cols_ready, silu_ready, cond_ready = (sem(n) for n in ("rowsT_done", "cols_ready", "silu_ready", "cond_ready"))
        var_ready, root_done = sem("var_ready"), sem("root_done")
        ssum_ready, xn_ready = sem("ssum_ready"), sem("xn_ready")
        ada_done, m4_ready, conv_done, conv_ev = (sem(n) for n in ("ada_done", "m4_ready", "conv_done", "conv_ev"))
        grow_out = [sem(f"grow_out{i}") for i in range(2)]
        piece_done, ev_act, ev_dve = sem("piece_done"), sem("ev_act"), sem("ev_dve")
        hf_ready, h_hi_ready, h_ready = sem("hf_ready"), sem("h_hi_ready"), sem("h_ready")
        tab_ready, wspT_done, wspT_ready = sem("tab_ready"), sem("wspT_done"), sem("wspT_ready")
        sq_free, rstd_ready, swp_ready, qk_ready = (sem(n) for n in ("sq_free", "rstd_ready", "swp_ready", "qk_ready"))
        qk_out = [sem(f"qk_out{i}") for i in range(2)]
        stage_out = [sem(f"stage_out{i}") for i in range(NSTAGE)]
        stage_full, stage_mul = sem("stage_full"), sem("stage_mul")
        zn_pre, zn_ready = sem("zn_pre"), sem("zn_ready")
        dv, po = sem("dv"), sem("po")
        lam_e, lam_x = sem("lam_e"), sem("lam_x")
        qkv_in = [sem(f"qkv_in{i}") for i in range(2)]
        tr_done, tr_ev = sem("tr_done"), sem("tr_ev")
        sc_done = [sem(f"sc_done{i}") for i in range(2)]
        nb_done, exp_done = [sem(f"nb_done{i}") for i in range(2)], [sem(f"exp_done{i}") for i in range(2)]
        a_done, pv_done, o_ev = sem("a_done"), sem("pv_done"), sem("o_ev")
        osq_ready, merged, sag_ready, gate1_in = (sem(n) for n in ("osq_ready", "merged", "sag_ready", "gate1_in"))
        sa_in, x2_in = [sem(f"sa_in{i}") for i in range(2)], [sem(f"x2_in{t}") for t in range(NT)]
        p2_done, p2_ev, mhi_ready = sem("p2_done"), sem("p2_ev"), sem("mhi_ready")
        x2_ready, x2_sq, xn2_ready, xnhi_ready, x2_out = (sem(n) for n in ("x2_ready", "x2_sq", "xn2_ready", "xnhi_ready", "x2_out"))
        wr_in, lgb_ready, lge_ready, aff_ready = (sem(n) for n in ("wr_in", "lgb_ready", "lge_ready", "aff_ready"))
        idx_ready, idx_out, idxb_in, tok_in, sel_ready = (sem(n) for n in ("idx_ready", "idx_out", "idxb_in", "tok_in", "sel_ready"))
        xeh_done, xe_ready, gu_done, sg_ready, hid_ready = (sem(n) for n in ("xeh_done", "xe_ready", "gu_done", "sg_ready", "hid_ready"))
        ht_done, hth_ready, ht_ready, dn_done, yeh_ready, ye_ready = (sem(n) for n in ("ht_done", "hth_ready", "ht_ready", "dn_done", "yeh_ready", "ye_ready"))
        sc2_done, sc2_ev, yacc_in, gate2_in, yeg_ready, y_out = (sem(n) for n in ("sc2_done", "sc2_ev", "yacc_in", "gate2_in", "yeg_ready", "y_out"))
        sel_done = sem("sel_done")

        block = ctx.enter_context(nc.Block())

        def raw_count(n):
            return 16 * (n // NRAW + 1)

        def wait_read(eng, n):
            b = n // 2
            kind, j = BLOCKS[b]
            if kind == "ada":
                eng.wait_ge(ada_done, j + 1)
            elif kind == "wo":
                eng.wait_ge(p2_done, P2.index(("W", NT - 1, j)) + 1)
            else:
                eng.wait_ge(piece_done, PIECE_AT[b, NT - 1] + 1)

        @block.sync
        def _(sp):
            def load(n):
                if n >= NRAW:
                    sp.wait_ge(lo_done, n - NRAW + 1)
                src = chunk_source(n) if n < PRE else expert_source(0, n - PRE)
                sp.dma_start(raw[:, n % NRAW], src).then_inc(raw_in[n % NRAW], 16)

            for i, name in enumerate(["c", "c_ctx", "norm1_g", "norm2_g"]):
                v = A[name]
                flat = v.rearrange("(k p) -> k p", p=P) if len(v.shape) == 1 else v.rearrange("z (k p) -> (z k) p", p=P)
                sp.dma_start(rows40[8 * i:8 * i + 8, :], flat).then_inc(rows_in, 16)
            sp.dma_start(rows40[32:40, :], A["b_spatial"].rearrange("z g p -> (z g) p")).then_inc(rows_in, 16)
            sp.dma_start(ident[:, :], A["ident"]).then_inc(rows_in, 16)
            load(0)
            load(1)
            sp.dma_start(x_in[:, 0:NL, :], x_l).then_inc(x_load, 16)
            sp.dma_start(x_in[:, NL:NT, :], x_c).then_inc(x_load, 16)
            sp.dma_start(hilo[:, :], A["hilo"]).then_inc(const_in, 16)
            sp.dma_start(pick[:, :, :].rearrange("p a b -> p (a b)"), A["pick"]).then_inc(const_in, 16)
            sp.dma_start(b12[:, :], A["b_ada"].rearrange("z (a n) -> (z a) n", n=CW)).then_inc(const_in, 16)
            load(2)
            for i, name in enumerate(["q_norm_g", "k_norm_g"]):
                sp.dma_start(tab[:, i, :, :, :].rearrange("p a t d -> p (a t d)"), A["rope"]).then_inc(lam_in, 16)
                sp.dma_start(gain[:, i, :], A[name].broadcast_to([P, HD])).then_inc(lam_in, 16)
            for i, name in enumerate(["lambda_q1", "lambda_k1", "lambda_q2", "lambda_k2"]):
                sp.dma_start(lamv[:, i, :], A[name].broadcast_to([P, HD])).then_inc(lam_in, 16)
            sp.dma_start(g_sub[:, :], A["subln_g"].broadcast_to([P, VD])).then_inc(lam_in, 16)
            sp.dma_start(w_sp[:, :, :], A["w_spatial"].rearrange("z g p q -> p (z g) q")).then_inc(wsp_in, 16)
            sp.dma_start(w_r[:, :, :], A["w_router"].rearrange("z (k p) e -> p (z k) e", p=P)).then_inc(wr_in, 16)
            sp.dma_start(token[:, :], A["token"]).then_inc(wr_in, 16)

            def load_head(h):
                p = h % 2
                if h >= 2:
                    sp.wait_ge(pv_done, NT * (h - 1))
                c = slice(h * P, h * P + P)
                sp.dma_start(q_h[p][:, :, :], tiles(q_d)[:, :, c]).then_inc(qkv_in[p], 16)
                sp.dma_start(k_h[p][:, 0:NPAST], ck[:, :, h, :]).then_inc(qkv_in[p], 16)
                sp.dma_start(k_h[p][:, NPAST:], tiles(k_d)[:, :, c]).then_inc(qkv_in[p], 16)
                sp.dma_start(v_h[p][:, 0:NPAST], cv[:, :, h, :]).then_inc(qkv_in[p], 16)
                sp.dma_start(v_h[p][:, NPAST:], tiles(v_d)[:, :, c]).then_inc(qkv_in[p], 16)

            def load_gates(h):
                if h >= 2:
                    sp.wait_ge(o_ev, NT * (h - 1))
                sp.dma_start(sa_h[:, h % 2], tiles(sa_d)[:, :, h * P:h * P + P]).then_inc(sa_in[h % 2], 16)

            for n in range(NRAW, PRE + NRAW):
                load(n)
                if n == 2 * BLOCKS.index(("gb", 0)):
                    sp.wait_ge(qk_out[0], 48)
                    sp.wait_ge(qk_out[1], 48)
                    for s in range(NSTAGE):
                        last = max(n for n in range(len(STAGED)) if n % NSTAGE == s and BLOCKS[STAGED[n][0]][0] == "v")
                        sp.wait_ge(stage_out[s], stage_stored(last))
                    sp.wait_ge(sq_free, 4)
                    load_head(0)

            for s in range(NSTAGE):
                last = max(n for n in range(len(STAGED)) if n % NSTAGE == s and stores_of(n))
                sp.wait_ge(stage_out[s], stage_stored(last))
            sp.wait_ge(grow_out[0], 32)
            sp.wait_ge(grow_out[1], 32)
            sp.wait_ge(conv_ev, 12)
            sp.wait_ge(piece_done, len(PIECES))
            sp.wait_ge(stage_mul, multiplied(len(STAGED) - 1))
            load_gates(0)
            load_head(1)
            load_gates(1)
            for i in range(2):
                sp.dma_start(gate1[:, i, :], gate_d[i, 0:1, :].broadcast_to([P, D])).then_inc(gate1_in, 16)
            for h in range(2, H):
                load_head(h)
                load_gates(h)
            for t in range(NT):
                sp.wait_ge(merged, t + 1)
                sp.dma_start(x2[:, t, :], x_l[:, t, :] if t < NL else x_c[:, 0, :]).then_inc(x2_in[t], 16)
            for t in range(NT):
                sp.wait_ge(x2_ready, t + 1)
                sp.dma_start(x2_d[t * P:(t + 1) * P, :], x2[:, t, :]).then_inc(x2_out, 16)
            sp.wait_ge(idx_ready, 1)
            sp.dma_start(idx_d, idx_f[:, :]).then_inc(idx_out, 16)
            sp.wait_ge(idx_out, 16)
            sp.dma_start(idx_b[:, :, :].rearrange("p e c -> p (e c)"),
                         idx_d.rearrange("e c -> (e c)").unsqueeze(0).broadcast_to([P, E * CAP])).then_inc(idxb_in, 16)
            sp.dma_start(tokens[:, :], A["tokens"]).then_inc(tok_in, 16)

            def expert_loads(e, last):
                for i in range(EC):
                    j = i + NRAWE
                    if j >= EC and last:
                        continue
                    slot = EXPERT_SLOT[j % NRAWE]
                    src = expert_source(e, j) if j < EC else expert_source(e + 1, j - EC)
                    if not last:
                        sp.lower_val(src.offset * 4)
                    sp.wait_ge(lo_done, e * EC + (PRE + i + 1))
                    sp.dma_start(raw_slot(slot), src).then_inc(raw_in[slot], 16)

            sp.wait_ge(p2_done, N_P2)
            sp.dma_start(raw_x[:, :, :], expert_source(0, NRAW)).then_inc(raw_in[NRAW], 16)
            sp.wait_ge(x2_out, 16 * NT)
            sp.dma_start(yacc[:, :, :], tiles(x2_d)).then_inc(yacc_in, 16)
            sp.dma_start(gate2[0:CAP_L, :], gate_d[0, 1:2, :].broadcast_to([CAP_L, D])).then_inc(gate2_in, 16)
            sp.dma_start(gate2[CAP_L:CAP, :], gate_d[1, 1:2, :].broadcast_to([CAP_C, D])).then_inc(gate2_in, 16)
            with sp.Fori(0, E - 1) as e:
                expert_loads(e, False)
            expert_loads(E - 1, True)

            for t in range(NT):
                sp.wait_ge(sc2_ev, (E - 1) * 2 * NT + 2 * (t + 1))
                out = y_l[:, t, :] if t < NL else y_c[:, 0, :]
                sp.dma_start(out, yacc[:, t, :]).then_inc(y_out, 16)
            sp.wait_ge(y_out, 16 * NT)

        @block.scalar
        def _(act):
            def hi(n):
                act.wait_ge(raw_in[n % NRAW], raw_count(n))
                slot = split_slot(n) if n < PRE else (n - PRE) % NSPLIT
                before = split_before(n) if n < PRE else PRE - NSPLIT + n - PRE
                if before is not None:
                    wait_read(act, before)
                nc.scalar.activation(w_hi[:, slot], raw[:, n % NRAW], ACT.Copy).then_inc(hi_done, 1)

            def ahead(b):
                hi(2 * b + 2)
                hi(2 * b + 3)

            def take_root(n, width, c=0):
                act.wait_ge(var_ready, n + 1)
                nc.scalar.activation(root[:, c:c + width], var[:, c:c + width], ACT.Sqrt).then_inc(root_done, 1)

            act.wait_ge(cols_ready, 1)
            nc.scalar.activation(silu_c[:, :, :].rearrange("p a k -> p (a k)"), cols[:, 0:16], ACT.Silu).then_inc(silu_ready, 1)
            hi(0)
            hi(1)
            act.wait_ge(x_load, 32)
            for t in range(NT):
                if t >= 1:
                    act.wait_ge(ssum_ready, t)
                nc.scalar.activation(x_junk[:, :], x_in[:, t, :], ACT.Square, accum_out=newton[:, t:t + 1]).then_inc(ssum_ready, 1)
            take_root(0, NT)
            act.wait_ge(lam_e, 1)
            nc.scalar.activation(lam[:, 2:4], lam[:, 0:2], ACT.Exp).then_inc(lam_x, 1)

            roots = [1]
            qk_pending = []
            for b in range(FIRST_WO):
                kind, j = BLOCKS[b]
                if not amid(b):
                    ahead(b)
                if qk_pending:
                    take_root(roots[0], 8 * NT)
                    roots[0] += 1
                    qk_pending.clear()
                if kind == "ga" and j == 0:
                    take_root(roots[0], NT)
                    roots[0] += 1
                if kind == "ada":
                    act.wait_ge(ada_done, j + 1)
                    if j >= 2:
                        act.wait_ge(conv_done, j - 1)
                    nc.scalar.activation(m4[:, j % 2, :], bank(6)[0:4, :], ACT.Copy).then_inc(m4_ready, 1)
                    if j == 3:
                        for p in range(2 * NT):
                            act.wait_ge(ev_dve, p + 1)
                            src = stage[:, p % NSTAGE, :]
                            if p < KT:
                                out = h_hi[:, p, 0:LAT]
                            else:
                                k0 = 4 * (p - KT)
                                out = h_hi[:, k0:k0 + 4, LAT:TOK]
                                src = src.rearrange("p (k t) -> p k t", k=4)
                            nc.scalar.activation(out, src, ACT.Copy).then_inc(h_hi_ready, 1)
                    continue
                for t in range(NT):
                    n = PIECE_AT[b, t]
                    act.wait_ge(piece_done, n + 1)
                    ps = bank(n % RING)
                    if kind in ("q", "k"):
                        i = {"k": 0, "q": 2}[kind] + j
                        if t == 0 and i >= 2:
                            act.wait_ge(qk_out[i % 2], 32)
                        if t == 0 and i >= 1:
                            act.wait_ge(sq_free, i)
                        swapped = qk_swp[i % 2][:, t, :].rearrange("p (a s c) -> p a s c", s=2, c=HD // 4)[:, :, ::-1, :]
                        nc.scalar.activation(qk_raw[i % 2][:, t, :], ps, ACT.Copy)
                        nc.scalar.activation(swapped, ps.rearrange("p (a s c) -> p a s c", s=2, c=HD // 4), ACT.Copy)
                        nc.scalar.activation(qk_sq[:, t, :], ps, ACT.Square).then_inc(ev_act, 1)
                        qk_pending.append(1)
                    elif kind == "zv":
                        if t == 0 and j == 0:
                            act.wait_ge(qk_out[0], 48)
                            act.wait_ge(qk_out[1], 48)
                        nc.scalar.activation(ob[:, t, j * CW:(j + 1) * CW], ps, ACT.Gelu_apprx_tanh).then_inc(ev_act, 1)
                    else:
                        s = STAGE_AT[b, t]
                        if s >= NSTAGE:
                            m = s - NSTAGE
                            if stores_of(m):
                                act.wait_ge(stage_out[m % NSTAGE], stage_stored(m))
                            else:
                                act.wait_ge(stage_mul, multiplied(m))
                        func = {"v": ACT.Copy, "ga": ACT.Sigmoid, "gb": ACT.Sigmoid, "zu": ACT.Gelu_apprx_tanh}[kind]
                        nc.scalar.activation(stage[:, s % NSTAGE, :], ps, func).then_inc(ev_act, 1)
                    if t == AMID_TILE and amid(b + 1):
                        ahead(b + 1)
            ahead(FIRST_WO)

            seen = [0]

            def copy_out(want):
                while seen[0] < want:
                    n = seen[0]
                    what, which, first, k = TRANSPOSED[n]
                    act.wait_ge(tr_done, n + 1)
                    ps = bank(4 + n % 2)
                    if what == "a":
                        if which >= 2 and first == 0:
                            act.wait_ge(pv_done, which - 1)
                        out = aT[:, which % 2, first * P:(first + k) * P]
                        nc.scalar.activation(out, ps[:, 0:k * P], ACT.Copy).then_inc(tr_ev, 1)
                    elif first < 4:
                        nc.scalar.activation(qT[:, which % 2, 0:4 * P], ps[:, 0:4 * P], ACT.Copy).then_inc(tr_ev, 1)
                    elif first < 8:
                        nc.scalar.activation(qT[:, which % 2, 4 * P:5 * P], ps[:, 0:P], ACT.Copy)
                        nc.scalar.activation(kT[:, which % 2, 0:3 * P], ps[:, P:4 * P], ACT.Copy).then_inc(tr_ev, 1)
                    else:
                        nc.scalar.activation(kT[:, which % 2, 3 * P:7 * P], ps[:, 0:4 * P], ACT.Copy).then_inc(tr_ev, 1)
                    seen[0] += 1

            def square_out(u):
                act.wait_ge(o_ev, u + 1)
                if u == 0:
                    act.wait_ge(root_done, roots[0])
                h, t = u // NT, u % NT
                nc.scalar.activation(sq_junk[:, u % 2, :], bank(6 + u % 2)[:, 0:P], ACT.Square,
                                     accum_out=var[:, t * H + h:t * H + h + 1]).then_inc(osq_ready, 1)

            copy_out(transposed_upto("qk", 0))
            for u in range(NU):
                nk = unit_keys(u)[1] * P
                for s in range(2):
                    act.wait_ge(nb_done[s], u + 1)
                    if u >= NP and s == 0:
                        act.wait_ge(tr_done, transposed_upto("a", u - NP))
                    out = (p_0, p_1)[s][:, u % NP, 0:nk]
                    nc.scalar.activation(out, bank_all[:, 2 * s:2 * s + 2, :].rearrange("p a n -> p (a n)")[:, 0:nk], ACT.Exp,
                                         bias=nbias[:, u % 2, s:s + 1], scale=HD ** -0.5,
                                         accum_out=rsum[:, u % NP, s:s + 1]).then_inc(exp_done[s], 1)
                if u >= 2:
                    copy_out(transposed_upto("a", u - 2))
                if u >= 4:
                    square_out(u - 4)
                if u % NT == 3 and u // NT + 1 < H:
                    copy_out(transposed_upto("qk", u // NT + 1))
            copy_out(len(TRANSPOSED))
            for u in range(NU - 4, NU):
                square_out(u)

            take_root(roots[0], H * NT)
            roots[0] += 1
            for what, t in STEPS:
                if what == "T":
                    for half in range(2):
                        n = P2.index(("T", t, half))
                        act.wait_ge(p2_done, n + 1)
                        nc.scalar.activation(m_hi[:, t, 4 * half:4 * half + 4, :], bank(n % RING).rearrange("p (k t) -> p k t", k=4),
                                             ACT.Copy).then_inc(mhi_ready, 1)
                if what == "W":
                    act.wait_ge(x2_ready, t + 1)
                    if t == 0:
                        act.wait_ge(p2_done, P2.index(("T", 1, 1)) + 1)
                    nc.scalar.activation(p_sq[:, :], x2[:, t, :], ACT.Square, accum_out=newton[:, 8 + t:9 + t]).then_inc(x2_sq, 1)
                    take_root(roots[0], 1, t)
                    roots[0] += 1
                    act.wait_ge(xn2_ready, t + 1)
                    nc.scalar.activation(xn_hi[:, t, :], xn[t % 2][:, :], ACT.Copy).then_inc(xnhi_ready, 1)
            for t in range(NT):
                act.wait_ge(lgb_ready, t + 1)
                nc.scalar.activation(lg[:, t, :], lg[:, t, :], ACT.Exp, bias=rst[:, t, 0:1], scale=1.0,
                                     accum_out=rst[:, t, 1:2]).then_inc(lge_ready, 1)
            for i in range(NRAW):
                hi(PRE + i)

            act.wait_ge(p2_ev, N_P2)

            def output_hi(e, half):
                act.wait_ge(yeg_ready, e * 2 + (half + 1))
                c = slice(half * CW, (half + 1) * CW)
                nc.scalar.activation(ye_hi[:, c], yeg[:, c], ACT.Copy).then_inc(yeh_ready, 1)

            def expert(e, first, last):
                for i in range(EC):
                    j = i + AHEAD
                    if i == 1 and not first:
                        output_hi(e - 1, 1)
                    fb = SG_STEP.get(i)
                    if fb is not None:
                        act.wait_ge(used, e * EC + i)
                        if not first or fb >= 2:
                            act.wait_ge(hid_ready, e * 4 + (fb - 1))
                        nc.scalar.activation(sg[:, fb % 2, :], bank(fb % 2 * 2)[0:CAP, :], ACT.Silu).then_inc(sg_ready, 1)
                    fb = HTO_STEP.get(i)
                    if fb is not None:
                        act.wait_ge(ht_done, e * 4 + (fb + 1))
                        nc.scalar.activation(hT_hi[:, 4 * fb:4 * fb + 4, :], bank(6)[:, 0:4 * CAP].rearrange("p (k c) -> p k c", k=4),
                                             ACT.Copy).then_inc(hth_ready, 1)
                    if i == YE_STEP + 1:
                        output_hi(e, 0)
                    if not (last and j >= EC):
                        slot = EXPERT_SLOT[j % NRAWE]
                        act.wait_ge(raw_in[slot], e * (16 * EC // NRAWE) + 16 * (RAW_BEFORE[slot] + j // NRAWE + 1))
                        if first and j < NSPLIT:
                            wait_read(act, PRE + j - NSPLIT)
                        else:
                            act.wait_ge(used, e * EC + (j - NSPLIT + 1))
                        nc.scalar.activation(w_hi[:, j % NSPLIT], raw_slot(slot), ACT.Copy).then_inc(hi_done, 1)

            expert(0, True, False)
            with act.Fori(1, E - 1) as e:
                expert(e, False, False)
            expert(E - 1, False, True)
            output_hi(E - 1, 1)

        @block.vector
        def _(dve):
            chain = [0]

            def link(ins):
                chain[0] += 1
                ins.then_inc(dv, 1)
                dve.wait_ge(dv, chain[0])

            def lo(n):
                dve.wait_ge(hi_done, n + 1)
                slot = split_slot(n) if n < PRE else (n - PRE) % NSPLIT
                nc.vector.tensor_tensor(w_lo[:, slot], raw[:, n % NRAW], w_hi[:, slot], ALU.subtract).then_inc(lo_done, 1)

            def ahead(b):
                lo(2 * b + 2)
                lo(2 * b + 3)

            rooted = [0]

            def ask_root(ins):
                ins.then_inc(var_ready, 1)

            def finish_root(width, signal=None, c=0):
                rooted[0] += 1
                dve.wait_ge(root_done, rooted[0])
                r, t, v = rstd[:, c:c + width], newton[:, c:c + width], var[:, c:c + width]
                link(nc.vector.reciprocal(r, root[:, c:c + width]))
                link(nc.vector.tensor_tensor(t, r, r, ALU.mult))
                link(nc.vector.tensor_tensor(t, t, v, ALU.mult))
                link(nc.vector.tensor_scalar(t, t, -0.5, 1.5, ALU.mult, ALU.add))
                last = nc.vector.tensor_tensor(r, r, t, ALU.mult)
                if signal is None:
                    link(last)
                else:
                    last.then_inc(signal[0], 1)
                    dve.wait_ge(*signal)

            dve.wait_ge(rowsT_done, 1)
            nc.vector.tensor_copy(cols[:, :], bank(7)[:, 0:40]).then_inc(cols_ready, 1)
            dve.wait_ge(silu_ready, 1)
            sc = silu_c[:, :, :].rearrange("p a k -> p k a")
            link(nc.vector.tensor_copy(cond[:, :, 0:2], sc))
            nc.vector.tensor_tensor(cond[:, :, 2:4], sc, cond[:, :, 0:2], ALU.subtract).then_inc(cond_ready, 1)
            lo(0)
            lo(1)
            dve.wait_ge(ssum_ready, NT)
            ask_root(nc.vector.tensor_scalar(var[:, 0:NT], newton[:, 0:NT], 1.0 / D, EPS, ALU.mult, ALU.add))
            dve.wait_ge(var_ready, 1)
            finish_root(NT)
            for t in range(NT):
                nc.vector.tensor_scalar(x_in[:, t, :], x_in[:, t, :], rstd[:, t:t + 1], None, ALU.mult).then_inc(xn_ready, 1)
            dve.wait_ge(lam_in, 16 * 9)
            for i in range(2):
                link(nc.vector.tensor_tensor(lamv[:, 2 * i, :], lamv[:, 2 * i, :], lamv[:, 2 * i + 1, :], ALU.mult))
            nc.vector.tensor_reduce(lam[:, 0:2], lamv[:, :, :].rearrange("p (a b) d -> p a b d", b=2)[:, :, 0, :], axis=AX.X,
                                    op=ALU.add).then_inc(lam_e, 1)
            dve.wait_ge(lam_x, 1)
            link(nc.vector.tensor_tensor(lam[:, 4:5], lam[:, 2:3], lam[:, 3:4], ALU.subtract))
            link(nc.vector.tensor_scalar(lam[:, 5:6], lam[:, 4:5], LAMBDA_INIT, None, ALU.add))
            for i in range(2):
                for c in range(2):
                    g = gain[:, i, :].rearrange("p (a s c) -> p a s c", s=2, c=HD // 4)
                    g = g[:, :, ::-1, :] if c else g
                    for t in range(NT):
                        v = tab[:, i, c, t, :].rearrange("p (a s c) -> p a s c", s=2, c=HD // 4)
                        nc.vector.tensor_tensor(v, v, g, ALU.mult)
            nc.vector.tensor_scalar(g_sub[:, :], g_sub[:, :], 1.0 - LAMBDA_INIT, None, ALU.mult).then_inc(tab_ready, 1)
            dve.wait_ge(tab_ready, 1)
            for i in range(2):
                dve.wait_ge(wspT_done, i + 1)
                nc.vector.tensor_copy(wspT[:, 4 * i:4 * i + 4, :].rearrange("p g q -> p (g q)"), bank(5)[:, :]).then_inc(wspT_ready, 1)

            def conv(a):
                dve.wait_ge(conv_done, a + 1)
                if a in GATES:
                    g = GATES.index(a)
                    if g >= 2:
                        dve.wait_ge(grow_out[g % 2], 16)
                    nc.vector.tensor_copy(grow[:, g % 2, :], bank(7)[0:2, :]).then_inc(conv_ev, 1)
                else:
                    nc.vector.tensor_copy(mcol[:, VEC[a], 4 * (a % 2):4 * (a % 2) + 4, :].rearrange("p k c -> p (k c)"),
                                          bank(7)[:, 0:8]).then_inc(conv_ev, 1)
                dve.wait_ge(conv_ev, a + 1)

            def amplitude(out, vec, first):
                g = cols[:, first:first + KT].unsqueeze(2).broadcast_to([P, KT, 2])
                link(nc.vector.scalar_tensor_tensor(out=out[:, :, :], in0=mcol[:, vec, :, :], scalar=1.0, in1=g,
                                                    op0=ALU.add, op1=ALU.mult))

            def modulated(out, ps, k, n, amp, shift):
                v = ps.rearrange("p (k t) -> p k t", k=n)
                o = out.rearrange("p (k t) -> p k t", k=n)
                link(nc.vector.tensor_tensor(o, v, amp.unsqueeze(2).broadcast_to([P, n, P]), ALU.mult))
                return nc.vector.tensor_tensor(o, o, shift.unsqueeze(2).broadcast_to([P, n, P]), ALU.add)

            pending = []
            i_qk = [0]

            def qk_first():
                n = pending[0]
                dve.wait_ge(ev_act, emptied_before(PIECE_AT[n, NT - 1] + 1, "act"))
                nc.vector.tensor_reduce(var[:, 0:8 * NT], qk_sq[:, :, :].rearrange("p t (s d) -> p (t s) d", d=HD), axis=AX.X,
                                        op=ALU.add).then_inc(sq_free, 1)
                dve.wait_ge(sq_free, i_qk[0] + 1)
                nc.vector.tensor_scalar(var[:, 0:8 * NT], var[:, 0:8 * NT], 1.0 / HD, EPS, ALU.mult, ALU.add).then_inc(var_ready, 1)

            def qk_rest():
                i = i_qk[0]
                dve.wait_ge(var_ready, rooted[0] + 1)
                finish_root(8 * NT, (rstd_ready, i + 1))
                v = qk_raw[i % 2][:, :, :].rearrange("p t (s d) -> p (t s) d", d=HD)
                link(nc.vector.tensor_tensor(v, v, rstd[:, 0:8 * NT].unsqueeze(2).broadcast_to([P, 8 * NT, HD]), ALU.mult))
                c = tab[:, 1 if i < 2 else 0, 0]
                for t in range(NT):
                    w = qk_raw[i % 2][:, t, :].rearrange("p (s d) -> p s d", d=HD)
                    last = nc.vector.tensor_tensor(w, w, c[:, t, :].unsqueeze(1).broadcast_to([P, 8, HD]), ALU.mult)
                link(last)
                dve.wait_ge(swp_ready, i + 1)
                nc.vector.tensor_tensor(qk_raw[i % 2][:, :, :], qk_raw[i % 2][:, :, :], qk_swp[i % 2][:, :, :], ALU.add).then_inc(qk_ready, 1)
                i_qk[0] += 1
                pending.clear()

            converted = [0]
            for b in range(FIRST_WO):
                kind, j = BLOCKS[b]
                if pending:
                    qk_first()
                if not amid(b):
                    ahead(b)
                if pending:
                    qk_rest()
                if kind == "ada" and b < 4:
                    if j >= 1:
                        conv(j - 1)
                    if j == 3:
                        conv(3)
                        amplitude(amp1, 1, 16)
                        for p in range(2 * NT):
                            dve.wait_ge(piece_done, p + 1)
                            if p >= NSTAGE:
                                dve.wait_ge(h_ready, p - NSTAGE + 1)
                            if p < KT:
                                last = nc.vector.tensor_scalar(stage[:, p % NSTAGE, :], bank(p % RING), amp1[:, p, 0:1], mcol[:, 0, p, 0:1],
                                                               ALU.mult, ALU.add)
                            else:
                                k0 = 4 * (p - KT)
                                last = modulated(stage[:, p % NSTAGE, :], bank(p % RING), k0, 4, amp1[:, k0:k0 + 4, 1], mcol[:, 0, k0:k0 + 4, 1])
                            last.then_inc(ev_dve, 1)
                    continue
                if kind in ("q", "k"):
                    pending.append(b)
                if kind == "ga" and j == 0:
                    for t in range(NT):
                        last = nc.vector.bn_aggr(mv[:, t, :], bstat[:, t, :, :].rearrange("p a s -> p (a s)"))
                    link(last)
                    nc.vector.tensor_scalar(var[:, 0:NT], mv[:, :, 1], EPS, None, ALU.add).then_inc(var_ready, 1)
                    dve.wait_ge(var_ready, rooted[0] + 1)
                    finish_root(NT)
                    dve.wait_ge(ln_in, 32)
                    for t in range(NT):
                        link(nc.vector.tensor_scalar(ob[:, t, :], ob[:, t, :], mv[:, t, 0:1], rstd[:, t:t + 1], ALU.subtract, ALU.mult))
                        nc.vector.tensor_tensor(ob[:, t, :], ob[:, t, :], ln_g[:, :], ALU.mult).then_inc(zn_pre, 1)
                for t in range(NT):
                    if kind == "zv":
                        n = PIECE_AT[b, t]
                        dve.wait_ge(ev_act, emptied_before(n + 1, "act"))
                        last = nc.vector.bn_stats(bstat[:, t, j, :], ob[:, t, j * CW:(j + 1) * CW])
                        if t == NT - 1:
                            link(last)
                    if kind in ("zu", "gb"):
                        s = STAGE_AT[b, t]
                        dve.wait_ge(ev_act, emptied_before(PIECE_AT[b, t] + 1, "act"))
                        if kind == "gb":
                            dve.wait_ge(stage_mul, multiplied(STAGE_AT[BLOCKS.index(("zu", j)), t]))
                        w = ob[:, t, j * CW:(j + 1) * CW]
                        nc.vector.tensor_tensor(w, w, stage[:, s % NSTAGE, :], ALU.mult).then_inc(stage_mul, 1)
                    if t == 0 and b > 4 and BLOCKS[b - 1][0] == "ada":
                        conv(BLOCKS[b - 1][1])
                    if t == AMID_TILE and amid(b + 1):
                        ahead(b + 1)
                if b == SPATIAL_AFTER:
                    for i in range(2 * NT):
                        t, half = i // 2, i % 2
                        n = PIECE_AT["sp", i]
                        dve.wait_ge(piece_done, n + 1)
                        w = ob[:, t, half * CW:(half + 1) * CW].rearrange("p (g c) -> p g c", c=P)
                        bias = cols[:, 32 + 4 * half:36 + 4 * half].unsqueeze(2).broadcast_to([P, 4, P])
                        nc.vector.tensor_tensor(w, bank(n % RING).rearrange("p (g c) -> p g c", c=P), bias, ALU.add).then_inc(ev_dve, 1)
                    dve.wait_ge(ev_dve, emptied_before(PIECE_AT["sp", 2 * NT - 1] + 1, "dve"))
            ahead(FIRST_WO)
            amplitude(amp2, 3, 24)

            def combine(u):
                p, nk = u % NP, unit_keys(u)[1] * P
                dve.wait_ge(exp_done[0], u + 1)
                dve.wait_ge(exp_done[1], u + 1)
                link(nc.vector.reciprocal(rinv[:, u % 2, :], rsum[:, p, :]))
                link(nc.vector.tensor_tensor(rinv[:, u % 2, 1:2], rinv[:, u % 2, 1:2], lam[:, 5:6], ALU.mult))
                link(nc.vector.tensor_scalar(p_1[:, p, 0:nk], p_1[:, p, 0:nk], rinv[:, u % 2, 1:2], None, ALU.mult))
                nc.vector.scalar_tensor_tensor(out=p_0[:, p, 0:nk], in0=p_0[:, p, 0:nk], scalar=rinv[:, u % 2, 0:1], in1=p_1[:, p, 0:nk],
                                               op0=ALU.mult, op1=ALU.subtract).then_inc(a_done, 1)

            def o_out(u):
                h, t = u // NT, u % NT
                dve.wait_ge(pv_done, u + 1)
                dve.wait_ge(sag_ready, h + 1)
                nc.vector.tensor_tensor(o_t[:, t, h * P:(h + 1) * P], bank(6 + u % 2)[:, 0:P], sa_h[:, h % 2, t, :],
                                        ALU.mult).then_inc(o_ev, 1)

            for u in range(NU):
                nk = unit_keys(u)[1] * P
                for s in range(2):
                    dve.wait_ge(sc_done[s], u + 1)
                    nb = nbias[:, u % 2, s:s + 1]
                    src = bank_all[:, 2 * s:2 * s + 2, :].rearrange("p a n -> p (a n)")[:, 0:nk]
                    link(nc.vector.tensor_reduce(nb, src, axis=AX.X, op=ALU.max))
                    nc.vector.tensor_scalar(nb, nb, -HD ** -0.5, None, ALU.mult).then_inc(nb_done[s], 1)
                if u >= 1:
                    combine(u - 1)
                if u >= 4:
                    o_out(u - 4)
            combine(NU - 1)
            for u in range(NU - 4, NU):
                o_out(u)
            dve.wait_ge(o_ev, NU)

            dve.wait_ge(osq_ready, NU)
            nc.vector.tensor_scalar(var[:, 0:H * NT], var[:, 0:H * NT], 1.0 / VD, EPS, ALU.mult, ALU.add).then_inc(var_ready, 1)
            dve.wait_ge(var_ready, rooted[0] + 1)
            finish_root(H * NT)
            n2 = [0]

            def next_piece():
                n2[0] += 1
                dve.wait_ge(p2_done, n2[0])
                return bank((n2[0] - 1) % RING)

            for what, t in STEPS:
                if what == "M":
                    for h in range(H):
                        c = slice(h * VD, (h + 1) * VD)
                        last = nc.vector.scalar_tensor_tensor(out=o_t[:, t, c], in0=o_t[:, t, c], scalar=rstd[:, t * H + h:t * H + h + 1],
                                                              in1=ob[:, t, c], op0=ALU.mult, op1=ALU.add)
                    last.then_inc(merged, 1)
                elif what == "T":
                    for half in range(2):
                        ps = next_piece()
                        dve.wait_ge(mhi_ready, 2 * t + half + 1)
                        c = slice(4 * half, 4 * half + 4)
                        nc.vector.tensor_tensor(m_lo[:, t, c, :], ps.rearrange("p (k t) -> p k t", k=4), m_hi[:, t, c, :],
                                                ALU.subtract).then_inc(p2_ev, 1)
                elif what == "W":
                    if t == 0:
                        dve.wait_ge(gate1_in, 32)
                    dve.wait_ge(x2_in[t], 16)
                    for half in range(2):
                        ps = next_piece()
                        c = slice(half * CW, (half + 1) * CW)
                        tmp = xw[:, c]
                        nc.vector.tensor_tensor(tmp, ps, gate1[:, int(t == NL), c], ALU.mult).then_inc(p2_ev, 1)
                        dve.wait_ge(p2_ev, n2[0])
                        last = nc.vector.tensor_tensor(x2[:, t, c], x2[:, t, c], tmp, ALU.add)
                    last.then_inc(x2_ready, 1)
                    dve.wait_ge(x2_sq, t + 1)
                    nc.vector.tensor_scalar(var[:, t:t + 1], newton[:, 8 + t:9 + t], 1.0 / D, EPS, ALU.mult, ALU.add).then_inc(var_ready, 1)
                    dve.wait_ge(var_ready, rooted[0] + 1)
                    finish_root(1, c=t)
                    if t >= 2:
                        dve.wait_ge(p2_done, P2.index(("X", t - 2, 1)) + 1)
                    nc.vector.tensor_scalar(xn[t % 2][:, :], x2[:, t, :], rstd[:, t:t + 1], None, ALU.mult).then_inc(xn2_ready, 1)
                    dve.wait_ge(xnhi_ready, t + 1)
                    link(nc.vector.tensor_tensor(xn_lo[:, t, :], xn[t % 2][:, :], xn_hi[:, t, :], ALU.subtract))
                elif what == "X":
                    if t == 0:
                        dve.wait_ge(wr_in, 32)
                    if t >= 2:
                        dve.wait_ge(p2_done, P2.index(("L", t - 2, 0)) + 1)
                    cd = int(t == NL)
                    for half in range(2):
                        ps = next_piece()
                        k = 4 * half
                        modulated(h2T[t % 2][:, k:k + 4, :].rearrange("p k t -> p (k t)"), ps, k, 4,
                                  amp2[:, k:k + 4, cd], mcol[:, 2, k:k + 4, cd]).then_inc(p2_ev, 1)
                elif what == "L":
                    nc.vector.tensor_copy(lg[:, t, :], next_piece()[:, 0:E]).then_inc(p2_ev, 1)
                    dve.wait_ge(p2_ev, n2[0])
                    link(nc.vector.tensor_reduce(rst[:, t, 2:3], lg[:, t, :], axis=AX.X, op=ALU.max))
                    nc.vector.tensor_scalar(rst[:, t, 0:1], rst[:, t, 2:3], -1.0, None, ALU.mult).then_inc(lgb_ready, 1)
            for t in range(NT):
                dve.wait_ge(lge_ready, t + 1)
                link(nc.vector.reciprocal(rst[:, t, 3:4], rst[:, t, 1:2]))
                nc.vector.tensor_scalar(lg[:, t, :], lg[:, t, :], rst[:, t, 3:4], None, ALU.mult).then_inc(aff_ready, 1)
            for t in range(NT):
                n = n2[0]
                dve.wait_ge(p2_done, n + 1)
                nc.vector.tensor_copy(affT[:, t * P:(t + 1) * P], bank(n % RING)[0:E, 0:P]).then_inc(p2_ev, 1)
                n2[0] += 1
            dve.wait_ge(p2_ev, n2[0])
            for start, width, cap, off in ((0, LAT, CAP_L, 0), (LAT, CTX, CAP_C, CAP_L)):
                bufs = [affT, affW]
                for r in range(cap // 8):
                    v = gate_v[:, off + 8 * r:off + 8 * r + 8]
                    src, dst = bufs[r % 2][:, start:start + width], bufs[(r + 1) % 2][:, start:start + width]
                    link(nc.vector.max(v, src))
                    link(nc.vector.max_index(idx_u[:, off + 8 * r:off + 8 * r + 8], v, src))
                    if r < cap // 8 - 1:
                        link(nc.vector.match_replace(dst, v, src, -1.0))
            link(nc.vector.tensor_copy(idx_f[:, :], idx_u[:, :]))
            nc.vector.tensor_scalar(idx_f[:, CAP_L:CAP], idx_f[:, CAP_L:CAP], float(LAT), None, ALU.add).then_inc(idx_ready, 1)
            for i in range(NRAW):
                lo(PRE + i)
            for dst in (idx_c, gate_c):
                n = n2[0]
                dve.wait_ge(p2_done, n + 1)
                nc.vector.tensor_copy(dst[:, :], bank(n % RING)[0:CAP, 0:E]).then_inc(p2_ev, 1)
                n2[0] += 1
            dve.wait_ge(p2_ev, n2[0])
            dve.wait_ge(idxb_in, 16)
            dve.wait_ge(x2_out, 16 * NT)
            for t in range(NL):
                nc.vector.tensor_scalar(sel_l[:, t, :, :], idx_b[:, :, 0:CAP_L], token[:, t:t + 1], None, ALU.is_equal)
            nc.vector.tensor_scalar(sel_c[:, :, :], idx_b[:, :, CAP_L:CAP], token[:, NL:NT], None, ALU.is_equal).then_inc(sel_ready, 1)
            xe4 = xeT[:, :, :].rearrange("p e (k c) -> p e k c", k=KT)
            for k in range(KT):
                for part in range(3):
                    n = n2[0]
                    dve.wait_ge(p2_done, n + 1)
                    if part < 2:
                        out, src, cd = xe4[:, 8 * part:8 * part + 8, k, 0:CAP_L], bank(n % RING).rearrange("p (e c) -> p e c", c=CAP_L), 0
                    else:
                        out, src, cd = xe4[:, :, k, CAP_L:CAP], bank(n % RING)[:, 0:E * CAP_C].rearrange("p (e c) -> p e c", c=CAP_C), 1
                    nc.vector.tensor_scalar(out, src, amp2[:, k, cd:cd + 1], mcol[:, 2, k, cd:cd + 1], ALU.mult, ALU.add).then_inc(p2_ev, 1)
                    n2[0] += 1
            assert n2[0] == N_P2, n2[0]
            dve.wait_ge(p2_ev, N_P2)
            dve.wait_ge(tok_in, 16)

            link(nc.vector.tensor_scalar(xe_hi[:, :], xeT[:, 0, :], 1.0, None, ALU.mult))
            nc.vector.tensor_tensor(xe_lo[:, :], xeT[:, 0, :], xe_hi[:, :], ALU.subtract).then_inc(xe_ready, 1)

            def col(a, x):
                return a[:, x:x + 1] if isinstance(x, int) else a[:, bass.ds(x, 1)]

            def added(e, s, n):
                dve.wait_ge(sc2_done, e * (2 * NT) + (s + 1))
                w = yacc[:, s // 2, (s % 2) * CW:(s % 2 + 1) * CW]
                nc.vector.tensor_tensor(w, w, bank(n)[:, :], ALU.add).then_inc(sc2_ev, 1)

            def gated_output(e, half):
                dve.wait_ge(used, e * EC + (YE_STEP + 4 * half))
                c = slice(half * CW, (half + 1) * CW)
                nc.vector.tensor_tensor(yeg[:, c], bank(4 + half)[0:CAP, :], gate2[:, c], ALU.mult).then_inc(yeg_ready, 1)

            def output_lo(e, half):
                dve.wait_ge(yeh_ready, e * 2 + (half + 1))
                c = slice(half * CW, (half + 1) * CW)
                nc.vector.tensor_tensor(ye_lo[:, c], yeg[:, c], ye_hi[:, c], ALU.subtract).then_inc(ye_ready, 1)

            def expert(e, first, last):
                for i in range(EC):
                    j = i + AHEAD
                    if i == 0 and not first:
                        gated_output(e - 1, 1)
                    if i == 2 and not first:
                        output_lo(e - 1, 1)
                    fb = HID_STEP.get(i)
                    if fb is not None:
                        dve.wait_ge(sg_ready, e * 4 + (fb + 1))
                        dve.wait_ge(used, e * EC + 4 * (fb + 1))
                        if not first or fb >= 2:
                            dve.wait_ge(ht_done, e * 4 + (fb - 1))
                        nc.vector.scalar_tensor_tensor(out=hid[:, fb % 2, :], in0=bank(fb % 2 * 2 + 1)[0:CAP, :], scalar=col(gate_c, e),
                                                       in1=sg[:, fb % 2, :], op0=ALU.mult, op1=ALU.mult).then_inc(hid_ready, 1)
                    fb = HTO_STEP.get(i)
                    if fb is not None:
                        dve.wait_ge(hth_ready, e * 4 + (fb + 1))
                        nc.vector.tensor_tensor(hT_lo[:, 4 * fb:4 * fb + 4, :], bank(6)[:, 0:4 * CAP].rearrange("p (k c) -> p k c", k=4),
                                                hT_hi[:, 4 * fb:4 * fb + 4, :], ALU.subtract).then_inc(ht_ready, 1)
                    if i == YE_STEP:
                        if first:
                            dve.wait_ge(gate2_in, 32)
                        gated_output(e, 0)
                    if i == YE_STEP + 2:
                        output_lo(e, 0)
                    if i == XE_STEP and not last:
                        src = xeT[:, e + 1, :] if isinstance(e, int) else xeT[:, bass.ds(e + 1, 1), :].rearrange("p e n -> p (e n)")
                        dve.wait_ge(used, e * EC + 16)
                        nc.vector.tensor_scalar(xe_hi[:, :], src, 1.0, None, ALU.mult).then_inc(xeh_done, 1)
                        dve.wait_ge(xeh_done, e + 1)
                        nc.vector.tensor_tensor(xe_lo[:, :], src, xe_hi[:, :], ALU.subtract).then_inc(xe_ready, 1)
                    if i == SEL_STEP:
                        nc.vector.tensor_scalar(selT[:, :], tokens[0:CAP, :], col(idx_c, e), None, ALU.is_equal).then_inc(sel_done, 1)
                    if i - 1 in SC_STEPS and not first:
                        added(e - 1, SC_STEPS.index(i - 1), 7)
                    if not (last and j >= EC):
                        dve.wait_ge(hi_done, e * EC + (PRE + j + 1))
                        nc.vector.tensor_tensor(w_lo[:, j % NSPLIT], raw_slot(EXPERT_SLOT[j % NRAWE]), w_hi[:, j % NSPLIT],
                                                ALU.subtract).then_inc(lo_done, 1)

            expert(0, True, False)
            dve.wait_ge(yacc_in, 16)
            with dve.Fori(1, E - 1) as e:
                expert(e, False, False)
            expert(E - 1, False, True)
            gated_output(E - 1, 1)
            output_lo(E - 1, 1)
            for s in range(2 * NT):
                added(E - 1, s, END_BANKS[s % len(END_BANKS)])

        @block.gpsimd
        def _(pool):
            for p in range(2 * NT):
                pool.wait_ge(h_hi_ready, p + 1)
                src = stage[:, p % NSTAGE, :]
                if p < KT:
                    h, l = h_hi[:, p, 0:LAT], h_lo[:, p, 0:LAT]
                else:
                    k0 = 4 * (p - KT)
                    h, l = h_hi[:, k0:k0 + 4, LAT:TOK], h_lo[:, k0:k0 + 4, LAT:TOK]
                    src = src.rearrange("p (k t) -> p k t", k=4)
                nc.gpsimd.tensor_tensor(l, src, h, ALU.subtract).then_inc(h_ready, 1)
            def swapped_part(i):
                if i == 0:
                    pool.wait_ge(tab_ready, 1)
                pool.wait_ge(rstd_ready, i + 1)
                w = qk_swp[i % 2]
                v = w[:, :, :].rearrange("p t (s d) -> p (t s) d", d=HD)
                nc.gpsimd.tensor_tensor(v, v, rstd[:, 0:8 * NT].unsqueeze(2).broadcast_to([P, 8 * NT, HD]), ALU.mult).then_inc(po, 1)
                pool.wait_ge(po, i + 1)
                s = tab[:, 1 if i < 2 else 0, 1]
                for t in range(NT):
                    x = w[:, t, :].rearrange("p (s d) -> p s d", d=HD)
                    last = nc.gpsimd.tensor_tensor(x, x, s[:, t, :].unsqueeze(1).broadcast_to([P, 8, HD]), ALU.mult)
                last.then_inc(swp_ready, 1)

            def gate_store(g):
                a = GATES[g]
                pool.wait_ge(conv_ev, a + 1)
                pool.dma_start(gate_d[:, g // 2, (g % 2) * CW:(g % 2 + 1) * CW], grow[:, g % 2, :]).then_inc(grow_out[g % 2], 16)

            def qk_store(which):
                kind, j = which
                i = {"k": 0, "q": 2}[kind] + j
                pool.wait_ge(qk_ready, i + 1)
                c = j * CW
                src = qk_raw[i % 2]
                pool.dma_start(tiles(k_d if kind == "k" else q_d)[:, :, c:c + CW], src[:, :, :]).then_inc(qk_out[i % 2], 16)
                if kind == "k":
                    pool.dma_start(out_k[:, c:c + CW], src[:, NL, :]).then_inc(qk_out[i % 2], 16)
                if (kind, j) == ("q", 1):
                    pool.wait_ge(sq_free, 4)
                    pool.wait_ge(qk_out[0], 48)
                    pool.wait_ge(qk_out[1], 48)
                    pool.dma_start(ln_g[:, :], A["gmlp_ln_g"].broadcast_to([P, D])).then_inc(ln_in, 16)
                    pool.dma_start(ln_b[:, :], A["gmlp_ln_b"].broadcast_to([P, D])).then_inc(ln_in, 16)

            for b in range(5, FIRST_WO):
                kind, j = BLOCKS[b]
                c = j * CW
                if BLOCKS[b - 1][0] in ("k", "q"):
                    swapped_part({"k": 0, "q": 2}[BLOCKS[b - 1][0]] + BLOCKS[b - 1][1])
                    qk_store(BLOCKS[b - 1])
                if BLOCKS[b - 1][0] == "ada" and BLOCKS[b - 1][1] in GATES:
                    gate_store(GATES.index(BLOCKS[b - 1][1]))
                if kind in ("v", "ga"):
                    for t in range(NT):
                        if kind == "ga" and j == 0:
                            pool.wait_ge(zn_pre, t + 1)
                            nc.gpsimd.tensor_tensor(ob[:, t, :], ob[:, t, :], ln_b[:, :], ALU.add).then_inc(zn_ready, 1)
                        n = STAGE_AT[b, t]
                        pool.wait_ge(ev_act, emptied_before(PIECE_AT[b, t] + 1, "act"))
                        out = (v_d if kind == "v" else sa_d)[t * P:(t + 1) * P, c:c + CW]
                        pool.dma_start(out, stage[:, n % NSTAGE, :]).then_inc(stage_out[n % NSTAGE], 16)
                        if stores_of(n) == 2:
                            pool.dma_start(out_v[:, c:c + CW], stage[:, n % NSTAGE, :]).then_inc(stage_out[n % NSTAGE], 16)
            for h in range(H):
                pool.wait_ge(sa_in[h % 2], 16 * (h // 2 + 1))
                w = sa_h[:, h % 2]
                nc.gpsimd.tensor_tensor(w, w, g_sub[:, :].unsqueeze(1).broadcast_to([P, NT, VD]), ALU.mult).then_inc(sag_ready, 1)

        @block.tensor
        def _(pe):
            def split3(ps, hi, lo, wh, wl, first, last):
                nc.tensor.matmul(ps, hi, wh, start=first, stop=False)
                nc.tensor.matmul(ps, lo, wh, start=False, stop=False)
                return nc.tensor.matmul(ps, hi, wl, start=False, stop=last)

            def piece(n):
                if n >= RING:
                    who = PIECES[n - RING][2]
                    pe.wait_ge(ev_act if who == "act" else ev_dve, emptied_before(n - RING + 1, who))
                return bank(n % RING)

            def ada(a, b):
                pe.wait_ge(lo_done, 2 * b + 2)
                if a >= 1:
                    pe.wait_ge(m4_ready, a)
                ps = bank(6)[0:4, :]
                for n in (2 * b, 2 * b + 1):
                    for k in range(CK):
                        kk = (n % 2) * CK + k
                        nc.tensor.matmul(ps, cond[:, kk, :], w_hi[:, split_slot(n), k, :], start=(kk == 0), stop=False)
                        last = nc.tensor.matmul(ps, cond[:, kk, :], w_lo[:, split_slot(n), k, :], start=False, stop=(kk == KT - 1))
                last.then_inc(ada_done, 1)

            def conv(a):
                pe.wait_ge(m4_ready, a + 1)
                if a >= 1:
                    pe.wait_ge(conv_ev, a)
                if a in GATES:
                    nc.tensor.matmul(bank(7)[0:2, :], hilo[0:4, :], m4[:, a % 2, :], start=True, stop=False)
                    last = nc.tensor.matmul(bank(7)[0:2, :], pick[0:12, a, :], b12[:, :], start=False, stop=True)
                else:
                    for k in range(4):
                        out = bank(7)[:, 2 * k:2 * k + 2]
                        nc.tensor.matmul(out, m4[:, a % 2, k * P:(k + 1) * P], hilo[0:4, :], start=True, stop=False)
                        last = nc.tensor.matmul(out, b12[:, k * P:(k + 1) * P], pick[0:12, a, :], start=False, stop=True)
                last.then_inc(conv_done, 1)

            def token_pieces(lo_, hi_):
                for p in range(lo_, hi_):
                    ps = piece(p)
                    for i in range(4):
                        t, k = (i, p) if p < KT else (NL, 4 * (p - KT) + i)
                        last = nc.tensor.transpose(ps[:, i * P:(i + 1) * P], x_in[:, t, k * P:(k + 1) * P], ident[:, :])
                    last.then_inc(piece_done, 1)

            pe.wait_ge(rows_in, 96)
            nc.tensor.transpose(bank(7)[:, 0:40], rows40[:, :], ident[0:40, 0:40]).then_inc(rowsT_done, 1)
            pe.wait_ge(const_in, 48)
            pe.wait_ge(cond_ready, 1)
            ada(0, 0)
            pe.wait_ge(xn_ready, NT)
            pe.wait_ge(wsp_in, 16)
            for i in range(2):
                if i == 1:
                    pe.wait_ge(wspT_ready, 1)
                for g in range(4):
                    last = nc.tensor.transpose(bank(5)[:, g * P:(g + 1) * P], w_sp[:, 4 * i + g, :], ident[:, :])
                last.then_inc(wspT_done, 1)
            token_pieces(0, 3)
            ada(1, 1)
            conv(0)
            pe.wait_ge(wspT_ready, 2)
            token_pieces(3, 6)
            ada(2, 2)
            conv(1)
            ada(3, 3)
            conv(2)
            conv(3)
            token_pieces(6, 2 * NT)
            pe.wait_ge(h_ready, 2 * NT)
            for b in range(4, FIRST_WO):
                kind, j = BLOCKS[b]
                if not amid(b):
                    for t in range(NT):
                        ps = piece(PIECE_AT[b, t])
                        for n in (2 * b, 2 * b + 1):
                            if t == 0:
                                pe.wait_ge(lo_done, n + 1)
                            for k in range(CK):
                                kk = (n % 2) * CK + k
                                last = split3(ps, h_hi[:, kk, t * P:(t + 1) * P], h_lo[:, kk, t * P:(t + 1) * P],
                                              w_hi[:, split_slot(n), k, :], w_lo[:, split_slot(n), k, :], kk == 0, kk == KT - 1)
                        last.then_inc(piece_done, 1)
                        if t == 0 and BLOCKS[b - 1][0] == "ada" and b > 4:
                            conv(BLOCKS[b - 1][1])
                        if t == AMID_TILE and amid(b + 1):
                            ada(BLOCKS[b + 1][1], b + 1)
                if b == SPATIAL_AFTER:
                    for i in range(2 * NT):
                        t, half = i // 2, i % 2
                        pe.wait_ge(zn_ready, t + 1)
                        ps = piece(PIECE_AT["sp", i])
                        for g in range(4):
                            gg = 4 * half + g
                            last = nc.tensor.matmul(ps[:, g * P:(g + 1) * P], wspT[:, gg, :], ob[:, t, gg * P:(gg + 1) * P], start=True, stop=True)
                        last.then_inc(piece_done, 1)

            pe.wait_ge(ev_act, emptied_before(len(PIECES), "act"))
            pe.wait_ge(ev_dve, emptied_before(len(PIECES), "dve"))
            pe.wait_ge(conv_ev, 12)
            done = [0]

            def transposes(want):
                while done[0] < want:
                    n = done[0]
                    what, which, first, k = TRANSPOSED[n]
                    if n >= 2:
                        pe.wait_ge(tr_ev, n - 1)
                    if what == "a":
                        pe.wait_ge(a_done, which + 1)
                    elif first == 0:
                        pe.wait_ge(qkv_in[which % 2], 80 * (which // 2 + 1))
                    for i in range(k):
                        m = first + i
                        if what == "a":
                            src = p_0[:, which % NP, m * P:(m + 1) * P]
                        else:
                            src = q_h[which % 2][:, m, :] if m < NT else k_h[which % 2][:, m - NT, :]
                        last = nc.tensor.transpose(bank(4 + n % 2)[:, i * P:(i + 1) * P], src, ident[:, :])
                    last.then_inc(tr_done, 1)
                    done[0] += 1

            def scores(u):
                h, t = u // NT, u % NT
                k0, nk = unit_keys(u)
                if t == 0:
                    pe.wait_ge(tr_ev, transposed_upto("qk", h))
                for s in range(2):
                    if u >= 1:
                        pe.wait_ge(exp_done[s], u)
                    q = qT[HD * s:HD * s + HD, h % 2, t * P:(t + 1) * P]
                    for b, w in ((0, min(nk, 4) * P), (1, (nk - 4) * P)):
                        if w > 0:
                            c = k0 * P + b * CW
                            last = nc.tensor.matmul(bank(2 * s + b)[:, 0:w], q, kT[HD * s:HD * s + HD, h % 2, c:c + w], start=True, stop=True)
                    last.then_inc(sc_done[s], 1)

            def weigh(u):
                h = u // NT
                k0, nk = unit_keys(u)
                pe.wait_ge(tr_ev, transposed_upto("a", u))
                if u >= 2:
                    pe.wait_ge(osq_ready, u - 1)
                for k in range(nk):
                    last = nc.tensor.matmul(bank(6 + u % 2)[:, 0:P], aT[:, u % 2, k * P:(k + 1) * P], v_h[h % 2][:, k0 + k, :],
                                            start=(k == 0), stop=(k == nk - 1))
                last.then_inc(pv_done, 1)

            transposes(transposed_upto("qk", 0))
            for u in range(NU):
                scores(u)
                if u >= 3:
                    weigh(u - 3)
                if u >= 2:
                    transposes(transposed_upto("a", u - 2))
                if u % NT == 3 and u // NT + 1 < H:
                    transposes(transposed_upto("qk", u // NT + 1))
            weigh(NU - 3)
            transposes(len(TRANSPOSED))
            weigh(NU - 2)
            weigh(NU - 1)

            n2 = [0]

            def piece2():
                n = n2[0]
                if n >= RING:
                    pe.wait_ge(p2_ev, n - RING + 1)
                n2[0] += 1
                return bank(n % RING)

            for what, t in STEPS:
                if what == "T":
                    pe.wait_ge(merged, t + 1)
                    for half in range(2):
                        ps = piece2()
                        for i in range(4):
                            k = 4 * half + i
                            last = nc.tensor.transpose(ps[:, i * P:(i + 1) * P], o_t[:, t, k * P:(k + 1) * P], ident[:, :])
                        last.then_inc(p2_done, 1)
                elif what == "W":
                    pe.wait_ge(p2_ev, P2.index(("T", t, 1)) + 1)
                    for half in range(2):
                        b = FIRST_WO + half
                        if t == 0:
                            pe.wait_ge(lo_done, 2 * b + 2)
                        ps = piece2()
                        for n in (2 * b, 2 * b + 1):
                            for k in range(CK):
                                kk = (n % 2) * CK + k
                                last = split3(ps, m_hi[:, t, kk, :], m_lo[:, t, kk, :], w_hi[:, split_slot(n), k, :],
                                              w_lo[:, split_slot(n), k, :], kk == 0, kk == KT - 1)
                        last.then_inc(p2_done, 1)
                elif what == "X":
                    pe.wait_ge(xn2_ready, t + 1)
                    for half in range(2):
                        ps = piece2()
                        for i in range(4):
                            k = 4 * half + i
                            last = nc.tensor.transpose(ps[:, i * P:(i + 1) * P], xn[t % 2][:, k * P:(k + 1) * P], ident[:, :])
                        last.then_inc(p2_done, 1)
                elif what == "L":
                    pe.wait_ge(p2_ev, P2.index(("X", t, 1)) + 1)
                    ps = piece2()
                    for k in range(KT):
                        last = nc.tensor.matmul(ps[:, 0:E], h2T[t % 2][:, k, :], w_r[:, k, :], start=(k == 0), stop=(k == KT - 1))
                    last.then_inc(p2_done, 1)
            for t in range(NT):
                pe.wait_ge(aff_ready, t + 1)
                nc.tensor.transpose(piece2()[0:E, 0:P], lg[:, t, :], ident[:, :]).then_inc(p2_done, 1)
            pe.wait_ge(idx_ready, 1)
            for src in (idx_f, gate_v):
                nc.tensor.transpose(piece2()[0:CAP, 0:E], src[:, :], ident[0:E, 0:E]).then_inc(p2_done, 1)
            pe.wait_ge(sel_ready, 1)
            for k in range(KT):
                c = slice(k * P, (k + 1) * P)
                for part in range(3):
                    ps = piece2()
                    if part < 2:
                        for t in range(NL):
                            r = sel_l[:, t, 8 * part:8 * part + 8, :].rearrange("p e c -> p (e c)")
                            nc.tensor.matmul(ps, xn_hi[:, t, c], r, start=(t == 0), stop=False)
                            last = nc.tensor.matmul(ps, xn_lo[:, t, c], r, start=False, stop=(t == NL - 1))
                    else:
                        r = sel_c[:, :, :].rearrange("p e c -> p (e c)")
                        nc.tensor.matmul(ps[:, 0:E * CAP_C], xn_hi[:, NL, c], r, start=True, stop=False)
                        last = nc.tensor.matmul(ps[:, 0:E * CAP_C], xn_lo[:, NL, c], r, start=False, stop=True)
                    last.then_inc(p2_done, 1)
            pe.wait_ge(p2_ev, N_P2)

            def hid_transposes(e, fb):
                pe.wait_ge(hid_ready, e * 4 + (fb + 1))
                if not (isinstance(e, int) and e == 0 and fb == 0):
                    pe.wait_ge(ht_ready, e * 4 + fb)
                for k in range(4):
                    last = nc.tensor.transpose(bank(6)[:, k * CAP:(k + 1) * CAP], hid[:, fb % 2, k * P:(k + 1) * P], ident[0:CAP, 0:CAP])
                last.then_inc(ht_done, 1)

            def scatter(e, s, banks):
                t, half = s // 2, s % 2
                ps = bank(banks[s % len(banks)])
                if s == 0:
                    pe.wait_ge(sel_done, e + 1)
                if s < 2:
                    pe.wait_ge(ye_ready, e * 2 + (s + 1))
                if s >= len(banks):
                    pe.wait_ge(sc2_ev, e * (2 * NT) + (s + 1 - len(banks)))
                c = slice(half * CW, (half + 1) * CW)
                nc.tensor.matmul(ps, selT[:, t * P:(t + 1) * P], ye_hi[:, c], start=True, stop=False)
                nc.tensor.matmul(ps, selT[:, t * P:(t + 1) * P], ye_lo[:, c], start=False, stop=True).then_inc(sc2_done, 1)

            def expert(e, first, last_e):
                pe.wait_ge(xe_ready, e + 1)
                for i in range(EC):
                    s = i % NSPLIT
                    pe.wait_ge(lo_done, e * EC + (PRE + i + 1))
                    if i < 16:
                        fb, which, half = i // 4, i // 2 % 2, i % 2
                        ps = bank(fb % 2 * 2 + which)[0:CAP, :]
                        if half == 0 and (not first or fb >= 2):
                            pe.wait_ge(hid_ready, e * 4 + (fb - 1))
                        for k in range(CK):
                            kk = half * CK + k
                            c = slice(kk * CAP, (kk + 1) * CAP)
                            last = split3(ps, xe_hi[:, c], xe_lo[:, c], w_hi[:, s, k, :], w_lo[:, s, k, :], kk == 0, kk == KT - 1)
                    else:
                        half, q = (i - 16) // 4, (i - 16) % 4
                        ps = bank(4 + half)[0:CAP, :]
                        if q == 0 and not first:
                            pe.wait_ge(yeg_ready, e * 2 + (half - 1))
                        pe.wait_ge(ht_ready, e * 4 + (q + 1))
                        for k in range(CK):
                            f = q * CK + k
                            last = split3(ps, hT_hi[:, f, :], hT_lo[:, f, :], w_hi[:, s, k, :], w_lo[:, s, k, :], f == 0, f == FE // P - 1)
                    last.then_inc(used, 1)
                    if i in HID_STEP:
                        hid_transposes(e, HID_STEP[i])
                    if i in SC_STEPS and not first:
                        scatter(e - 1, SC_STEPS.index(i), [7])

            expert(0, True, False)
            with pe.Fori(1, E - 1) as e:
                expert(e, False, False)
            expert(E - 1, False, True)
            for s in range(2 * NT):
                scatter(E - 1, s, END_BANKS)


_INS = ["x_prompt", "x_sample", "cache_k", "cache_v", "c", "c_ctx", "w_ada", "b_ada", "norm1_g", "norm2_g", "w_in",
        "q_norm_g", "k_norm_g", "lambda_q1", "lambda_k1", "lambda_q2", "lambda_k2", "subln_g", "gmlp_ln_g",
        "gmlp_ln_b", "w_spatial", "b_spatial", "w_out", "w_router", "w_gate_e", "w_up_e", "w_down_e"]
_OUTS = [(1, CTX, D), (1, LAT, D), (1, 1, CTX, H, 2, HD), (1, 1, CTX, H, VD)]


def kernel(**inputs):
    import numpy as _np
    import concourse.bacc as _bacc
    from concourse import mybir as _mybir
    from concourse.bass_utils import run_bass_kernel_spmd as _run

    nc = _bacc.Bacc("TRN2", target_bir_lowering=False, num_devices=1)
    arrays = {f"in_{name}": _np.ascontiguousarray(inputs[name]) for name in _INS}
    arrays.update({f"in_{name}": _np.ascontiguousarray(a) for name, a in constants().items()})
    aps = {name[3:]: nc.dram_tensor(name, a.shape, _mybir.dt.from_np(a.dtype), kind="ExternalInput").ap()
           for name, a in arrays.items()}
    outs = [nc.dram_tensor(f"out_{i}", shape, F32, kind="ExternalOutput").ap() for i, shape in enumerate(_OUTS)]
    trunk_program(nc, aps, *outs)
    r = _run(nc, [arrays], core_ids=[0])
    return tuple(r.results[0][f"out_{i}"] for i in range(len(_OUTS)))
```

```python
from contextlib import ExitStack

import numpy as np
import concourse.bass as bass
from concourse import mybir

F32 = mybir.dt.float32
F32R = mybir.dt.float32r
U32 = mybir.dt.uint32
ALU = mybir.AluOpType
ACT = mybir.ActivationFunctionType
AX = mybir.AxisListType

P = 128
D = 1024
KT = D // P
LAT = 512
CTX = 128
NL = LAT // P
NT = NL + CTX // P
TOK = LAT + CTX
PAST = 256
NPAST = PAST // P
H = 8
HD = 64
VD = 128
G = 8
E = 16
FE = 2048
CAP_L = 2 * LAT // E
CAP_C = 2 * CTX // E
CAP = CAP_L + CAP_C
GRID_W = 64
EPS = 1e-6
LAMBDA_INIT = 0.8 - 0.6
CW = 512
CK = 4
NRAW = 3
NRAWE = NRAW + 1
NR = 6
NP = 3
NSPLIT = 4

BLOCKS = ([("ada", a) for a in range(4)]
          + [("k", 0), ("k", 1), ("q", 0), ("q", 1), ("v", 0), ("ada", 4), ("v", 1), ("ada", 5),
             ("zv", 0), ("ada", 6), ("zv", 1), ("ada", 7), ("ga", 0), ("ada", 8), ("ga", 1), ("ada", 9),
             ("zu", 0), ("ada", 10), ("zu", 1), ("ada", 11), ("gb", 0), ("gb", 1), ("wo", 0), ("wo", 1)])
COLUMN = {"q": 0, "k": 2, "v": 4, "zu": 6, "zv": 8, "ga": 10, "gb": 12}
NB = len(BLOCKS)
FIRST_WO = NB - 2
PRE = 2 * NB
EC = 24
GATES = [4, 5, 10, 11]
VEC = {0: 0, 1: 0, 2: 1, 3: 1, 6: 2, 7: 2, 8: 3, 9: 3}
EXPERT_SLOT = [(PRE + j) % NRAW for j in range(NRAW)] + [NRAW]
RAW_BEFORE = [len(range(s, PRE, NRAW)) for s in range(NRAW)] + [0]
SPATIAL_AFTER = BLOCKS.index(("ada", 8))


def is_in(kind):
    return kind in COLUMN


def amid(b):
    return b > 4 and b < NB and BLOCKS[b][0] == "ada"


def split_pairs():
    pair = []
    for b in range(NB):
        pair.append(0 if b == 0 else pair[-1] if amid(b - 1) else 1 - pair[-1])
    return pair


PAIR = split_pairs()
assert PAIR[-1] == 1
AMID_TILE = 2


def split_slot(n):
    return 2 * PAIR[n // 2] + n % 2


def split_before(n):
    before = [m for m in range(n) if split_slot(m) == split_slot(n)]
    return before[-1] if before else None


def piece_plan():
    plan = [("xt", i, "dve") for i in range(2 * NT)]
    for b, (kind, j) in enumerate(BLOCKS[:FIRST_WO]):
        if is_in(kind):
            plan += [(b, t, "act") for t in range(NT)]
        if b == SPATIAL_AFTER:
            plan += [("sp", i, "dve") for i in range(2 * NT)]
    return plan


PIECES = piece_plan()
PIECE_AT = {(a, i): n for n, (a, i, _) in enumerate(PIECES)}
RING = 6


def emptied_before(n, who):
    return sum(1 for p in PIECES[:n] if p[2] == who)


STAGED = [(b, t) for b, (kind, _) in enumerate(BLOCKS) if kind in ("v", "ga", "zu", "gb") for t in range(NT)]
STAGE_AT = {s: n for n, s in enumerate(STAGED)}
NSTAGE = 3


def stores_of(n):
    b, t = STAGED[n]
    kind = BLOCKS[b][0]
    return (2 if kind == "v" and t == NL else 1) if kind in ("v", "ga") else 0


def stage_stored(n):
    return 16 * sum(stores_of(m) for m in range(n % NSTAGE, n + 1, NSTAGE))


def multiplied(n):
    return sum(1 for m in range(n + 1) if stores_of(m) == 0)


NU = H * NT


def unit_keys(u):
    return (0, NPAST + NL) if u % NT < NL else (NPAST + NL, 1)


EARLY_QK = 2


def before_head(u, n):
    return u % NT == NT - n and u // NT + 1 < H


def transposed_plan():
    def of_head(h):
        return [("qk", h, i, 4) for i in range(0, 12, 4)]

    def of_unit(u):
        n = unit_keys(u)[1]
        return [("a", u, i, min(4, n - i)) for i in range(0, n, 4)]

    plan = of_head(0)
    for u in range(NU):
        plan += of_head(u // NT + 1)[EARLY_QK:] if before_head(u, 1) else []
        if u >= 2:
            plan += of_unit(u - 2)
        plan += of_head(u // NT + 1)[:EARLY_QK] if before_head(u, 2) else []
    return plan + of_unit(NU - 2) + of_unit(NU - 1)


TRANSPOSED = transposed_plan()


def transposed_upto(what, which):
    return max(n for n, p in enumerate(TRANSPOSED) if p[:2] == (what, which)) + 1


def qk_upto(h, pieces):
    return TRANSPOSED.index(("qk", h, 4 * (pieces - 1), 4)) + 1


def of_kind(n, what):
    return sum(1 for p in TRANSPOSED[:n] if p[0] == what)


SG_STEP = {4 * fb + 2: fb for fb in range(4)}
HID_STEP = {4 * fb + 4: fb for fb in range(4)}
HT_STEP = {4 * fb + 5: fb for fb in range(4)}
HTO_STEP = {4 * fb + 6: fb for fb in range(4)}
YE_STEP = 20
XE_STEP = 21
SEL_STEP = 22
SC_STEPS = [0, 2, 4, 6, 8, 10, 12, 14, 16, 18]
SC_PIECES = list(range(0, 2 * NT, 2)) + list(range(1, 2 * NT, 2))
AHEAD = NSPLIT - 1
END_STEP = 22
END_BANKS = [7, 0, 1, 2, 3, 6]
STEPS = [("M", 0), ("M", 1), ("T", 0), ("T", 1), ("M", 2), ("M", 3), ("W", 0, 0), ("W", 0, 1), ("N", 0), ("R", 0), ("T", 2), ("M", 4),
         ("W", 1, 0), ("W", 1, 1), ("N", 1), ("R", 1), ("T", 3), ("X", 0), ("W", 2, 0), ("W", 2, 1), ("N", 2), ("R", 2), ("L", 0), ("T", 4), ("X", 1),
         ("W", 3, 0), ("W", 3, 1), ("N", 3), ("R", 3), ("L", 1), ("X", 2), ("W", 4, 0), ("L", 2), ("X", 3), ("L", 3), ("A", 0),
         ("K", 0), ("K", 1), ("K", 2), ("W", 4, 1), ("K", 3), ("N", 4), ("K", 4), ("R", 4), ("K", 5),
         ("X", 4), ("K", 6), ("L", 4), ("K", 7), ("A", 1), ("K", 8), ("K", 9)]
GROUP = [range(NL), range(NL, NT)]


def pieces_of(step):
    if step[0] == "W":
        return [step]
    return [(step[0], step[1], i) for i in range({"T": 2, "X": 2, "L": 1, "A": 1}.get(step[0], 0))]


P2 = [p for step in STEPS for p in pieces_of(step)]
N_P2 = len(P2) + 2 + 3 * KT


def constants():
    half = HD // 4
    inv = np.float32(10000.0) ** (-np.arange(half, dtype=np.float32) / np.float32(half))
    row = np.repeat(np.arange(LAT // GRID_W, dtype=np.float32), GRID_W)[:, None] * inv
    col = np.tile(np.arange(GRID_W, dtype=np.float32), LAT // GRID_W)[:, None] * inv
    ang = np.concatenate([row, row, col, col], axis=-1).astype(np.float32)
    sign = np.repeat(np.array([-1, 1, -1, 1], np.float32), half)
    cos = np.ones((TOK, HD), np.float32)
    sin = np.zeros((TOK, HD), np.float32)
    cos[:LAT] = np.cos(ang)
    sin[:LAT] = np.sin(ang) * sign
    rope = np.stack([a.reshape(NT, P, HD).transpose(1, 0, 2) for a in (cos, sin)], axis=1)
    ident = np.eye(P, dtype=np.float32)
    token = (np.arange(P)[:, None] + P * np.arange(NT)[None]).astype(np.float32)
    tokens = np.tile(np.arange(TOK, dtype=np.float32)[None], (P, 1))
    hilo = np.zeros((P, 2), np.float32)
    hilo[:4] = np.tile(np.eye(2, dtype=np.float32), (2, 1))
    pick = np.zeros((P, 12, 2), np.float32)
    for a in range(12):
        pick[a, a] = 1.0
    return {"rope": rope.reshape(P, -1), "ident": ident, "token": token, "tokens": tokens,
            "hilo": hilo, "pick": pick.reshape(P, -1)}


def trunk_program(nc, A, O_y, O_ys, O_k, O_v):
    def scratch(name, shape):
        return nc.dram_tensor(name, shape, F32, kind="Internal").ap()

    q_d, k_d, v_d = (scratch(n, [TOK, D]) for n in ("q_scr", "k_scr", "v_scr"))
    sa_d, x2_d = (scratch(n, [TOK, D]) for n in ("sa_scr", "x2_scr"))
    gate_d = scratch("gate_scr", [2, 2, D])
    idx_d = scratch("idx_scr", [E, CAP])
    w_ada = A["w_ada"].rearrange("z k n -> (z k) n")
    w_in = A["w_in"].rearrange("z k n -> (z k) n")
    w_out = A["w_out"].rearrange("z k n -> (z k) n")
    w_gate = A["w_gate_e"].rearrange("z e (k p) n -> (z e) p k n", p=P)
    w_up = A["w_up_e"].rearrange("z e (k p) n -> (z e) p k n", p=P)
    w_down = A["w_down_e"].rearrange("z e (k p) n -> (z e) p k n", p=P)
    x_l = A["x_sample"].rearrange("b (t p) d -> p (b t) d", p=P)
    x_c = A["x_prompt"].rearrange("b p d -> p b d")
    ck = A["cache_k"].rearrange("b z (t p) h s d -> p (b z t) h (s d)", p=P)
    cv = A["cache_v"].rearrange("b z (t p) h d -> p (b z t) h d", p=P)
    out_k = O_k.rearrange("b z p h s d -> p (b z h s d)")
    out_v = O_v.rearrange("b z p h d -> p (b z h d)")
    y_l = O_ys.rearrange("b (t p) d -> p (b t) d", p=P)
    y_c = O_y.rearrange("b p d -> p b d")

    def tiles(d):
        return d.rearrange("(t p) n -> p t n", p=P)

    def chunk_source(n):
        kind, j = BLOCKS[n // 2]
        w = {"ada": w_ada, "wo": w_out}.get(kind, w_in)
        c = (COLUMN.get(kind, 0) + j) * CW
        r = (n % 2) * CK * P
        return w[r:r + CK * P, c:c + CW].rearrange("(k p) n -> p k n", p=P)

    def expert_source(e, i):
        if i < 16:
            w, fb, half = (w_gate, w_up)[i // 2 % 2], i // 4, i % 2
            return w[e, :, half * CK:half * CK + CK, fb * CW:fb * CW + CW] if isinstance(e, int) else \
                w[bass.ds(e, 1), :, half * CK:half * CK + CK, fb * CW:fb * CW + CW].rearrange("e p k n -> p (e k) n")
        half, q = (i - 16) // 4, (i - 16) % 4
        return w_down[e, :, q * CK:q * CK + CK, half * CW:half * CW + CW] if isinstance(e, int) else \
            w_down[bass.ds(e, 1), :, q * CK:q * CK + CK, half * CW:half * CW + CW].rearrange("e p k n -> p (e k) n")

    base = (nc.sbuf_base + 31) // 32 * 32
    end = nc.sbuf_usable_end // 32 * 32
    at = [base]

    def place(name, shape, dt=F32, offset=None):
        size = 4 * int(np.prod(shape[1:]))
        o = at[0] if offset is None else offset
        assert o + size <= end, (name, o + size - end)
        if offset is None:
            at[0] += (size + 31) // 32 * 32
        return nc.alloc_sbuf_tensor_at(name, list(shape), dt, offset=o)

    raw = place("raw", [P, NRAW, CK, CW])
    w_hi = place("w_hi", [P, NSPLIT, CK, CW], F32R)
    w_lo = place("w_lo", [P, NSPLIT, CK, CW], F32R)
    MID = at[0]
    h_hi = place("h_hi", [P, KT, TOK], F32R)
    h_lo = place("h_lo", [P, KT, TOK], F32R)
    LOW = at[0]
    ident = place("ident_sb", [P, P])
    token = place("token_sb", [P, NT])
    cols = place("cols", [P, 40])
    mcol = place("mcol", [P, 4, KT, 2])
    amp1 = place("amp1", [P, KT, 2])
    amp2 = place("amp2", [P, KT, 2])
    var = place("var", [P, 40])
    root = place("root", [P, 40])
    rstd = place("rstd", [P, 40])
    newton = place("newton", [P, 40])
    lam = place("lam", [P, 8])
    w_r = place("w_r", [P, KT, E])
    g_sub = place("g_sub", [P, VD])
    gate_v = place("gate_v", [E, CAP])
    idx_u = place("idx_u", [E, CAP], U32)
    idx_f = place("idx_f", [E, CAP])
    KEEP = at[0]
    tab = place("tab", [P, 2, 2, NT, HD])
    gain = place("gain", [P, 2, HD])
    hilo = place("hilo_sb", [P, 2])
    pick = place("pick_sb", [P, 12, 2])
    b12 = place("b12", [12, CW])
    m4 = place("m4", [4, 2, CW])
    grow = place("grow", [2, 2, CW])
    silu_c = place("silu_c", [P, 2, KT])
    cond = place("cond", [P, KT, 4], F32R)
    bstat = place("bstat", [P, NT, 2, 6])
    mv = place("mv", [P, NT, 2])
    wspT = place("wspT", [P, G, P])
    stage = place("stage", [P, NSTAGE, CW])
    WORK = at[0]
    qk_raw = [place(f"qk_raw{i}", [P, NT, CW]) for i in range(2)]
    qk_swp = [place(f"qk_swp{i}", [P, NT, CW]) for i in range(2)]
    qk_sq = place("qk_sq", [P, NT, CW])
    lamv = place("lamv", [P, 4, HD], offset=WORK + 4 * 4 * NT * CW)
    x_in = place("x_in", [P, NT, D], offset=WORK)
    x_junk = place("x_junk", [P, D], offset=WORK + 4 * NT * D)
    rows40 = place("rows40", [40, P], offset=WORK + 4 * NT * D + 4096)
    w_sp = place("w_sp", [P, G, P], offset=WORK + 4 * NT * D + 8192)
    ob = place("ob", [P, NT, D], offset=WORK)
    ln_g = place("ln_g", [P, D], offset=WORK + 4 * NT * D)
    ln_b = place("ln_b", [P, D], offset=WORK + 4 * NT * D + 4096)
    p_0 = place("p_0", [P, NP, PAST + LAT], offset=MID)
    at[0] = MID + 4 * NP * (PAST + LAT)
    p_1 = place("p_1", [P, NP, PAST + LAT])
    aT = place("aT", [P, 2, PAST + LAT])
    qT_hi = place("qT_hi", [P, 2, TOK], F32R)
    kT_hi = place("kT_hi", [P, 2, PAST + TOK], F32R)
    qT_lo0 = place("qT_lo0", [P, TOK], F32R)
    assert at[0] <= LOW

    def head_slot(i):
        return [place(f"{n}{i}", [P, w, P]) for n, w in (("q_h", NT), ("k_h", NPAST + NT), ("v_h", NPAST + NT))]

    at[0] = KEEP
    slot1 = head_slot(1)
    sa_h = place("sa_h", [P, 2, NT, P])
    kT_lo = place("kT_lo", [P, 2, PAST + TOK], F32R)
    qT_lo = [qT_lo0, place("qT_lo1", [P, TOK], F32R)]
    nbias = place("nbias", [P, 2, 2])
    rsum = place("rsum", [P, NP, 2])
    rinv = place("rinv", [P, NR, 2])
    sq_junk = place("sq_junk", [P, 2, P])
    lg = place("lg", [P, NT, E])
    rst = place("rst", [P, NT, 4])
    assert at[0] <= WORK
    at[0] = WORK + 4 * NT * D
    o_t = place("o_t", [P, NT, D])
    q_h, k_h, v_h = zip(head_slot(0), slot1)
    m_hi = place("m_hi", [P, NT, KT, P], F32R, offset=MID)
    m_lo = place("m_lo", [P, NT, KT, P], F32R, offset=MID + 4 * KT * TOK)
    x2 = place("x2", [P, NT, D], offset=WORK)
    xw = place("xw", [P, 2 * CW], offset=WORK + 4 * NT * D)
    p_sq = place("p_sq", [P, D], offset=WORK + 4 * NT * D + 4 * D)
    xn = [place(f"xn{i}", [P, D], offset=WORK + 8 * NT * D + 4 * D * i) for i in range(2)]
    gate1 = place("gate1", [P, 2, D], offset=KEEP)
    h2T = [place(f"h2T{i}", [P, KT, P], offset=KEEP + 4 * (5 * NT + 2 * NPAST) * P + 4 * D * i) for i in range(2)]
    affT = place("affT", [E, TOK], offset=KEEP + 4 * (3 * NT + 2 * NPAST) * P)
    affW = place("affW", [E, TOK], offset=KEEP + 4 * (4 * NT + 2 * NPAST) * P)
    xn_hi = place("xn_hi", [P, NT, D], F32R, offset=MID)
    xn_lo = place("xn_lo", [P, NT, D], F32R, offset=MID + 4 * NT * D)
    at[0] = KEEP
    idx_c = place("idx_c", [CAP, E])
    gate_c = place("gate_c", [CAP, E])
    tokens = place("tokens_sb", [P, TOK])
    selT = place("selT", [CAP, TOK], F32R)
    XE = at[0]
    sel_l = place("sel_l", [P, NL, E, CAP_L], F32R, offset=end - 4 * (NL * E * CAP_L + E * CAP_C) - 32)
    sel_c = place("sel_c", [P, E, CAP_C], F32R, offset=end - 4 * E * CAP_C - 32)
    idx_b = place("idx_b", [P, E, CAP], offset=XE)
    xeT = place("xeT", [P, E, KT * CAP], offset=XE + 4 * E * CAP)
    assert XE + 4 * E * CAP + 4 * E * KT * CAP <= end - 4 * (NL * E * CAP_L + E * CAP_C) - 32
    at[0] = XE + 4 * E * CAP + 4 * E * KT * CAP
    raw_x = place("raw_x", [P, CK, CW])
    hT_hi = place("hT_hi", [P, FE // P, CAP], F32R)
    hT_lo = place("hT_lo", [P, FE // P, CAP], F32R)
    xe_hi = place("xe_hi", [P, KT * CAP], F32R)
    xe_lo = place("xe_lo", [P, KT * CAP], F32R)
    ye_hi = place("ye_hi", [CAP, D], F32R, offset=XE)
    at[0] = MID
    yacc = place("yacc", [P, NT, D])
    gate2 = place("gate2", [CAP, D])
    yeg = place("yeg", [CAP, D])
    ye_lo = place("ye_lo", [CAP, D], F32R)
    sg = place("sg", [CAP, 2, CW])
    hid = place("hid", [CAP, 2, CW])
    assert at[0] <= LOW

    def raw_slot(i):
        return raw[:, i] if i < NRAW else raw_x[:, :, :]

    ctx = ExitStack()
    bank_all = nc.alloc_psum_tensor("banks", [P, 8, CW], F32)

    def bank(i):
        return bank_all[:, i, :]

    with ctx:
        def sem(name):
            return ctx.enter_context(nc.semaphore(name))

        def sems(names):
            return [sem(n) for n in names.split()]

        raw_in = [sem(f"raw_in{i}") for i in range(NRAWE)]
        hi_done, lo_done, chunk_read = sems("hi_done lo_done chunk_read")
        dve_self, pool_self = sems("dve_self pool_self")
        rows_in, const_in, x_load, lam_in, wsp_in, ln_in, wr_in = sems("rows_in const_in x_load lam_in wsp_in ln_in wr_in")
        rowsT_done, cols_ready, silu_ready, cond_ready, lam_sums, lam_exps = sems("rowsT_done cols_ready silu_ready cond_ready lam_sums lam_exps")
        var_ready, root_done = sems("var_ready root_done")
        ssum_ready, xn_ready, h_hi_ready, h_ready = sems("ssum_ready xn_ready h_hi_ready h_ready")
        ada_done, m4_ready, conv_done, conv_ready = sems("ada_done m4_ready conv_done conv_ready")
        grow_out = [sem(f"grow_out{i}") for i in range(2)]
        piece_done, piece_out_act, piece_out_dve = sems("piece_done piece_out_act piece_out_dve")
        tab_ready, wspT_done, wspT_ready = sems("tab_ready wspT_done wspT_ready")
        sq_free, rstd_ready, swp_ready, qk_ready = sems("sq_free rstd_ready swp_ready qk_ready")
        qk_out = [sem(f"qk_out{i}") for i in range(2)]
        stage_out = [sem(f"stage_out{i}") for i in range(NSTAGE)]
        stage_mul, zn_pre, zn_ready = sems("stage_mul zn_pre zn_ready")
        qkv_in, sa_in = [sem(f"qkv_in{i}") for i in range(2)], [sem(f"sa_in{i}") for i in range(2)]
        tr_done, qk_hi = sems("tr_done qk_hi")
        tr_emptied = {"qk": sem("qk_lo"), "a": sem("aT_ready")}
        sc_done, max_done, exp_done = ([sem(f"{n}{i}") for i in range(2)] for n in ("sc_done", "max_done", "exp_done"))
        a_done, pv_done, o_ready, osq_ready, sag_ready, og_ready = sems("a_done pv_done o_ready osq_ready sag_ready og_ready")
        merged, mhi_ready, gate1_in, x2_ready, x2_sq, xn2_ready, xnhi_ready, xnlo_ready, x2_out = sems("merged mhi_ready gate1_in x2_ready x2_sq xn2_ready xnhi_ready xnlo_ready x2_out")
        x2_in = [sem(f"x2_in{t}") for t in range(NT)]
        p2_done, p2_emptied = sems("p2_done p2_emptied")
        lgb_ready, lge_ready, aff_ready, idx_ready, idx_out, idxb_in, tok_in, sel_ready = sems("lgb_ready lge_ready aff_ready idx_ready idx_out idxb_in tok_in sel_ready")
        xeh_done, xe_ready, sg_ready, hid_ready, ht_done, hth_ready, ht_ready = sems("xeh_done xe_ready sg_ready hid_ready ht_done hth_ready ht_ready")
        yeg_ready, yeh_ready, ye_ready, sel_done, out_placed, out_added = sems("yeg_ready yeh_ready ye_ready sel_done out_placed out_added")
        yacc_in, gate2_in, y_out = sems("yacc_in gate2_in y_out")

        block = ctx.enter_context(nc.Block())

        def qk_parts(h, first, ps):
            p = h % 2
            if first < 4:
                return [(qT_hi[:, p, 0:4 * P], qT_lo[p][:, 0:4 * P], ps[:, 0:4 * P])]
            if first < 8:
                return [(qT_hi[:, p, 4 * P:5 * P], qT_lo[p][:, 4 * P:5 * P], ps[:, 0:P]),
                        (kT_hi[:, p, 0:3 * P], kT_lo[:, p, 0:3 * P], ps[:, P:4 * P])]
            return [(kT_hi[:, p, 3 * P:7 * P], kT_lo[:, p, 3 * P:7 * P], ps[:, 0:4 * P])]

        def raw_count(n):
            return 16 * (n // NRAW + 1)

        def wait_read(eng, n):
            b = n // 2
            kind, j = BLOCKS[b]
            if kind == "ada":
                eng.wait_ge(ada_done, j + 1)
            elif kind == "wo":
                eng.wait_ge(p2_done, P2.index(("W", NT - 1, j)) + 1)
            else:
                eng.wait_ge(piece_done, PIECE_AT[b, NT - 1] + 1)

        @block.sync
        def _(sp):
            def load(n):
                if n >= NRAW:
                    sp.wait_ge(lo_done, n - NRAW + 1)
                src = chunk_source(n) if n < PRE else expert_source(0, n - PRE)
                sp.dma_start(raw[:, n % NRAW], src).then_inc(raw_in[n % NRAW], 16)

            for i, name in enumerate(["c", "c_ctx", "norm1_g", "norm2_g"]):
                v = A[name]
                flat = v.rearrange("(k p) -> k p", p=P) if len(v.shape) == 1 else v.rearrange("z (k p) -> (z k) p", p=P)
                sp.dma_start(rows40[8 * i:8 * i + 8, :], flat).then_inc(rows_in, 16)
            sp.dma_start(rows40[32:40, :], A["b_spatial"].rearrange("z g p -> (z g) p")).then_inc(rows_in, 16)
            sp.dma_start(ident[:, :], A["ident"]).then_inc(rows_in, 16)
            load(0)
            load(1)
            sp.dma_start(x_in[:, 0:NL, :], x_l).then_inc(x_load, 16)
            sp.dma_start(x_in[:, NL:NT, :], x_c).then_inc(x_load, 16)
            sp.dma_start(hilo[:, :], A["hilo"]).then_inc(const_in, 16)
            sp.dma_start(pick[:, :, :].rearrange("p a b -> p (a b)"), A["pick"]).then_inc(const_in, 16)
            sp.dma_start(b12[:, :], A["b_ada"].rearrange("z (a n) -> (z a) n", n=CW)).then_inc(const_in, 16)
            load(2)
            for i, name in enumerate(["q_norm_g", "k_norm_g"]):
                sp.dma_start(tab[:, i, :, :, :].rearrange("p a t d -> p (a t d)"), A["rope"]).then_inc(lam_in, 16)
                sp.dma_start(gain[:, i, :], A[name].broadcast_to([P, HD])).then_inc(lam_in, 16)
            for i, name in enumerate(["lambda_q1", "lambda_k1", "lambda_q2", "lambda_k2"]):
                sp.dma_start(lamv[:, i, :], A[name].broadcast_to([P, HD])).then_inc(lam_in, 16)
            sp.dma_start(g_sub[:, :], A["subln_g"].broadcast_to([P, VD])).then_inc(lam_in, 16)
            sp.dma_start(w_sp[:, :, :], A["w_spatial"].rearrange("z g p q -> p (z g) q")).then_inc(wsp_in, 16)
            sp.dma_start(w_r[:, :, :], A["w_router"].rearrange("z (k p) e -> p (z k) e", p=P)).then_inc(wr_in, 16)
            sp.dma_start(token[:, :], A["token"]).then_inc(wr_in, 16)

            def load_head(h):
                p = h % 2
                if h >= 2:
                    sp.wait_ge(pv_done, NT * (h - 1))
                c = slice(h * P, h * P + P)
                sp.dma_start(q_h[p][:, :, :], tiles(q_d)[:, :, c]).then_inc(qkv_in[p], 16)
                sp.dma_start(k_h[p][:, 0:NPAST], ck[:, :, h, :]).then_inc(qkv_in[p], 16)
                sp.dma_start(k_h[p][:, NPAST:], tiles(k_d)[:, :, c]).then_inc(qkv_in[p], 16)
                sp.dma_start(v_h[p][:, 0:NPAST], cv[:, :, h, :]).then_inc(qkv_in[p], 16)
                sp.dma_start(v_h[p][:, NPAST:], tiles(v_d)[:, :, c]).then_inc(qkv_in[p], 16)

            def load_gates(h):
                if h >= 2:
                    sp.wait_ge(og_ready, NT * (h - 1))
                sp.dma_start(sa_h[:, h % 2], tiles(sa_d)[:, :, h * P:h * P + P]).then_inc(sa_in[h % 2], 16)

            for n in range(NRAW, PRE + NRAW - 2):
                load(n)
                if n == 2 * BLOCKS.index(("gb", 0)):
                    sp.wait_ge(qk_out[0], 48)
                    sp.wait_ge(qk_out[1], 48)
                    for s in range(NSTAGE):
                        last = max(n for n in range(len(STAGED)) if n % NSTAGE == s and BLOCKS[STAGED[n][0]][0] == "v")
                        sp.wait_ge(stage_out[s], stage_stored(last))
                    sp.wait_ge(sq_free, 4)
                    load_head(0)

            for s in range(NSTAGE):
                last = max(n for n in range(len(STAGED)) if n % NSTAGE == s and stores_of(n))
                sp.wait_ge(stage_out[s], stage_stored(last))
            sp.wait_ge(grow_out[0], 32)
            sp.wait_ge(grow_out[1], 32)
            sp.wait_ge(conv_ready, 12)
            sp.wait_ge(piece_done, len(PIECES))
            sp.wait_ge(stage_mul, multiplied(len(STAGED) - 1))
            load_gates(0)
            load_head(1)
            load_gates(1)
            load(PRE + NRAW - 2)
            load(PRE + NRAW - 1)
            for h in range(2, H):
                load_head(h)
                load_gates(h)
            sp.wait_ge(pv_done, NU)
            for i in range(2):
                sp.dma_start(gate1[:, i, :], gate_d[i, 0:1, :].broadcast_to([P, D])).then_inc(gate1_in, 16)
            for t in range(NT):
                sp.wait_ge(merged, t + 1)
                sp.dma_start(x2[:, t, :], x_l[:, t, :] if t < NL else x_c[:, 0, :]).then_inc(x2_in[t], 16)
            for t in range(NT):
                sp.wait_ge(x2_ready, t + 1)
                sp.dma_start(x2_d[t * P:(t + 1) * P, :], x2[:, t, :]).then_inc(x2_out, 16)
            sp.wait_ge(idx_ready, 1)
            sp.dma_start(idx_d, idx_f[:, :]).then_inc(idx_out, 16)
            sp.wait_ge(idx_out, 16)
            sp.dma_start(idx_b[:, :, :].rearrange("p e c -> p (e c)"),
                         idx_d.rearrange("e c -> (e c)").unsqueeze(0).broadcast_to([P, E * CAP])).then_inc(idxb_in, 16)
            sp.dma_start(tokens[:, :], A["tokens"]).then_inc(tok_in, 16)

            def expert_loads(e, last):
                for i in range(EC):
                    j = i + NRAWE
                    if j >= EC and last:
                        continue
                    if isinstance(e, int) and e == 0 and i == NRAW:
                        sp.wait_ge(p2_done, N_P2)
                        sp.wait_ge(x2_out, 16 * NT)
                        sp.dma_start(yacc[:, :, :], tiles(x2_d)).then_inc(yacc_in, 16)
                        sp.dma_start(gate2[0:CAP_L, :], gate_d[0, 1:2, :].broadcast_to([CAP_L, D])).then_inc(gate2_in, 16)
                        sp.dma_start(gate2[CAP_L:CAP, :], gate_d[1, 1:2, :].broadcast_to([CAP_C, D])).then_inc(gate2_in, 16)
                    slot = EXPERT_SLOT[j % NRAWE]
                    src = expert_source(e, j) if j < EC else expert_source(e + 1, j - EC)
                    if not isinstance(e, int):
                        sp.lower_val(src.offset * 4)
                    sp.wait_ge(lo_done, e * EC + (PRE + i + 1))
                    sp.dma_start(raw_slot(slot), src).then_inc(raw_in[slot], 16)

            sp.wait_ge(p2_done, P2.index(("T", 2, 1)) + 1)
            sp.wait_ge(x2_sq, NT)
            sp.dma_start(raw_x[:, :, :], expert_source(0, NRAW)).then_inc(raw_in[NRAW], 16)
            expert_loads(0, False)
            with sp.Fori(1, E - 1) as e:
                expert_loads(e, False)
            expert_loads(E - 1, True)

            for n in range(2 * NT):
                t, c = SC_PIECES[n] // 2, slice(SC_PIECES[n] % 2 * CW, (SC_PIECES[n] % 2 + 1) * CW)
                sp.wait_ge(out_added, (E - 1) * 2 * NT + n + 1)
                out = y_l[:, t, c] if t < NL else y_c[:, 0, c]
                sp.dma_start(out, yacc[:, t, c]).then_inc(y_out, 16)
            sp.wait_ge(y_out, 16 * 2 * NT)

        @block.scalar
        def _(act):
            def hi(n):
                act.wait_ge(raw_in[n % NRAW], raw_count(n))
                slot = split_slot(n) if n < PRE else (n - PRE) % NSPLIT
                before = split_before(n) if n < PRE else PRE - NSPLIT + n - PRE
                if before is not None:
                    wait_read(act, before)
                nc.scalar.activation(w_hi[:, slot], raw[:, n % NRAW], ACT.Copy).then_inc(hi_done, 1)

            def ahead(b):
                hi(2 * b + 2)
                hi(2 * b + 3)

            def take_root(n, width, c=0):
                act.wait_ge(var_ready, n + 1)
                nc.scalar.activation(root[:, c:c + width], var[:, c:c + width], ACT.Sqrt).then_inc(root_done, 1)

            act.wait_ge(cols_ready, 1)
            nc.scalar.activation(silu_c[:, :, :].rearrange("p a k -> p (a k)"), cols[:, 0:16], ACT.Silu).then_inc(silu_ready, 1)
            hi(0)
            hi(1)
            act.wait_ge(x_load, 32)
            for t in range(NT):
                if t >= 1:
                    act.wait_ge(ssum_ready, t)
                nc.scalar.activation(x_junk[:, :], x_in[:, t, :], ACT.Square, accum_out=newton[:, t:t + 1]).then_inc(ssum_ready, 1)
            take_root(0, NT)

            roots = [1]
            qk_pending = []
            for b in range(FIRST_WO):
                kind, j = BLOCKS[b]
                if not amid(b):
                    ahead(b)
                if b == 4:
                    act.wait_ge(lam_sums, 1)
                    nc.scalar.activation(lam[:, 2:4], lam[:, 0:2], ACT.Exp).then_inc(lam_exps, 1)
                if qk_pending:
                    take_root(roots[0], 8 * NT)
                    roots[0] += 1
                    qk_pending.clear()
                if kind == "ga" and j == 0:
                    take_root(roots[0], NT)
                    roots[0] += 1
                if kind == "ada":
                    act.wait_ge(ada_done, j + 1)
                    if j >= 2:
                        act.wait_ge(conv_done, j - 1)
                    nc.scalar.activation(m4[:, j % 2, :], bank(6)[0:4, :], ACT.Copy).then_inc(m4_ready, 1)
                    if j == 3:
                        for p in range(2 * NT):
                            act.wait_ge(piece_out_dve, p + 1)
                            src = stage[:, p % NSTAGE, :]
                            if p < KT:
                                out = h_hi[:, p, 0:LAT]
                            else:
                                k0 = 4 * (p - KT)
                                out = h_hi[:, k0:k0 + 4, LAT:TOK]
                                src = src.rearrange("p (k t) -> p k t", k=4)
                            nc.scalar.activation(out, src, ACT.Copy).then_inc(h_hi_ready, 1)
                    continue
                for t in range(NT):
                    n = PIECE_AT[b, t]
                    act.wait_ge(piece_done, n + 1)
                    ps = bank(n % RING)
                    if kind in ("q", "k"):
                        i = {"k": 0, "q": 2}[kind] + j
                        if t == 0 and i >= 2:
                            act.wait_ge(qk_out[i % 2], 32)
                        if t == 0 and i >= 1:
                            act.wait_ge(sq_free, i)
                        swapped = qk_swp[i % 2][:, t, :].rearrange("p (a s c) -> p a s c", s=2, c=HD // 4)[:, :, ::-1, :]
                        nc.scalar.activation(qk_raw[i % 2][:, t, :], ps, ACT.Copy)
                        nc.scalar.activation(swapped, ps.rearrange("p (a s c) -> p a s c", s=2, c=HD // 4), ACT.Copy)
                        nc.scalar.activation(qk_sq[:, t, :], ps, ACT.Square).then_inc(piece_out_act, 1)
                        qk_pending.append(1)
                    elif kind == "zv":
                        if t == 0 and j == 0:
                            act.wait_ge(qk_out[0], 48)
                            act.wait_ge(qk_out[1], 48)
                        nc.scalar.activation(ob[:, t, j * CW:(j + 1) * CW], ps, ACT.Gelu_apprx_tanh).then_inc(piece_out_act, 1)
                    else:
                        s = STAGE_AT[b, t]
                        if s >= NSTAGE:
                            m = s - NSTAGE
                            if stores_of(m):
                                act.wait_ge(stage_out[m % NSTAGE], stage_stored(m))
                            else:
                                act.wait_ge(stage_mul, multiplied(m))
                        func = {"v": ACT.Copy, "ga": ACT.Sigmoid, "gb": ACT.Sigmoid, "zu": ACT.Gelu_apprx_tanh}[kind]
                        nc.scalar.activation(stage[:, s % NSTAGE, :], ps, func).then_inc(piece_out_act, 1)
                    if t == AMID_TILE and amid(b + 1):
                        ahead(b + 1)

            seen = [0]

            def copy_out(want):
                while seen[0] < want:
                    n = seen[0]
                    what, which, first, k = TRANSPOSED[n]
                    act.wait_ge(tr_done, n + 1)
                    ps = bank(4 + n % 2)
                    if what == "a":
                        if which >= 2 and first == 0:
                            act.wait_ge(pv_done, which - 1)
                        out = aT[:, which % 2, first * P:(first + k) * P]
                        nc.scalar.activation(out, ps[:, 0:k * P], ACT.Copy).then_inc(tr_emptied["a"], 1)
                    else:
                        for out, _, src in qk_parts(which, first, ps):
                            last = nc.scalar.activation(out, src, ACT.Copy)
                        last.then_inc(qk_hi, 1)
                    seen[0] += 1

            def output(u):
                act.wait_ge(pv_done, u + 1)
                if u == 0:
                    act.wait_ge(root_done, roots[0])
                h, t = u // NT, u % NT
                ps, scale = bank(6 + u % 2)[:, 0:P], rinv[:, u % NR, 0:1]
                nc.scalar.activation(o_t[:, t, h * P:(h + 1) * P], ps, ACT.Copy, scale=scale).then_inc(o_ready, 1)
                nc.scalar.activation(sq_junk[:, u % 2, :], ps, ACT.Square, scale=scale,
                                     accum_out=var[:, t * H + h:t * H + h + 1]).then_inc(osq_ready, 1)

            copy_out(transposed_upto("qk", 0))
            for u in range(NU):
                if u == 1:
                    ahead(FIRST_WO)
                nk = unit_keys(u)[1] * P
                for s in range(2):
                    act.wait_ge(max_done[s], u + 1)
                    if u >= NP and s == 0:
                        act.wait_ge(tr_done, transposed_upto("a", u - NP))
                    out = (p_0, p_1)[s][:, u % NP, 0:nk]
                    nc.scalar.activation(out, bank_all[:, 2 * s:2 * s + 2, :].rearrange("p a n -> p (a n)")[:, 0:nk], ACT.Exp,
                                         bias=nbias[:, u % 2, s:s + 1], scale=HD ** -0.5,
                                         accum_out=rsum[:, u % NP, s:s + 1]).then_inc(exp_done[s], 1)
                if before_head(u, 1):
                    copy_out(transposed_upto("qk", u // NT + 1))
                if u >= 2:
                    copy_out(transposed_upto("a", u - 2))
                if u >= 4:
                    output(u - 4)
                if before_head(u, 2):
                    copy_out(qk_upto(u // NT + 1, EARLY_QK))
            copy_out(len(TRANSPOSED))
            for u in range(NU - 4, NU):
                output(u)

            take_root(roots[0], H * NT)
            roots[0] += 1
            for what, t, *half in STEPS:
                if what == "T":
                    for half in range(2):
                        n = P2.index(("T", t, half))
                        act.wait_ge(p2_done, n + 1)
                        nc.scalar.activation(m_hi[:, t, 4 * half:4 * half + 4, :], bank(n % RING).rearrange("p (k t) -> p k t", k=4),
                                             ACT.Copy).then_inc(mhi_ready, 1)
                elif what == "N":
                    act.wait_ge(x2_ready, t + 1)
                    if t == 0:
                        act.wait_ge(p2_done, P2.index(("T", 1, 1)) + 1)
                    nc.scalar.activation(p_sq[:, :], x2[:, t, :], ACT.Square, accum_out=newton[:, 8 + t:9 + t]).then_inc(x2_sq, 1)
                    take_root(roots[0], 1, t)
                    roots[0] += 1
                    act.wait_ge(xn2_ready, t + 1)
                    nc.scalar.activation(xn_hi[:, t, :], xn[t % 2][:, :], ACT.Copy).then_inc(xnhi_ready, 1)
                elif what == "A":
                    for t in GROUP[t]:
                        act.wait_ge(lgb_ready, t + 1)
                        nc.scalar.activation(lg[:, t, :], lg[:, t, :], ACT.Exp, bias=rst[:, t, 0:1], scale=1.0,
                                             accum_out=rst[:, t, 1:2]).then_inc(lge_ready, 1)
            for i in range(NRAW):
                hi(PRE + i)

            act.wait_ge(p2_emptied, N_P2)

            def output_hi(e, half):
                act.wait_ge(yeg_ready, e * 2 + (half + 1))
                c = slice(half * CW, (half + 1) * CW)
                nc.scalar.activation(ye_hi[:, c], yeg[:, c], ACT.Copy).then_inc(yeh_ready, 1)

            def expert(e, first, last):
                for i in range(EC):
                    j = i + AHEAD
                    if i == 1 and not first:
                        output_hi(e - 1, 1)
                    fb = SG_STEP.get(i)
                    if fb is not None:
                        act.wait_ge(chunk_read, e * EC + i)
                        if not first or fb >= 2:
                            act.wait_ge(hid_ready, e * 4 + (fb - 1))
                        nc.scalar.activation(sg[:, fb % 2, :], bank(fb % 2 * 2)[0:CAP, :], ACT.Silu).then_inc(sg_ready, 1)
                    fb = HTO_STEP.get(i)
                    if fb is not None:
                        act.wait_ge(ht_done, e * 4 + (fb + 1))
                        nc.scalar.activation(hT_hi[:, 4 * fb:4 * fb + 4, :], bank(6)[:, 0:4 * CAP].rearrange("p (k c) -> p k c", k=4),
                                             ACT.Copy).then_inc(hth_ready, 1)
                    if i == YE_STEP + 1:
                        output_hi(e, 0)
                    if not (last and j >= EC):
                        slot = EXPERT_SLOT[j % NRAWE]
                        act.wait_ge(raw_in[slot], e * (16 * EC // NRAWE) + 16 * (RAW_BEFORE[slot] + j // NRAWE + 1))
                        if first and j < NSPLIT:
                            wait_read(act, PRE + j - NSPLIT)
                        else:
                            act.wait_ge(chunk_read, e * EC + (j - NSPLIT + 1))
                        nc.scalar.activation(w_hi[:, j % NSPLIT], raw_slot(slot), ACT.Copy).then_inc(hi_done, 1)

            expert(0, True, False)
            with act.Fori(1, E - 1) as e:
                expert(e, False, False)
            expert(E - 1, False, True)
            output_hi(E - 1, 1)

        @block.vector
        def _(dve):
            chain = [0]

            def link(ins):
                chain[0] += 1
                ins.then_inc(dve_self, 1)
                dve.wait_ge(dve_self, chain[0])

            def lo(n):
                dve.wait_ge(hi_done, n + 1)
                slot = split_slot(n) if n < PRE else (n - PRE) % NSPLIT
                nc.vector.tensor_tensor(w_lo[:, slot], raw[:, n % NRAW], w_hi[:, slot], ALU.subtract).then_inc(lo_done, 1)

            def ahead(b):
                lo(2 * b + 2)
                lo(2 * b + 3)

            rooted = [0]

            def ask_root(ins):
                ins.then_inc(var_ready, 1)

            def finish_root(width, signal=None, c=0):
                rooted[0] += 1
                dve.wait_ge(root_done, rooted[0])
                r, t, v = rstd[:, c:c + width], newton[:, c:c + width], var[:, c:c + width]
                link(nc.vector.reciprocal(r, root[:, c:c + width]))
                link(nc.vector.tensor_tensor(t, r, r, ALU.mult))
                link(nc.vector.tensor_tensor(t, t, v, ALU.mult))
                link(nc.vector.tensor_scalar(t, t, -0.5, 1.5, ALU.mult, ALU.add))
                last = nc.vector.tensor_tensor(r, r, t, ALU.mult)
                if signal is None:
                    link(last)
                else:
                    last.then_inc(signal[0], 1)
                    dve.wait_ge(*signal)

            dve.wait_ge(rowsT_done, 1)
            nc.vector.tensor_copy(cols[:, :], bank(7)[:, 0:40]).then_inc(cols_ready, 1)
            dve.wait_ge(silu_ready, 1)
            sc = silu_c[:, :, :].rearrange("p a k -> p k a")
            link(nc.vector.tensor_copy(cond[:, :, 0:2], sc))
            nc.vector.tensor_tensor(cond[:, :, 2:4], sc, cond[:, :, 0:2], ALU.subtract).then_inc(cond_ready, 1)
            lo(0)
            lo(1)
            dve.wait_ge(ssum_ready, NT)
            ask_root(nc.vector.tensor_scalar(var[:, 0:NT], newton[:, 0:NT], 1.0 / D, EPS, ALU.mult, ALU.add))
            dve.wait_ge(var_ready, 1)
            finish_root(NT)
            for t in range(NT):
                nc.vector.tensor_scalar(x_in[:, t, :], x_in[:, t, :], rstd[:, t:t + 1], None, ALU.mult).then_inc(xn_ready, 1)
            def conv(a):
                dve.wait_ge(conv_done, a + 1)
                if a in GATES:
                    g = GATES.index(a)
                    if g >= 2:
                        dve.wait_ge(grow_out[g % 2], 16)
                    nc.vector.tensor_copy(grow[:, g % 2, :], bank(7)[0:2, :]).then_inc(conv_ready, 1)
                else:
                    nc.vector.tensor_copy(mcol[:, VEC[a], 4 * (a % 2):4 * (a % 2) + 4, :].rearrange("p k c -> p (k c)"),
                                          bank(7)[:, 0:8]).then_inc(conv_ready, 1)
                dve.wait_ge(conv_ready, a + 1)

            def amplitude(out, vec, first):
                g = cols[:, first:first + KT].unsqueeze(2).broadcast_to([P, KT, 2])
                link(nc.vector.scalar_tensor_tensor(out=out[:, :, :], in0=mcol[:, vec, :, :], scalar=1.0, in1=g,
                                                    op0=ALU.add, op1=ALU.mult))

            def modulated(out, ps, k, n, amp, shift):
                v = ps.rearrange("p (k t) -> p k t", k=n)
                o = out.rearrange("p (k t) -> p k t", k=n)
                link(nc.vector.tensor_tensor(o, v, amp.unsqueeze(2).broadcast_to([P, n, P]), ALU.mult))
                return nc.vector.tensor_tensor(o, o, shift.unsqueeze(2).broadcast_to([P, n, P]), ALU.add)

            pending = []
            i_qk = [0]

            def qk_first():
                n = pending[0]
                dve.wait_ge(piece_out_act, emptied_before(PIECE_AT[n, NT - 1] + 1, "act"))
                nc.vector.tensor_reduce(var[:, 0:8 * NT], qk_sq[:, :, :].rearrange("p t (s d) -> p (t s) d", d=HD), axis=AX.X,
                                        op=ALU.add).then_inc(sq_free, 1)
                dve.wait_ge(sq_free, i_qk[0] + 1)
                nc.vector.tensor_scalar(var[:, 0:8 * NT], var[:, 0:8 * NT], 1.0 / HD, EPS, ALU.mult, ALU.add).then_inc(var_ready, 1)

            def qk_rest():
                i = i_qk[0]
                dve.wait_ge(var_ready, rooted[0] + 1)
                finish_root(8 * NT, (rstd_ready, i + 1))
                v = qk_raw[i % 2][:, :, :].rearrange("p t (s d) -> p (t s) d", d=HD)
                link(nc.vector.tensor_tensor(v, v, rstd[:, 0:8 * NT].unsqueeze(2).broadcast_to([P, 8 * NT, HD]), ALU.mult))
                c = tab[:, 1 if i < 2 else 0, 0]
                for t in range(NT):
                    w = qk_raw[i % 2][:, t, :].rearrange("p (s d) -> p s d", d=HD)
                    last = nc.vector.tensor_tensor(w, w, c[:, t, :].unsqueeze(1).broadcast_to([P, 8, HD]), ALU.mult)
                link(last)
                dve.wait_ge(swp_ready, i + 1)
                nc.vector.tensor_tensor(qk_raw[i % 2][:, :, :], qk_raw[i % 2][:, :, :], qk_swp[i % 2][:, :, :], ALU.add).then_inc(qk_ready, 1)
                i_qk[0] += 1
                pending.clear()

            for b in range(FIRST_WO):
                kind, j = BLOCKS[b]
                if pending:
                    qk_first()
                if not amid(b):
                    ahead(b)
                if pending:
                    qk_rest()
                if kind == "ada" and b < 4:
                    if j >= 1:
                        conv(j - 1)
                    if j == 3:
                        conv(3)
                        amplitude(amp1, 1, 16)
                        for p in range(2 * NT):
                            dve.wait_ge(piece_done, p + 1)
                            if p >= NSTAGE:
                                dve.wait_ge(h_ready, p - NSTAGE + 1)
                            if p < KT:
                                last = nc.vector.tensor_scalar(stage[:, p % NSTAGE, :], bank(p % RING), amp1[:, p, 0:1], mcol[:, 0, p, 0:1],
                                                               ALU.mult, ALU.add)
                            else:
                                k0 = 4 * (p - KT)
                                last = modulated(stage[:, p % NSTAGE, :], bank(p % RING), k0, 4, amp1[:, k0:k0 + 4, 1], mcol[:, 0, k0:k0 + 4, 1])
                            last.then_inc(piece_out_dve, 1)
                        dve.wait_ge(lam_in, 16 * 9)
                        for i in range(2):
                            link(nc.vector.tensor_tensor(lamv[:, 2 * i, :], lamv[:, 2 * i, :], lamv[:, 2 * i + 1, :], ALU.mult))
                        nc.vector.tensor_reduce(lam[:, 0:2], lamv[:, :, :].rearrange("p (a b) d -> p a b d", b=2)[:, :, 0, :], axis=AX.X,
                                                op=ALU.add).then_inc(lam_sums, 1)
                        for i in range(2):
                            dve.wait_ge(wspT_done, i + 1)
                            nc.vector.tensor_copy(wspT[:, 4 * i:4 * i + 4, :].rearrange("p g q -> p (g q)"), bank(6)[:, :]).then_inc(wspT_ready, 1)
                    continue
                if b == 4:
                    for i in range(2):
                        for c in range(2):
                            g = gain[:, i, :].rearrange("p (a s c) -> p a s c", s=2, c=HD // 4)
                            g = g[:, :, ::-1, :] if c else g
                            for t in range(NT):
                                v = tab[:, i, c, t, :].rearrange("p (a s c) -> p a s c", s=2, c=HD // 4)
                                nc.vector.tensor_tensor(v, v, g, ALU.mult)
                    nc.vector.tensor_scalar(g_sub[:, :], g_sub[:, :], 1.0 - LAMBDA_INIT, None, ALU.mult).then_inc(tab_ready, 1)
                    dve.wait_ge(tab_ready, 1)
                if b == 5:
                    dve.wait_ge(lam_exps, 1)
                    link(nc.vector.tensor_tensor(lam[:, 4:5], lam[:, 2:3], lam[:, 3:4], ALU.subtract))
                    link(nc.vector.tensor_scalar(lam[:, 5:6], lam[:, 4:5], -1.0, -LAMBDA_INIT, ALU.mult, ALU.add))
                if kind in ("q", "k"):
                    pending.append(b)
                if kind == "ga" and j == 0:
                    for t in range(NT):
                        last = nc.vector.bn_aggr(mv[:, t, :], bstat[:, t, :, :].rearrange("p a s -> p (a s)"))
                    link(last)
                    nc.vector.tensor_scalar(var[:, 0:NT], mv[:, :, 1], EPS, None, ALU.add).then_inc(var_ready, 1)
                    dve.wait_ge(var_ready, rooted[0] + 1)
                    finish_root(NT)
                    dve.wait_ge(ln_in, 32)
                    for t in range(NT):
                        link(nc.vector.tensor_scalar(ob[:, t, :], ob[:, t, :], mv[:, t, 0:1], rstd[:, t:t + 1], ALU.subtract, ALU.mult))
                        nc.vector.tensor_tensor(ob[:, t, :], ob[:, t, :], ln_g[:, :], ALU.mult).then_inc(zn_pre, 1)
                for t in range(NT):
                    if kind == "zv":
                        n = PIECE_AT[b, t]
                        dve.wait_ge(piece_out_act, emptied_before(n + 1, "act"))
                        last = nc.vector.bn_stats(bstat[:, t, j, :], ob[:, t, j * CW:(j + 1) * CW])
                        if t == NT - 1:
                            link(last)
                    if kind in ("zu", "gb"):
                        s = STAGE_AT[b, t]
                        dve.wait_ge(piece_out_act, emptied_before(PIECE_AT[b, t] + 1, "act"))
                        if kind == "gb":
                            dve.wait_ge(stage_mul, multiplied(STAGE_AT[BLOCKS.index(("zu", j)), t]))
                        w = ob[:, t, j * CW:(j + 1) * CW]
                        nc.vector.tensor_tensor(w, w, stage[:, s % NSTAGE, :], ALU.mult).then_inc(stage_mul, 1)
                    if t == 0 and b > 4 and BLOCKS[b - 1][0] == "ada":
                        conv(BLOCKS[b - 1][1])
                    if t == AMID_TILE and amid(b + 1):
                        ahead(b + 1)
                if b == SPATIAL_AFTER:
                    for i in range(2 * NT):
                        t, half = i // 2, i % 2
                        n = PIECE_AT["sp", i]
                        dve.wait_ge(piece_done, n + 1)
                        w = ob[:, t, half * CW:(half + 1) * CW].rearrange("p (g c) -> p g c", c=P)
                        bias = cols[:, 32 + 4 * half:36 + 4 * half].unsqueeze(2).broadcast_to([P, 4, P])
                        nc.vector.tensor_tensor(w, bank(n % RING).rearrange("p (g c) -> p g c", c=P), bias, ALU.add).then_inc(piece_out_dve, 1)
                    dve.wait_ge(piece_out_dve, emptied_before(PIECE_AT["sp", 2 * NT - 1] + 1, "dve"))
            amplitude(amp2, 3, 24)

            def combine(u):
                p, nk = u % NP, unit_keys(u)[1] * P
                rin = rinv[:, u % NR, :]
                dve.wait_ge(exp_done[0], u + 1)
                dve.wait_ge(exp_done[1], u + 1)
                link(nc.vector.reciprocal(rin, rsum[:, p, :]))
                link(nc.vector.scalar_tensor_tensor(out=rin[:, 1:2], in0=rsum[:, p, 0:1], scalar=lam[:, 5:6], in1=rin[:, 1:2],
                                                    op0=ALU.mult, op1=ALU.mult))
                nc.vector.scalar_tensor_tensor(out=p_0[:, p, 0:nk], in0=p_1[:, p, 0:nk], scalar=rin[:, 1:2], in1=p_0[:, p, 0:nk],
                                               op0=ALU.mult, op1=ALU.add).then_inc(a_done, 1)

            def qk_low(h, first, last):
                for i in range(first, last):
                    n = qk_upto(h, i + 1) - 1
                    dve.wait_ge(qk_hi, of_kind(n + 1, "qk"))
                    for hi, out, src in qk_parts(h, 4 * i, bank(4 + n % 2)):
                        last = nc.vector.tensor_tensor(out, src, hi, ALU.subtract)
                    last.then_inc(tr_emptied["qk"], 1)

            for i in range(2):
                dve.wait_ge(grow_out[i], 32)
            for s in range(NSTAGE):
                last = max(n for n in range(len(STAGED)) if n % NSTAGE == s and stores_of(n))
                dve.wait_ge(stage_out[s], stage_stored(last))
            qk_low(0, 0, 3)
            for u in range(NU):
                nk = unit_keys(u)[1] * P
                for s in range(2):
                    dve.wait_ge(sc_done[s], u + 1)
                    nb = nbias[:, u % 2, s:s + 1]
                    src = bank_all[:, 2 * s:2 * s + 2, :].rearrange("p a n -> p (a n)")[:, 0:nk]
                    link(nc.vector.tensor_reduce(nb, src, axis=AX.X, op=ALU.max))
                    nc.vector.tensor_scalar(nb, nb, -HD ** -0.5, None, ALU.mult).then_inc(max_done[s], 1)
                if before_head(u, 1):
                    qk_low(u // NT + 1, EARLY_QK, 3)
                if u >= 1:
                    combine(u - 1)
                if before_head(u, 2):
                    qk_low(u // NT + 1, 0, EARLY_QK)
                if u == 1:
                    ahead(FIRST_WO)
            combine(NU - 1)
            dve.wait_ge(og_ready, NU)

            dve.wait_ge(osq_ready, NU)
            nc.vector.tensor_scalar(var[:, 0:H * NT], var[:, 0:H * NT], 1.0 / VD, EPS, ALU.mult, ALU.add).then_inc(var_ready, 1)
            dve.wait_ge(var_ready, rooted[0] + 1)
            finish_root(H * NT)
            n2 = [0]

            def next_piece():
                n2[0] += 1
                dve.wait_ge(p2_done, n2[0])
                return bank((n2[0] - 1) % RING)

            for what, t, *half in STEPS:
                if what == "M":
                    for h in range(H):
                        c = slice(h * VD, (h + 1) * VD)
                        last = nc.vector.scalar_tensor_tensor(out=o_t[:, t, c], in0=o_t[:, t, c], scalar=rstd[:, t * H + h:t * H + h + 1],
                                                              in1=ob[:, t, c], op0=ALU.mult, op1=ALU.add)
                    last.then_inc(merged, 1)
                elif what == "T":
                    for half in range(2):
                        ps = next_piece()
                        dve.wait_ge(mhi_ready, 2 * t + half + 1)
                        c = slice(4 * half, 4 * half + 4)
                        nc.vector.tensor_tensor(m_lo[:, t, c, :], ps.rearrange("p (k t) -> p k t", k=4), m_hi[:, t, c, :],
                                                ALU.subtract).then_inc(p2_emptied, 1)
                elif what == "W":
                    half = half[0]
                    if t == 0 and half == 0:
                        dve.wait_ge(gate1_in, 32)
                    dve.wait_ge(x2_in[t], 16)
                    ps = next_piece()
                    c = slice(half * CW, (half + 1) * CW)
                    nc.vector.tensor_tensor(xw[:, c], ps, gate1[:, int(t == NL), c], ALU.mult).then_inc(p2_emptied, 1)
                    dve.wait_ge(p2_emptied, n2[0])
                    last = nc.vector.tensor_tensor(x2[:, t, c], x2[:, t, c], xw[:, c], ALU.add)
                    if half == 1:
                        last.then_inc(x2_ready, 1)
                elif what == "N":
                    dve.wait_ge(x2_sq, t + 1)
                    nc.vector.tensor_scalar(var[:, t:t + 1], newton[:, 8 + t:9 + t], 1.0 / D, EPS, ALU.mult, ALU.add).then_inc(var_ready, 1)
                elif what == "R":
                    dve.wait_ge(var_ready, rooted[0] + 1)
                    finish_root(1, c=t)
                    if t >= 2:
                        dve.wait_ge(p2_done, P2.index(("X", t - 2, 1)) + 1)
                        dve.wait_ge(xnlo_ready, t - 1)
                    nc.vector.tensor_scalar(xn[t % 2][:, :], x2[:, t, :], rstd[:, t:t + 1], None, ALU.mult).then_inc(xn2_ready, 1)
                elif what == "X":
                    if t == 0:
                        dve.wait_ge(wr_in, 32)
                    if t >= 2:
                        dve.wait_ge(p2_done, P2.index(("L", t - 2, 0)) + 1)
                    cd = int(t == NL)
                    for half in range(2):
                        ps = next_piece()
                        k = 4 * half
                        for i in range(4):
                            last = nc.vector.tensor_scalar(h2T[t % 2][:, k + i, :], ps[:, i * P:(i + 1) * P], amp2[:, k + i, cd:cd + 1],
                                                           mcol[:, 2, k + i, cd:cd + 1], ALU.mult, ALU.add)
                        last.then_inc(p2_emptied, 1)
                elif what == "L":
                    nc.vector.tensor_copy(lg[:, t, :], next_piece()[:, 0:E]).then_inc(p2_emptied, 1)
                    dve.wait_ge(p2_emptied, n2[0])
                    link(nc.vector.tensor_reduce(rst[:, t, 2:3], lg[:, t, :], axis=AX.X, op=ALU.max))
                    nc.vector.tensor_scalar(rst[:, t, 0:1], rst[:, t, 2:3], -1.0, None, ALU.mult).then_inc(lgb_ready, 1)
                elif what == "A":
                    group = GROUP[t]
                    g, n = slice(group[0], group[-1] + 1), len(group)
                    dve.wait_ge(lge_ready, group[-1] + 1)
                    link(nc.vector.reciprocal(rst[:, g, 3:4], rst[:, g, 1:2]))
                    nc.vector.tensor_tensor(lg[:, g, :], lg[:, g, :], rst[:, g, 3:4].broadcast_to([P, n, E]), ALU.mult).then_inc(aff_ready, 1)
                    nc.vector.tensor_copy(affT[:, group[0] * P:(group[-1] + 1) * P], next_piece()[0:E, 0:n * P]).then_inc(p2_emptied, 1)
                    dve.wait_ge(p2_emptied, n2[0])
                elif what == "K":
                    start, width, rounds, off, rnd = (0, LAT, CAP_L // 8, 0, t) if t < CAP_L // 8 else \
                        (LAT, CTX, CAP_C // 8, CAP_L, t - CAP_L // 8)
                    bufs = [affT, affW]
                    v = gate_v[:, off + 8 * rnd:off + 8 * rnd + 8]
                    src, dst = bufs[rnd % 2][:, start:start + width], bufs[(rnd + 1) % 2][:, start:start + width]
                    link(nc.vector.max(v, src))
                    found = nc.vector.max_index(idx_u[:, off + 8 * rnd:off + 8 * rnd + 8], v, src)
                    if rnd < rounds - 1:
                        link(nc.vector.match_replace(dst, v, src, -1.0))
                    else:
                        link(found)
            link(nc.vector.tensor_copy(idx_f[:, :], idx_u[:, :]))
            nc.vector.tensor_scalar(idx_f[:, CAP_L:CAP], idx_f[:, CAP_L:CAP], float(LAT), None, ALU.add).then_inc(idx_ready, 1)
            for i in range(NRAW - 1):
                lo(PRE + i)
            for dst in (idx_c, gate_c):
                n = n2[0]
                dve.wait_ge(p2_done, n + 1)
                nc.vector.tensor_copy(dst[:, :], bank(n % RING)[0:CAP, 0:E]).then_inc(p2_emptied, 1)
                n2[0] += 1
            dve.wait_ge(p2_emptied, n2[0])
            dve.wait_ge(idxb_in, 16)
            dve.wait_ge(x2_out, 16 * NT)
            dve.wait_ge(xnlo_ready, NT)
            for t in range(NL):
                nc.vector.tensor_scalar(sel_l[:, t, :, :], idx_b[:, :, 0:CAP_L], token[:, t:t + 1], None, ALU.is_equal).then_inc(sel_ready, 1)
            nc.vector.tensor_scalar(sel_c[:, :, :], idx_b[:, :, CAP_L:CAP], token[:, NL:NT], None, ALU.is_equal).then_inc(sel_ready, 1)
            lo(PRE + NRAW - 1)
            xe4 = xeT[:, :, :].rearrange("p e (k c) -> p e k c", k=KT)
            for k in range(KT):
                for part in range(3):
                    n = n2[0]
                    dve.wait_ge(p2_done, n + 1)
                    if part < 2:
                        out, src, cd = xe4[:, 8 * part:8 * part + 8, k, 0:CAP_L], bank(n % RING).rearrange("p (e c) -> p e c", c=CAP_L), 0
                    else:
                        out, src, cd = xe4[:, :, k, CAP_L:CAP], bank(n % RING)[:, 0:E * CAP_C].rearrange("p (e c) -> p e c", c=CAP_C), 1
                    nc.vector.tensor_scalar(out, src, amp2[:, k, cd:cd + 1], mcol[:, 2, k, cd:cd + 1], ALU.mult, ALU.add).then_inc(p2_emptied, 1)
                    n2[0] += 1
            assert n2[0] == N_P2, n2[0]
            dve.wait_ge(p2_emptied, N_P2)
            dve.wait_ge(tok_in, 16)

            link(nc.vector.tensor_scalar(xe_hi[:, :], xeT[:, 0, :], 1.0, None, ALU.mult))
            nc.vector.tensor_tensor(xe_lo[:, :], xeT[:, 0, :], xe_hi[:, :], ALU.subtract).then_inc(xe_ready, 1)

            def col(a, x):
                return a[:, x:x + 1] if isinstance(x, int) else a[:, bass.ds(x, 1)]

            def added(e, n, piece, b):
                dve.wait_ge(out_placed, e * (2 * NT) + (n + 1))
                w = yacc[:, piece // 2, (piece % 2) * CW:(piece % 2 + 1) * CW]
                nc.vector.tensor_tensor(w, w, bank(b)[:, :], ALU.add).then_inc(out_added, 1)

            def gated_output(e, half):
                dve.wait_ge(chunk_read, e * EC + (YE_STEP + 4 * half))
                c = slice(half * CW, (half + 1) * CW)
                nc.vector.tensor_tensor(yeg[:, c], bank(4 + half)[0:CAP, :], gate2[:, c], ALU.mult).then_inc(yeg_ready, 1)

            def output_lo(e, half):
                dve.wait_ge(yeh_ready, e * 2 + (half + 1))
                c = slice(half * CW, (half + 1) * CW)
                nc.vector.tensor_tensor(ye_lo[:, c], yeg[:, c], ye_hi[:, c], ALU.subtract).then_inc(ye_ready, 1)

            def expert(e, first, last):
                for i in range(EC):
                    j = i + AHEAD
                    if i == 0 and not first:
                        gated_output(e - 1, 1)
                    if i == 2 and not first:
                        output_lo(e - 1, 1)
                    fb = HID_STEP.get(i)
                    if fb is not None:
                        dve.wait_ge(sg_ready, e * 4 + (fb + 1))
                        dve.wait_ge(chunk_read, e * EC + 4 * (fb + 1))
                        if not first or fb >= 2:
                            dve.wait_ge(ht_done, e * 4 + (fb - 1))
                        nc.vector.scalar_tensor_tensor(out=hid[:, fb % 2, :], in0=bank(fb % 2 * 2 + 1)[0:CAP, :], scalar=col(gate_c, e),
                                                       in1=sg[:, fb % 2, :], op0=ALU.mult, op1=ALU.mult).then_inc(hid_ready, 1)
                    fb = HTO_STEP.get(i)
                    if fb is not None:
                        dve.wait_ge(hth_ready, e * 4 + (fb + 1))
                        nc.vector.tensor_tensor(hT_lo[:, 4 * fb:4 * fb + 4, :], bank(6)[:, 0:4 * CAP].rearrange("p (k c) -> p k c", k=4),
                                                hT_hi[:, 4 * fb:4 * fb + 4, :], ALU.subtract).then_inc(ht_ready, 1)
                    if i == YE_STEP:
                        if first:
                            dve.wait_ge(gate2_in, 32)
                        gated_output(e, 0)
                    if i == YE_STEP + 2:
                        output_lo(e, 0)
                    if i == XE_STEP and not last:
                        src = xeT[:, e + 1, :] if isinstance(e, int) else xeT[:, bass.ds(e + 1, 1), :].rearrange("p e n -> p (e n)")
                        dve.wait_ge(chunk_read, e * EC + 16)
                        nc.vector.tensor_scalar(xe_hi[:, :], src, 1.0, None, ALU.mult).then_inc(xeh_done, 1)
                        dve.wait_ge(xeh_done, e + 1)
                        nc.vector.tensor_tensor(xe_lo[:, :], src, xe_hi[:, :], ALU.subtract).then_inc(xe_ready, 1)
                    if i == SEL_STEP:
                        nc.vector.tensor_scalar(selT[:, :], tokens[0:CAP, :], col(idx_c, e), None, ALU.is_equal).then_inc(sel_done, 1)
                    if i - 1 in SC_STEPS and not first:
                        added(e - 1, SC_STEPS.index(i - 1), SC_PIECES[SC_STEPS.index(i - 1)], 7)
                    if last and i == END_STEP + 1:
                        for n in range(NT):
                            added(e, n, SC_PIECES[n], END_BANKS[n % len(END_BANKS)])
                    if not (last and j >= EC):
                        dve.wait_ge(hi_done, e * EC + (PRE + j + 1))
                        nc.vector.tensor_tensor(w_lo[:, j % NSPLIT], raw_slot(EXPERT_SLOT[j % NRAWE]), w_hi[:, j % NSPLIT],
                                                ALU.subtract).then_inc(lo_done, 1)

            expert(0, True, False)
            dve.wait_ge(yacc_in, 16)
            with dve.Fori(1, E - 1) as e:
                expert(e, False, False)
            expert(E - 1, False, True)
            gated_output(E - 1, 1)
            output_lo(E - 1, 1)
            for n in range(NT, 2 * NT):
                added(E - 1, n, SC_PIECES[n], END_BANKS[n % len(END_BANKS)])

        @block.gpsimd
        def _(pool):
            for p in range(2 * NT):
                pool.wait_ge(h_hi_ready, p + 1)
                src = stage[:, p % NSTAGE, :]
                if p < KT:
                    h, l = h_hi[:, p, 0:LAT], h_lo[:, p, 0:LAT]
                else:
                    k0 = 4 * (p - KT)
                    h, l = h_hi[:, k0:k0 + 4, LAT:TOK], h_lo[:, k0:k0 + 4, LAT:TOK]
                    src = src.rearrange("p (k t) -> p k t", k=4)
                nc.gpsimd.tensor_tensor(l, src, h, ALU.subtract).then_inc(h_ready, 1)
            def swapped_part(i):
                if i == 0:
                    pool.wait_ge(tab_ready, 1)
                pool.wait_ge(rstd_ready, i + 1)
                w = qk_swp[i % 2]
                v = w[:, :, :].rearrange("p t (s d) -> p (t s) d", d=HD)
                nc.gpsimd.tensor_tensor(v, v, rstd[:, 0:8 * NT].unsqueeze(2).broadcast_to([P, 8 * NT, HD]), ALU.mult).then_inc(pool_self, 1)
                pool.wait_ge(pool_self, i + 1)
                s = tab[:, 1 if i < 2 else 0, 1]
                for t in range(NT):
                    x = w[:, t, :].rearrange("p (s d) -> p s d", d=HD)
                    last = nc.gpsimd.tensor_tensor(x, x, s[:, t, :].unsqueeze(1).broadcast_to([P, 8, HD]), ALU.mult)
                last.then_inc(swp_ready, 1)

            def gate_store(g):
                a = GATES[g]
                pool.wait_ge(conv_ready, a + 1)
                pool.dma_start(gate_d[:, g // 2, (g % 2) * CW:(g % 2 + 1) * CW], grow[:, g % 2, :]).then_inc(grow_out[g % 2], 16)

            def qk_store(which):
                kind, j = which
                i = {"k": 0, "q": 2}[kind] + j
                pool.wait_ge(qk_ready, i + 1)
                c = j * CW
                src = qk_raw[i % 2]
                pool.dma_start(tiles(k_d if kind == "k" else q_d)[:, :, c:c + CW], src[:, :, :]).then_inc(qk_out[i % 2], 16)
                if kind == "k":
                    pool.dma_start(out_k[:, c:c + CW], src[:, NL, :]).then_inc(qk_out[i % 2], 16)

            for b in range(5, FIRST_WO):
                kind, j = BLOCKS[b]
                c = j * CW
                if BLOCKS[b - 1][0] in ("k", "q"):
                    swapped_part({"k": 0, "q": 2}[BLOCKS[b - 1][0]] + BLOCKS[b - 1][1])
                    qk_store(BLOCKS[b - 1])
                if BLOCKS[b - 1][0] == "ada" and BLOCKS[b - 1][1] in GATES:
                    gate_store(GATES.index(BLOCKS[b - 1][1]))
                if (kind, j) == ("v", 1):
                    pool.wait_ge(sq_free, 4)
                    pool.wait_ge(qk_out[0], 48)
                    pool.wait_ge(qk_out[1], 48)
                    pool.dma_start(ln_g[:, :], A["gmlp_ln_g"].broadcast_to([P, D])).then_inc(ln_in, 16)
                    pool.dma_start(ln_b[:, :], A["gmlp_ln_b"].broadcast_to([P, D])).then_inc(ln_in, 16)
                if kind in ("v", "ga"):
                    for t in range(NT):
                        if kind == "ga" and j == 0:
                            pool.wait_ge(zn_pre, t + 1)
                            nc.gpsimd.tensor_tensor(ob[:, t, :], ob[:, t, :], ln_b[:, :], ALU.add).then_inc(zn_ready, 1)
                        n = STAGE_AT[b, t]
                        pool.wait_ge(piece_out_act, emptied_before(PIECE_AT[b, t] + 1, "act"))
                        out = (v_d if kind == "v" else sa_d)[t * P:(t + 1) * P, c:c + CW]
                        pool.dma_start(out, stage[:, n % NSTAGE, :]).then_inc(stage_out[n % NSTAGE], 16)
                        if stores_of(n) == 2:
                            pool.dma_start(out_v[:, c:c + CW], stage[:, n % NSTAGE, :]).then_inc(stage_out[n % NSTAGE], 16)
            def gates(h):
                pool.wait_ge(sa_in[h % 2], 16 * (h // 2 + 1))
                w = sa_h[:, h % 2]
                nc.gpsimd.tensor_tensor(w, w, g_sub[:, :].unsqueeze(1).broadcast_to([P, NT, VD]), ALU.mult).then_inc(sag_ready, 1)

            gates(0)
            for u in range(NU):
                h, t = u // NT, u % NT
                if t == 1 and h + 1 < H:
                    gates(h + 1)
                if t == 0:
                    pool.wait_ge(sag_ready, h + 1)
                pool.wait_ge(o_ready, u + 1)
                w = o_t[:, t, h * P:(h + 1) * P]
                nc.gpsimd.tensor_tensor(w, w, sa_h[:, h % 2, t, :], ALU.mult).then_inc(og_ready, 1)
            for t in range(NT):
                pool.wait_ge(xnhi_ready, t + 1)
                nc.gpsimd.tensor_tensor(xn_lo[:, t, :], xn[t % 2][:, :], xn_hi[:, t, :], ALU.subtract).then_inc(xnlo_ready, 1)

        @block.tensor
        def _(pe):
            def split3(ps, hi, lo, wh, wl, first, last):
                nc.tensor.matmul(ps, hi, wh, start=first, stop=False)
                nc.tensor.matmul(ps, lo, wh, start=False, stop=False)
                return nc.tensor.matmul(ps, hi, wl, start=False, stop=last)

            def piece(n):
                if n >= RING:
                    who = PIECES[n - RING][2]
                    pe.wait_ge(piece_out_act if who == "act" else piece_out_dve, emptied_before(n - RING + 1, who))
                return bank(n % RING)

            def ada(a, b):
                pe.wait_ge(lo_done, 2 * b + 2)
                if a >= 1:
                    pe.wait_ge(m4_ready, a)
                ps = bank(6)[0:4, :]
                for n in (2 * b, 2 * b + 1):
                    for k in range(CK):
                        kk = (n % 2) * CK + k
                        nc.tensor.matmul(ps, cond[:, kk, :], w_hi[:, split_slot(n), k, :], start=(kk == 0), stop=False)
                        last = nc.tensor.matmul(ps, cond[:, kk, :], w_lo[:, split_slot(n), k, :], start=False, stop=(kk == KT - 1))
                last.then_inc(ada_done, 1)

            def conv(a):
                pe.wait_ge(m4_ready, a + 1)
                if a >= 1:
                    pe.wait_ge(conv_ready, a)
                if a in GATES:
                    nc.tensor.matmul(bank(7)[0:2, :], hilo[0:4, :], m4[:, a % 2, :], start=True, stop=False)
                    last = nc.tensor.matmul(bank(7)[0:2, :], pick[0:12, a, :], b12[:, :], start=False, stop=True)
                else:
                    for k in range(4):
                        out = bank(7)[:, 2 * k:2 * k + 2]
                        nc.tensor.matmul(out, m4[:, a % 2, k * P:(k + 1) * P], hilo[0:4, :], start=True, stop=False)
                        last = nc.tensor.matmul(out, b12[:, k * P:(k + 1) * P], pick[0:12, a, :], start=False, stop=True)
                last.then_inc(conv_done, 1)

            def token_pieces(lo_, hi_):
                for p in range(lo_, hi_):
                    ps = piece(p)
                    for i in range(4):
                        t, k = (i, p) if p < KT else (NL, 4 * (p - KT) + i)
                        last = nc.tensor.transpose(ps[:, i * P:(i + 1) * P], x_in[:, t, k * P:(k + 1) * P], ident[:, :])
                    last.then_inc(piece_done, 1)

            pe.wait_ge(rows_in, 96)
            nc.tensor.transpose(bank(7)[:, 0:40], rows40[:, :], ident[0:40, 0:40]).then_inc(rowsT_done, 1)
            pe.wait_ge(const_in, 48)
            pe.wait_ge(cond_ready, 1)
            ada(0, 0)
            pe.wait_ge(xn_ready, NT)
            token_pieces(0, 3)
            ada(1, 1)
            conv(0)
            token_pieces(3, 6)
            ada(2, 2)
            conv(1)
            ada(3, 3)
            conv(2)
            conv(3)
            token_pieces(6, 2 * NT)

            def spatial_transposes(i):
                if i == 0:
                    pe.wait_ge(m4_ready, 4)
                    pe.wait_ge(wsp_in, 16)
                else:
                    pe.wait_ge(wspT_ready, 1)
                for g in range(4):
                    last = nc.tensor.transpose(bank(6)[:, g * P:(g + 1) * P], w_sp[:, 4 * i + g, :], ident[:, :])
                last.then_inc(wspT_done, 1)

            spatial_transposes(0)
            for b in range(4, FIRST_WO):
                kind, j = BLOCKS[b]
                if not amid(b):
                    for t in range(NT):
                        ps = piece(PIECE_AT[b, t])
                        for n in (2 * b, 2 * b + 1):
                            if t == 0:
                                pe.wait_ge(lo_done, n + 1)
                            for k in range(CK):
                                kk = (n % 2) * CK + k
                                if b == 4 and t == 0:
                                    pe.wait_ge(h_ready, kk + 1)
                                if b == 4 and t == NL and kk == 0:
                                    pe.wait_ge(h_ready, 2 * NT)
                                last = split3(ps, h_hi[:, kk, t * P:(t + 1) * P], h_lo[:, kk, t * P:(t + 1) * P],
                                              w_hi[:, split_slot(n), k, :], w_lo[:, split_slot(n), k, :], kk == 0, kk == KT - 1)
                        last.then_inc(piece_done, 1)
                        if b == 4 and t == 0:
                            spatial_transposes(1)
                        if b == 4 and t == 1:
                            pe.wait_ge(wspT_ready, 2)
                        if t == 0 and BLOCKS[b - 1][0] == "ada" and b > 4:
                            conv(BLOCKS[b - 1][1])
                        if t == AMID_TILE and amid(b + 1):
                            ada(BLOCKS[b + 1][1], b + 1)
                if b == SPATIAL_AFTER:
                    for i in range(2 * NT):
                        t, half = i // 2, i % 2
                        pe.wait_ge(zn_ready, t + 1)
                        ps = piece(PIECE_AT["sp", i])
                        for g in range(4):
                            gg = 4 * half + g
                            last = nc.tensor.matmul(ps[:, g * P:(g + 1) * P], wspT[:, gg, :], ob[:, t, gg * P:(gg + 1) * P], start=True, stop=True)
                        last.then_inc(piece_done, 1)

            pe.wait_ge(piece_out_act, emptied_before(len(PIECES), "act"))
            pe.wait_ge(piece_out_dve, emptied_before(len(PIECES), "dve"))
            pe.wait_ge(conv_ready, 12)
            done = [0]

            def transposes(want):
                while done[0] < want:
                    n = done[0]
                    what, which, first, k = TRANSPOSED[n]
                    if n >= 2:
                        before = TRANSPOSED[n - 2][0]
                        pe.wait_ge(tr_emptied[before], of_kind(n - 1, before))
                    if what == "a":
                        pe.wait_ge(a_done, which + 1)
                    elif first == 0:
                        pe.wait_ge(qkv_in[which % 2], 80 * (which // 2 + 1))
                    for i in range(k):
                        m = first + i
                        if what == "a":
                            src = p_0[:, which % NP, m * P:(m + 1) * P]
                        else:
                            src = q_h[which % 2][:, m, :] if m < NT else k_h[which % 2][:, m - NT, :]
                        last = nc.tensor.transpose(bank(4 + n % 2)[:, i * P:(i + 1) * P], src, ident[:, :])
                    last.then_inc(tr_done, 1)
                    done[0] += 1

            def scores(u):
                h, t = u // NT, u % NT
                k0, nk = unit_keys(u)
                if t == 0:
                    pe.wait_ge(tr_emptied["qk"], of_kind(transposed_upto("qk", h), "qk"))
                for s in range(2):
                    if u >= 1:
                        pe.wait_ge(exp_done[s], u)
                    d, c = slice(HD * s, HD * s + HD), slice(t * P, (t + 1) * P)
                    for b, w in ((0, min(nk, 4) * P), (1, (nk - 4) * P)):
                        if w > 0:
                            k = slice(k0 * P + b * CW, k0 * P + b * CW + w)
                            last = split3(bank(2 * s + b)[:, 0:w], qT_hi[d, h % 2, c], qT_lo[h % 2][d, c],
                                          kT_hi[d, h % 2, k], kT_lo[d, h % 2, k], True, True)
                    last.then_inc(sc_done[s], 1)

            def weigh(u):
                h = u // NT
                k0, nk = unit_keys(u)
                pe.wait_ge(tr_emptied["a"], of_kind(transposed_upto("a", u), "a"))
                if u >= 2:
                    pe.wait_ge(osq_ready, u - 1)
                for k in range(nk):
                    last = nc.tensor.matmul(bank(6 + u % 2)[:, 0:P], aT[:, u % 2, k * P:(k + 1) * P], v_h[h % 2][:, k0 + k, :],
                                            start=(k == 0), stop=(k == nk - 1))
                last.then_inc(pv_done, 1)

            transposes(transposed_upto("qk", 0))
            for u in range(NU):
                scores(u)
                if before_head(u, 1):
                    transposes(transposed_upto("qk", u // NT + 1))
                if u >= 3:
                    weigh(u - 3)
                if u >= 2:
                    transposes(transposed_upto("a", u - 2))
                if before_head(u, 2):
                    transposes(qk_upto(u // NT + 1, EARLY_QK))
            weigh(NU - 3)
            transposes(len(TRANSPOSED))
            weigh(NU - 2)
            weigh(NU - 1)

            n2 = [0]

            def piece2():
                n = n2[0]
                if n >= RING:
                    pe.wait_ge(p2_emptied, n - RING + 1)
                n2[0] += 1
                return bank(n % RING)

            for what, t, *half in STEPS:
                if what == "T":
                    pe.wait_ge(merged, t + 1)
                    for half in range(2):
                        ps = piece2()
                        for i in range(4):
                            k = 4 * half + i
                            last = nc.tensor.transpose(ps[:, i * P:(i + 1) * P], o_t[:, t, k * P:(k + 1) * P], ident[:, :])
                        last.then_inc(p2_done, 1)
                elif what == "W":
                    pe.wait_ge(p2_emptied, P2.index(("T", t, 1)) + 1)
                    b = FIRST_WO + half[0]
                    if t == 0:
                        pe.wait_ge(lo_done, 2 * b + 2)
                    ps = piece2()
                    for n in (2 * b, 2 * b + 1):
                        for k in range(CK):
                            kk = (n % 2) * CK + k
                            last = split3(ps, m_hi[:, t, kk, :], m_lo[:, t, kk, :], w_hi[:, split_slot(n), k, :],
                                          w_lo[:, split_slot(n), k, :], kk == 0, kk == KT - 1)
                    last.then_inc(p2_done, 1)
                elif what == "X":
                    pe.wait_ge(xn2_ready, t + 1)
                    for half in range(2):
                        ps = piece2()
                        for i in range(4):
                            k = 4 * half + i
                            last = nc.tensor.transpose(ps[:, i * P:(i + 1) * P], xn[t % 2][:, k * P:(k + 1) * P], ident[:, :])
                        last.then_inc(p2_done, 1)
                elif what == "L":
                    pe.wait_ge(p2_emptied, P2.index(("X", t, 1)) + 1)
                    ps = piece2()
                    for k in range(KT):
                        last = nc.tensor.matmul(ps[:, 0:E], h2T[t % 2][:, k, :], w_r[:, k, :], start=(k == 0), stop=(k == KT - 1))
                    last.then_inc(p2_done, 1)
                elif what == "A":
                    pe.wait_ge(aff_ready, t + 1)
                    ps = piece2()
                    for i, t in enumerate(GROUP[t]):
                        last = nc.tensor.transpose(ps[0:E, i * P:(i + 1) * P], lg[:, t, :], ident[:, :])
                    last.then_inc(p2_done, 1)
            pe.wait_ge(idx_ready, 1)
            for src in (idx_f, gate_v):
                nc.tensor.transpose(piece2()[0:CAP, 0:E], src[:, :], ident[0:E, 0:E]).then_inc(p2_done, 1)
            pe.wait_ge(xnlo_ready, NT)
            for k in range(KT):
                c = slice(k * P, (k + 1) * P)
                for part in range(3):
                    ps = piece2()
                    if part < 2:
                        for t in range(NL):
                            if k == 0 and part == 0:
                                pe.wait_ge(sel_ready, t + 1)
                            r = sel_l[:, t, 8 * part:8 * part + 8, :].rearrange("p e c -> p (e c)")
                            nc.tensor.matmul(ps, xn_hi[:, t, c], r, start=(t == 0), stop=False)
                            last = nc.tensor.matmul(ps, xn_lo[:, t, c], r, start=False, stop=(t == NL - 1))
                    else:
                        if k == 0:
                            pe.wait_ge(sel_ready, NT)
                        r = sel_c[:, :, :].rearrange("p e c -> p (e c)")
                        nc.tensor.matmul(ps[:, 0:E * CAP_C], xn_hi[:, NL, c], r, start=True, stop=False)
                        last = nc.tensor.matmul(ps[:, 0:E * CAP_C], xn_lo[:, NL, c], r, start=False, stop=True)
                    last.then_inc(p2_done, 1)
            pe.wait_ge(p2_emptied, N_P2)

            def hid_transposes(e, fb):
                pe.wait_ge(hid_ready, e * 4 + (fb + 1))
                if not (isinstance(e, int) and e == 0 and fb == 0):
                    pe.wait_ge(ht_ready, e * 4 + fb)
                for k in range(4):
                    last = nc.tensor.transpose(bank(6)[:, k * CAP:(k + 1) * CAP], hid[:, fb % 2, k * P:(k + 1) * P], ident[0:CAP, 0:CAP])
                last.then_inc(ht_done, 1)

            def scatter(e, n, piece, banks):
                t, half = piece // 2, piece % 2
                ps = bank(banks[n % len(banks)])
                pe.wait_ge(sel_done, e + 1)
                pe.wait_ge(ye_ready, e * 2 + (half + 1))
                if n >= len(banks):
                    pe.wait_ge(out_added, e * (2 * NT) + (n + 1 - len(banks)))
                c = slice(half * CW, (half + 1) * CW)
                nc.tensor.matmul(ps, selT[:, t * P:(t + 1) * P], ye_hi[:, c], start=True, stop=False)
                nc.tensor.matmul(ps, selT[:, t * P:(t + 1) * P], ye_lo[:, c], start=False, stop=True).then_inc(out_placed, 1)

            def expert(e, first, last_e):
                pe.wait_ge(xe_ready, e + 1)
                for i in range(EC):
                    s = i % NSPLIT
                    pe.wait_ge(lo_done, e * EC + (PRE + i + 1))
                    if i < 16:
                        fb, which, half = i // 4, i // 2 % 2, i % 2
                        ps = bank(fb % 2 * 2 + which)[0:CAP, :]
                        if half == 0 and (not first or fb >= 2):
                            pe.wait_ge(hid_ready, e * 4 + (fb - 1))
                        for k in range(CK):
                            if k == CK // 2 and i in HT_STEP:
                                hid_transposes(e, HT_STEP[i])
                            kk = half * CK + k
                            c = slice(kk * CAP, (kk + 1) * CAP)
                            last = split3(ps, xe_hi[:, c], xe_lo[:, c], w_hi[:, s, k, :], w_lo[:, s, k, :], kk == 0, kk == KT - 1)
                    else:
                        half, q = (i - 16) // 4, (i - 16) % 4
                        ps = bank(4 + half)[0:CAP, :]
                        if q == 0 and not first:
                            pe.wait_ge(yeg_ready, e * 2 + (half - 1))
                        pe.wait_ge(ht_ready, e * 4 + (q + 1))
                        for k in range(CK):
                            if k == CK // 2 and i in HT_STEP:
                                hid_transposes(e, HT_STEP[i])
                            f = q * CK + k
                            last = split3(ps, hT_hi[:, f, :], hT_lo[:, f, :], w_hi[:, s, k, :], w_lo[:, s, k, :], f == 0, f == FE // P - 1)
                    last.then_inc(chunk_read, 1)
                    if i in SC_STEPS and not first:
                        scatter(e - 1, SC_STEPS.index(i), SC_PIECES[SC_STEPS.index(i)], [7])
                    if last_e and i == END_STEP:
                        for n in range(NT):
                            scatter(e, n, SC_PIECES[n], END_BANKS)

            expert(0, True, False)
            with pe.Fori(1, E - 1) as e:
                expert(e, False, False)
            expert(E - 1, False, True)
            for n in range(NT, 2 * NT):
                scatter(E - 1, n, SC_PIECES[n], END_BANKS)


_INS = ["x_prompt", "x_sample", "cache_k", "cache_v", "c", "c_ctx", "w_ada", "b_ada", "norm1_g", "norm2_g", "w_in",
        "q_norm_g", "k_norm_g", "lambda_q1", "lambda_k1", "lambda_q2", "lambda_k2", "subln_g", "gmlp_ln_g",
        "gmlp_ln_b", "w_spatial", "b_spatial", "w_out", "w_router", "w_gate_e", "w_up_e", "w_down_e"]
_OUTS = [(1, CTX, D), (1, LAT, D), (1, 1, CTX, H, 2, HD), (1, 1, CTX, H, VD)]


def kernel(**inputs):
    import numpy as _np
    import concourse.bacc as _bacc
    from concourse import mybir as _mybir
    from concourse.bass_utils import run_bass_kernel_spmd as _run

    nc = _bacc.Bacc("TRN2", target_bir_lowering=False, num_devices=1)
    arrays = {f"in_{name}": _np.ascontiguousarray(inputs[name]) for name in _INS}
    arrays.update({f"in_{name}": _np.ascontiguousarray(a) for name, a in constants().items()})
    aps = {name[3:]: nc.dram_tensor(name, a.shape, _mybir.dt.from_np(a.dtype), kind="ExternalInput").ap()
           for name, a in arrays.items()}
    outs = [nc.dram_tensor(f"out_{i}", shape, F32, kind="ExternalOutput").ap() for i, shape in enumerate(_OUTS)]
    trunk_program(nc, aps, *outs)
    r = _run(nc, [arrays], core_ids=[0])
    return tuple(r.results[0][f"out_{i}"] for i in range(len(_OUTS)))
```
